# Optimizing a Trainium2 kernel written in Bass

```python
import math
import jax
import jax.numpy as jnp
from jax import lax
import numpy as np
import jax, jax.numpy as jnp

D_MODEL = 1024
BATCH = 1
SEQ = 512
DEPTH = 2

N_MIXERS = 2
S5_GROUP = 16
S5_GROUPS = D_MODEL // S5_GROUP
S5_STATE = 64
N_HEADS = 16
HEAD_DIM = D_MODEL // N_HEADS
IDX_HEADS = 8
IDX_DIM = 64
TOPK_MAX = 256
Q_BLOCK = 128
ROPE_THETA = 10000.0
D_FF = ((8 * D_MODEL // 3 + 255) // 256) * 256
N_S5 = (DEPTH + 1) // 2
N_DSA = DEPTH // 2
DSA_PROJ = 3 * D_MODEL + IDX_HEADS * IDX_DIM + IDX_DIM + IDX_HEADS
EPS = 1e-6


def rmsnorm(x, gain):
    xf = x.astype(jnp.float32)
    y = xf * lax.rsqrt(jnp.mean(xf * xf, axis=-1, keepdims=True) + EPS)
    if gain is not None:
        y = y * gain.astype(jnp.float32)
    return y.astype(x.dtype)

def rope_tables(length):
    inv_freq = ROPE_THETA ** (-jnp.arange(0, HEAD_DIM, 2, dtype=jnp.float32) / HEAD_DIM)
    ang = jnp.arange(length, dtype=jnp.float32)[:, None] * inv_freq[None, :]
    return jnp.cos(ang), jnp.sin(ang)

def apply_rope(t, cos, sin):
    tf = t.astype(jnp.float32)
    t1, t2 = jnp.split(tf, 2, axis=-1)
    c = cos[None, :, None, :]
    s = sin[None, :, None, :]
    out = jnp.concatenate([t1 * c - t2 * s, t2 * c + t1 * s], axis=-1)
    return out.astype(t.dtype)

def _ssm_combine(e1, e2):
    a1, b1 = e1
    a2, b2 = e2
    return a1 * a2, a2 * b1 + b2

def s5_mixer(u, lam_re, lam_im, log_dt, b_re, b_im, c_re, c_im, d_skip, w_glu):
    bsz, length, _ = u.shape
    f32 = jnp.float32
    lam = lax.complex(lam_re.astype(f32), lam_im.astype(f32))
    dt = jnp.exp(log_dt.astype(f32))[:, None]
    a_bar = jnp.exp(lam * dt)
    b_bar = ((a_bar - 1.0) / lam)[..., None] * lax.complex(b_re.astype(f32), b_im.astype(f32))
    ug = u.astype(f32).reshape(bsz, length, S5_GROUPS, S5_GROUP).astype(jnp.complex64)
    bu = jnp.einsum('blgh,gph->blgp', ug, b_bar)
    a_seq = jnp.broadcast_to(a_bar, bu.shape)
    _, states = lax.associative_scan(_ssm_combine, (a_seq, bu), axis=1)
    c = lax.complex(c_re.astype(f32), c_im.astype(f32))
    y = jnp.einsum('blgp,ghp->blgh', states, c).real.reshape(bsz, length, D_MODEL)
    y = y + d_skip.astype(f32) * u.astype(f32)
    y = jax.nn.gelu(y).astype(u.dtype)
    val, gate = jnp.split(y @ w_glu, 2, axis=-1)
    return val * jax.nn.sigmoid(gate)

def dsa_mixer(h, w_in, q_gain, k_gain, w_o, cos, sin, topk):
    bsz, length, _ = h.shape
    f32 = jnp.float32
    proj = h @ w_in
    cuts = [D_MODEL, 2 * D_MODEL, 3 * D_MODEL, 3 * D_MODEL + IDX_HEADS * IDX_DIM,
            3 * D_MODEL + IDX_HEADS * IDX_DIM + IDX_DIM]
    q, k, v, qi, ki, wi = jnp.split(proj, cuts, axis=-1)
    q = q.reshape(bsz, length, N_HEADS, HEAD_DIM)
    k = k.reshape(bsz, length, N_HEADS, HEAD_DIM)
    v = v.reshape(bsz, length, N_HEADS, HEAD_DIM)
    qi = qi.reshape(bsz, length, IDX_HEADS, IDX_DIM)
    q = apply_rope(rmsnorm(q, q_gain), cos, sin)
    k = apply_rope(rmsnorm(k, k_gain), cos, sin)
    qi = apply_rope(qi, cos, sin)
    ki = apply_rope(rmsnorm(ki, None)[:, :, None, :], cos, sin)[:, :, 0, :]
    wi = wi.astype(f32) * (IDX_HEADS ** -0.5)
    nb = length // Q_BLOCK
    kpos = jnp.arange(length, dtype=jnp.int32)
    qpos_blocks = kpos.reshape(nb, Q_BLOCK)
    att_scale = HEAD_DIM ** -0.5
    idx_scale = IDX_DIM ** -0.5

    def to_blocks(t):
        return t.reshape(bsz, nb, Q_BLOCK, *t.shape[2:]).swapaxes(0, 1)

    def attend_block(args):
        qb, qib, wb, qpos = args
        s_idx = jnp.einsum('bqhd,bkd->bqhk', qib, ki).astype(f32) * idx_scale
        score = jnp.einsum('bqhk,bqh->bqk', jax.nn.relu(s_idx), wb)
        causal = kpos[None, None, :] <= qpos[None, :, None]
        score = jnp.where(causal, score, -jnp.inf)
        _, sel = lax.top_k(score, topk)
        kg = jax.vmap(lambda kb, ib: kb[ib])(k, sel)
        vg = jax.vmap(lambda vb, ib: vb[ib])(v, sel)
        logits = jnp.einsum('bqhd,bqkhd->bhqk', qb, kg).astype(f32) * att_scale
        valid = (sel <= qpos[None, :, None])[:, None, :, :]
        logits = jnp.where(valid, logits, -jnp.inf)
        p = jax.nn.softmax(logits, axis=-1).astype(vg.dtype)
        return jnp.einsum('bhqk,bqkhd->bqhd', p, vg)

    out = lax.map(attend_block, (to_blocks(q), to_blocks(qi), to_blocks(wi), qpos_blocks))
    out = out.swapaxes(0, 1).reshape(bsz, length, D_MODEL)
    return out @ w_o

def swiglu(h, w_gate_up, w_down):
    gate, up = jnp.split(h @ w_gate_up, 2, axis=-1)
    return (jax.nn.silu(gate) * up) @ w_down

def first_inputs(seed: int = 0) -> dict:
    key = jax.random.key(seed)
    ks = jax.random.split(key, 20)
    f32 = jnp.float32
    nrm = lambda k, shape, s: jax.random.normal(k, shape, f32) * s
    x = jax.random.normal(ks[0], (BATCH, SEQ, D_MODEL), f32)
    n_idx = jnp.arange(S5_STATE, dtype=f32)
    s5_lambda_re = -0.5 + nrm(ks[1], (N_S5, S5_GROUPS, S5_STATE), 0.01)
    s5_lambda_im = math.pi * n_idx[None, None, :] + nrm(ks[2], (N_S5, S5_GROUPS, S5_STATE), 0.01)
    s5_log_dt = jax.random.uniform(ks[3], (N_S5, S5_GROUPS), f32, math.log(1e-3), math.log(1e-1))
    s5_b_re = nrm(ks[4], (N_S5, S5_GROUPS, S5_STATE, S5_GROUP), (2 * S5_GROUP) ** -0.5)
    s5_b_im = nrm(ks[5], (N_S5, S5_GROUPS, S5_STATE, S5_GROUP), (2 * S5_GROUP) ** -0.5)
    s5_c_re = nrm(ks[6], (N_S5, S5_GROUPS, S5_GROUP, S5_STATE), (2 * S5_STATE) ** -0.5)
    s5_c_im = nrm(ks[7], (N_S5, S5_GROUPS, S5_GROUP, S5_STATE), (2 * S5_STATE) ** -0.5)
    s5_d = nrm(ks[8], (N_S5, D_MODEL), 1.0)
    s5_w_glu = nrm(ks[9], (N_S5, D_MODEL, 2 * D_MODEL), D_MODEL ** -0.5)
    dsa_w_in = nrm(ks[10], (N_DSA, D_MODEL, DSA_PROJ), D_MODEL ** -0.5)
    dsa_q_norm = 1.0 + nrm(ks[11], (N_DSA, HEAD_DIM), 0.02)
    dsa_k_norm = 1.0 + nrm(ks[12], (N_DSA, HEAD_DIM), 0.02)
    dsa_w_o = nrm(ks[13], (N_DSA, D_MODEL, D_MODEL), D_MODEL ** -0.5)
    ffn_w_gate_up = nrm(ks[14], (DEPTH, D_MODEL, 2 * D_FF), D_MODEL ** -0.5)
    ffn_w_down = nrm(ks[15], (DEPTH, D_FF, D_MODEL), D_FF ** -0.5)
    norm_mix = 1.0 + nrm(ks[16], (DEPTH, D_MODEL), 0.02)
    norm_ffn = 1.0 + nrm(ks[17], (DEPTH, D_MODEL), 0.02)
    return {'x': x, 's5_lambda_re': s5_lambda_re, 's5_lambda_im': s5_lambda_im, 's5_log_dt': s5_log_dt,
            's5_b_re': s5_b_re, 's5_b_im': s5_b_im, 's5_c_re': s5_c_re, 's5_c_im': s5_c_im,
            's5_d': s5_d, 's5_w_glu': s5_w_glu, 'dsa_w_in': dsa_w_in, 'dsa_q_norm': dsa_q_norm,
            'dsa_k_norm': dsa_k_norm, 'dsa_w_o': dsa_w_o, 'ffn_w_gate_up': ffn_w_gate_up,
            'ffn_w_down': ffn_w_down, 'norm_mix': norm_mix, 'norm_ffn': norm_ffn}

def first_block(x, s5_lambda_re, s5_lambda_im, s5_log_dt, s5_b_re, s5_b_im, s5_c_re, s5_c_im,
              s5_d, s5_w_glu, dsa_w_in, dsa_q_norm, dsa_k_norm, dsa_w_o, ffn_w_gate_up,
              ffn_w_down, norm_mix, norm_ffn):
    length = x.shape[1]
    topk = min(TOPK_MAX, length // 4)
    cos, sin = rope_tables(length)
    for i in range(DEPTH):
        h = rmsnorm(x, norm_mix[i])
        j = i // N_MIXERS
        if i % N_MIXERS == 0:
            mix = s5_mixer(h, s5_lambda_re[j], s5_lambda_im[j], s5_log_dt[j], s5_b_re[j], s5_b_im[j],
                           s5_c_re[j], s5_c_im[j], s5_d[j], s5_w_glu[j])
        else:
            mix = dsa_mixer(h, dsa_w_in[j], dsa_q_norm[j], dsa_k_norm[j], dsa_w_o[j], cos, sin, topk)
        x = x + mix.astype(x.dtype)
        x = x + swiglu(rmsnorm(x, norm_ffn[i]), ffn_w_gate_up[i], ffn_w_down[i]).astype(x.dtype)
    return x


DEPTH_2 = 1

HEAD_DIM_2 = 64
MEM_LEN = 256
NORM_EPS = 1e-6
NEG = -1e30
SCALE = HEAD_DIM_2 ** -0.5
A_HEADS = 4
A_CONFIGS = ((128, 1), (512, 4), (2048, 16))
B_HEADS = 4
SB_BLOCK = 128
C_HEADS = 4
C_KV_HEADS = 2
C_WINDOW = 128
D_HEADS = 4
MOBA_BLOCK = 256
MOBA_TOPK = 3
MOBA_QCHUNK = 16
BAND_BLOCK = 128
REL_BUCKETS = 32
REL_MAX_DIST = 2048
A_BIAS_LO = 0
C_BIAS_LO = A_HEADS
D_BIAS_LO = A_HEADS + C_HEADS
REL_HEADS = A_HEADS + C_HEADS + D_HEADS
X_HEADS = 4
X_HEAD_DIM = 64
X_W = X_HEADS * X_HEAD_DIM
X_SCALE = X_HEAD_DIM ** -0.5
D_FF_2 = 4 * D_MODEL
A_W = A_HEADS * HEAD_DIM_2
B_W = B_HEADS * HEAD_DIM_2
C_QW = C_HEADS * HEAD_DIM_2
C_KVW = C_KV_HEADS * HEAD_DIM_2
D_W = D_HEADS * HEAD_DIM_2
IN_WIDTH = 3 * A_W + 3 * B_W + C_QW + 2 * C_KVW + 3 * D_W
MIX_WIDTH = A_W + B_W + C_QW + D_W


def rmsnorm_2(x, g):
    xf = x.astype(jnp.float32)
    y = xf * lax.rsqrt(jnp.mean(xf * xf, axis=-1, keepdims=True) + NORM_EPS)
    return (y * g.astype(jnp.float32)).astype(x.dtype)

def rel_bucket(dist):
    max_exact = REL_BUCKETS // 2
    n = jnp.maximum(dist, 0)
    nf = jnp.maximum(n, 1).astype(jnp.float32)
    large = max_exact + (jnp.log(nf / max_exact) / math.log(REL_MAX_DIST / max_exact)
                         * (REL_BUCKETS - max_exact)).astype(jnp.int32)
    large = jnp.minimum(large, REL_BUCKETS - 1)
    return jnp.where(n < max_exact, n, large)

def rel_bias_heads(rel_table, dist, head_lo, n_heads):
    tab = rel_table[:, head_lo:head_lo + n_heads].astype(jnp.float32)
    return jnp.moveaxis(tab[rel_bucket(dist)], -1, 0)

def pad_to_multiple(x, axis, mult):
    n = x.shape[axis]
    pad = (-n) % mult
    if pad == 0:
        return x
    widths = [(0, 0)] * x.ndim
    widths[axis] = (0, pad)
    return jnp.pad(x, widths)

def to_blocks(x, blk):
    return x.reshape(x.shape[:-2] + (x.shape[-2] // blk, blk, x.shape[-1]))

def band_keys(xb):
    prev = jnp.concatenate([jnp.zeros_like(xb[..., :1, :, :]), xb[..., :-1, :, :]], axis=-3)
    return jnp.concatenate([prev, xb], axis=-2)

def band_geometry(n_blocks):
    qi = jnp.arange(BAND_BLOCK)[:, None]
    ki = jnp.arange(2 * BAND_BLOCK)[None, :]
    dist = qi + BAND_BLOCK - ki
    first_ok = (jnp.arange(n_blocks)[:, None, None] > 0) | (ki >= BAND_BLOCK)[None]
    return dist, first_ok

def dilated_attention(q, k, v, rel_table):
    B, H, S, E = q.shape
    blk = BAND_BLOCK
    nums, maxs, dens = [], [], []
    for window, dil in A_CONFIGS:
        span = window // dil
        L = S // dil

        def residue_blocks(t):
            t = t.reshape(B, H, L, dil, E).transpose(0, 1, 3, 2, 4)
            return to_blocks(pad_to_multiple(t, 3, blk), blk)

        qb = residue_blocks(q)
        kb = band_keys(residue_blocks(k))
        vb = band_keys(residue_blocks(v))
        nb = qb.shape[3]
        dist, first_ok = band_geometry(nb)
        valid = (dist >= 0) & (dist <= span) & first_ok
        bias = rel_bias_heads(rel_table, dist * dil, A_BIAS_LO, H)
        s = jnp.einsum("bhrnqe,bhrnke->bhrnqk", qb, kb) * SCALE + bias[None, :, None, None]
        s = jnp.where(valid, s, NEG)
        m = jnp.max(s, axis=-1)
        p = jnp.exp(s - m[..., None])
        l = jnp.sum(p, axis=-1)
        o = jnp.einsum("bhrnqk,bhrnke->bhrnqe", p, vb)

        def unres(t):
            t = t.reshape((B, H, dil, nb * blk) + t.shape[5:])[:, :, :, :L]
            t = jnp.swapaxes(t, 2, 3)
            return t.reshape((B, H, S) + t.shape[4:])

        nums.append(unres(o))
        maxs.append(unres(m))
        dens.append(unres(l))
    mx = jnp.stack(maxs)
    w = jnp.exp(mx - jnp.max(mx, axis=0, keepdims=True))
    num = jnp.einsum("cbhs,cbhse->bhse", w, jnp.stack(nums))
    den = jnp.sum(w * jnp.stack(dens), axis=0)
    return num / den[..., None]

def stick_breaking_attention(q, k, v):
    B, H, S, E = q.shape
    nblk = S // SB_BLOCK
    qs = q.reshape(B, H, nblk, SB_BLOCK, E).transpose(2, 0, 1, 3, 4)
    kpos = jnp.arange(S)

    def one_block(args):
        qb, i = args
        qpos = i * SB_BLOCK + jnp.arange(SB_BLOCK)
        z = jnp.einsum("bhqe,bhke->bhqk", qb, k) * SCALE
        past = kpos[None, :] < qpos[:, None]
        log_1m = jnp.where(past, jax.nn.log_sigmoid(-z), 0.0)
        suffix = lax.cumsum(log_1m, axis=3, reverse=True) - log_1m
        a = jnp.where(past, jnp.exp(jax.nn.log_sigmoid(z) + suffix), 0.0)
        return jnp.einsum("bhqk,bhke->bhqe", a, v)

    out = lax.map(one_block, (qs, jnp.arange(nblk)))
    return out.transpose(1, 2, 0, 3, 4).reshape(B, H, S, E)

def sliding_window_sink_attention(q, k, v, sinks, rel_table):
    B, Hq, S, E = q.shape
    G = k.shape[1]
    R = Hq // G
    blk = BAND_BLOCK
    qb = to_blocks(q.reshape(B, G, R, S, E), blk)
    kb = band_keys(to_blocks(k, blk))
    vb = band_keys(to_blocks(v, blk))
    nb = qb.shape[3]
    dist, first_ok = band_geometry(nb)
    valid = (dist >= 0) & (dist < C_WINDOW) & first_ok
    bias = rel_bias_heads(rel_table, dist, C_BIAS_LO, Hq).reshape(G, R, blk, 2 * blk)
    s = jnp.einsum("bgrnqe,bgnke->bgrnqk", qb, kb) * SCALE + bias[None, :, :, None]
    s = jnp.where(valid, s, NEG)
    sink = sinks.astype(jnp.float32).reshape(G, R)[None, :, :, None, None, None]
    m = jnp.maximum(jnp.max(s, axis=-1, keepdims=True), sink)
    p = jnp.exp(s - m)
    den = jnp.sum(p, axis=-1, keepdims=True) + jnp.exp(sink - m)
    o = jnp.einsum("bgrnqk,bgnke->bgrnqe", p / den, vb)
    return o.reshape(B, Hq, S, E)

def moba_attention(q, k, v, rel_table):
    B, H, S, E = q.shape
    blk = MOBA_BLOCK
    qp = pad_to_multiple(q, 2, blk)
    kp = pad_to_multiple(k, 2, blk)
    vp = pad_to_multiple(v, 2, blk)
    Sp = qp.shape[2]
    nblk = Sp // blk
    kblk = kp.reshape(B, H, nblk, blk, E)
    vblk = vp.reshape(B, H, nblk, blk, E)
    kmean = jnp.mean(kblk, axis=3)
    qblock = jnp.arange(Sp) // blk
    fully_past = jnp.arange(nblk)[None, :] < qblock[:, None]
    gate = jnp.where(fully_past, jnp.einsum("bhse,bhne->bhsn", qp, kmean), NEG)
    n_sel = min(MOBA_TOPK, nblk)
    _, sel = lax.top_k(gate, n_sel)
    sel_ok = sel < qblock[:, None]
    tab = rel_table[:, D_BIAS_LO:D_BIAS_LO + H].T.astype(jnp.float32)
    b_ix = jnp.arange(B)[:, None, None, None]
    h_ix = jnp.arange(H)[None, :, None, None]
    offs = jnp.arange(blk)

    def one_chunk(c):
        start = c * MOBA_QCHUNK
        qc = lax.dynamic_slice_in_dim(qp, start, MOBA_QCHUNK, axis=2)
        idx = lax.dynamic_slice_in_dim(sel, start, MOBA_QCHUNK, axis=2)
        ok = lax.dynamic_slice_in_dim(sel_ok, start, MOBA_QCHUNK, axis=2)
        tpos = start + jnp.arange(MOBA_QCHUNK)
        own = start // blk
        k_own = lax.dynamic_index_in_dim(kblk, own, axis=2, keepdims=False)
        v_own = lax.dynamic_index_in_dim(vblk, own, axis=2, keepdims=False)
        d_own = tpos[:, None] - (own * blk + offs)[None, :]
        s_own = jnp.einsum("bhqe,bhke->bhqk", qc, k_own) * SCALE + tab[:, rel_bucket(d_own)][None]
        s_own = jnp.where(d_own >= 0, s_own, NEG)
        k_sel = kblk[b_ix, h_ix, idx]
        v_sel = vblk[b_ix, h_ix, idx]
        d_sel = tpos[:, None, None] - (idx[..., None] * blk + offs)
        s_sel = (jnp.einsum("bhqe,bhqjke->bhqjk", qc, k_sel) * SCALE
                 + tab[h_ix[..., None], rel_bucket(d_sel)])
        s_sel = jnp.where(ok[..., None], s_sel, NEG).reshape(B, H, MOBA_QCHUNK, n_sel * blk)
        p = jax.nn.softmax(jnp.concatenate([s_own, s_sel], axis=-1), axis=-1)
        p_own = p[..., :blk]
        p_sel = p[..., blk:].reshape(B, H, MOBA_QCHUNK, n_sel, blk)
        return (jnp.einsum("bhqk,bhke->bhqe", p_own, v_own)
                + jnp.einsum("bhqjk,bhqjke->bhqe", p_sel, v_sel))

    out = lax.map(one_chunk, jnp.arange(Sp // MOBA_QCHUNK))
    return out.transpose(1, 2, 0, 3, 4).reshape(B, H, Sp, E)[:, :, :S]

def hybrid_mixer(h, w_in, g_group, sinks, w_out, rel_table):
    B, S, _ = h.shape
    proj = (h @ w_in).astype(jnp.float32)
    sizes = (A_W, A_W, A_W, B_W, B_W, B_W, C_QW, C_KVW, C_KVW, D_W, D_W, D_W)
    cuts = []
    acc = 0
    for sz in sizes[:-1]:
        acc += sz
        cuts.append(acc)
    aq, ak, av, bq, bk, bv, cq, ck, cv, dq, dk, dv = jnp.split(proj, cuts, axis=-1)

    def heads(t):
        return t.reshape(B, S, -1, HEAD_DIM_2).transpose(0, 2, 1, 3)

    ya = dilated_attention(heads(aq), heads(ak), heads(av), rel_table)
    yb = stick_breaking_attention(heads(bq), heads(bk), heads(bv))
    yc = sliding_window_sink_attention(heads(cq), heads(ck), heads(cv), sinks, rel_table)
    yd = moba_attention(heads(dq), heads(dk), heads(dv), rel_table)
    groups = []
    for y in (ya, yb, yc, yd):
        y = y.transpose(0, 2, 1, 3).reshape(B, S, -1)
        groups.append(y * lax.rsqrt(jnp.mean(y * y, axis=-1, keepdims=True) + NORM_EPS))
    y = jnp.concatenate(groups, axis=-1) * g_group.astype(jnp.float32)
    return y.astype(h.dtype) @ w_out

def memory_cross_attention(h, m, w_q, w_kv, w_o):
    B, S, _ = h.shape
    M = m.shape[1]
    q = (h @ w_q).astype(jnp.float32).reshape(B, S, X_HEADS, X_HEAD_DIM)
    kv = (m @ w_kv).astype(jnp.float32)
    k = kv[..., :X_W].reshape(B, M, X_HEADS, X_HEAD_DIM)
    v = kv[..., X_W:].reshape(B, M, X_HEADS, X_HEAD_DIM)
    p = jax.nn.softmax(jnp.einsum("bshe,bmhe->bhsm", q, k) * X_SCALE, axis=-1)
    o = jnp.einsum("bhsm,bmhe->bshe", p, v).reshape(B, S, X_W)
    return o.astype(h.dtype) @ w_o

def squared_relu_mlp(h, w_up, w_down):
    return jnp.square(jax.nn.relu(h @ w_up)) @ w_down

def second_inputs(seed: int = 0) -> dict:
    key = jax.random.key(seed)
    ks = jax.random.split(key, 17)
    f32 = jnp.float32

    def nrm(k, shape, scale):
        return jax.random.normal(k, shape, f32) * scale

    def gain(k, shape):
        return 1.0 + 0.02 * jax.random.normal(k, shape, f32)

    return {
        "x": nrm(ks[0], (BATCH, SEQ, D_MODEL), 1.0),
        "mem": nrm(ks[1], (BATCH, MEM_LEN, D_MODEL), 1.0),
        "rel_table": nrm(ks[2], (REL_BUCKETS, REL_HEADS), 0.5),
        "g_mix": gain(ks[3], (DEPTH_2, D_MODEL)),
        "w_in": nrm(ks[4], (DEPTH_2, D_MODEL, IN_WIDTH), D_MODEL ** -0.5),
        "g_group": gain(ks[5], (DEPTH_2, MIX_WIDTH)),
        "sinks": nrm(ks[6], (DEPTH_2, C_HEADS), 0.5),
        "w_out": nrm(ks[7], (DEPTH_2, MIX_WIDTH, D_MODEL), MIX_WIDTH ** -0.5),
        "g_cross": gain(ks[8], (DEPTH_2, D_MODEL)),
        "g_mem": gain(ks[9], (DEPTH_2, D_MODEL)),
        "w_xq": nrm(ks[10], (DEPTH_2, D_MODEL, X_W), D_MODEL ** -0.5),
        "w_xkv": nrm(ks[11], (DEPTH_2, D_MODEL, 2 * X_W), D_MODEL ** -0.5),
        "w_xo": nrm(ks[12], (DEPTH_2, X_W, D_MODEL), X_W ** -0.5),
        "g_mlp": gain(ks[13], (DEPTH_2, D_MODEL)),
        "w_up": nrm(ks[14], (DEPTH_2, D_MODEL, D_FF_2), D_MODEL ** -0.5),
        "w_down": nrm(ks[15], (DEPTH_2, D_FF_2, D_MODEL), D_FF_2 ** -0.5),
        "g_final": gain(ks[16], (D_MODEL,)),
    }

def second_block(x, mem, rel_table, g_mix, w_in, g_group, sinks, w_out, g_cross, g_mem,
              w_xq, w_xkv, w_xo, g_mlp, w_up, w_down, g_final):
    for l in range(DEPTH_2):
        x = x + hybrid_mixer(rmsnorm_2(x, g_mix[l]), w_in[l], g_group[l], sinks[l], w_out[l], rel_table)
        x = x + memory_cross_attention(rmsnorm_2(x, g_cross[l]), rmsnorm_2(mem, g_mem[l]),
                                       w_xq[l], w_xkv[l], w_xo[l])
        x = x + squared_relu_mlp(rmsnorm_2(x, g_mlp[l]), w_up[l], w_down[l])
    return rmsnorm_2(x, g_final)


def setup_inputs(seed=0):
    out = dict(first_inputs(seed))
    for name, value in second_inputs(seed + 1).items():
        if name != "x":
            out[name + "_2"] = value
    return out


def reference(
    x, s5_lambda_re, s5_lambda_im, s5_log_dt, s5_b_re, s5_b_im, s5_c_re, s5_c_im, s5_d,
    s5_w_glu, dsa_w_in, dsa_q_norm, dsa_k_norm, dsa_w_o, ffn_w_gate_up, ffn_w_down, norm_mix,
    norm_ffn, mem_2, rel_table_2, g_mix_2, w_in_2, g_group_2, sinks_2, w_out_2, g_cross_2,
    g_mem_2, w_xq_2, w_xkv_2, w_xo_2, g_mlp_2, w_up_2, w_down_2, g_final_2,
):
    x = first_block(
        x, s5_lambda_re, s5_lambda_im, s5_log_dt, s5_b_re, s5_b_im, s5_c_re, s5_c_im, s5_d,
        s5_w_glu, dsa_w_in, dsa_q_norm, dsa_k_norm, dsa_w_o, ffn_w_gate_up, ffn_w_down,
        norm_mix, norm_ffn,
    )
    return second_block(
        x, mem_2, rel_table_2, g_mix_2, w_in_2, g_group_2, sinks_2, w_out_2, g_cross_2, g_mem_2,
        w_xq_2, w_xkv_2, w_xo_2, g_mlp_2, w_up_2, w_down_2, g_final_2,
    )


_drawn_inputs = setup_inputs


def setup_inputs(seed=0):
    import zlib

    import numpy as np

    out = dict(_drawn_inputs(seed))
    spreads = {}
    factors = {'s5_lambda_re': 8.0,
     'dsa_q_norm': 8.0,
     'dsa_k_norm': 8.0,
     'g_mix_2': 3.471,
     'g_group_2': 4.552,
     'sinks_2': 8.0,
     'g_cross_2': 8.0,
     'g_mem_2': 8.0,
     'g_mlp_2': 4.118,
     'g_final_2': 2.745}
    for name, (base, spread) in spreads.items():
        noise = np.random.default_rng([zlib.crc32(name.encode()), seed]).standard_normal(out[name].shape)
        drawn = base * np.exp(spread * noise) if base else spread * noise
        out[name] = jnp.asarray(drawn.astype(out[name].dtype))
    for name, factor in factors.items():
        out[name] = (out[name] * factor).astype(out[name].dtype)
    return out
```

```python
from contextlib import ExitStack

import numpy as np

import concourse.bass as bass
from concourse import mybir

F32 = mybir.dt.float32
F32R = mybir.dt.float32r
I32 = mybir.dt.int32
ALU = mybir.AluOpType
ACT = mybir.ActivationFunctionType
AX = mybir.AxisListType

P = 128
S = 512
D = 1024
TB = S // P
KT = D // P
EPS = 1e-6
NEG = -1e30

G, GH, GP = 64, 16, 64
CH = P // GH
NC = S // CH
GB = P // GH
NB = G // GB

HD = 64
NH = 16
NI = 8
TOPK = min(256, S // 4)
DSA_W = 3 * D + NI * HD + HD + NI

FF = 2816
FT = FF // P
FF2 = 4096
MLP_PARTS = 2
MT = FF2 // P // MLP_PARTS

MEM = 256
NREL = 12
BUCKETS = 32
BIAS_W = S + P - 1

SLOT = 2048

GAINS = ["norm_mix0", "norm_mix1", "norm_ffn0", "norm_ffn1", "g_mix", "g_cross", "g_mem", "g_mlp", "g_group"]


def shape_constants():
    f = np.float32
    row, col = np.arange(P)[:, None], np.arange(P)[None, :]
    masks = np.stack([np.where(col <= row, 0, NEG), np.where(col < row, 0, NEG), col < row], 1).astype(f)
    inv = f(10000.0) ** (-np.arange(0, HD, 2, dtype=f) / f(HD))
    ang = np.arange(S, dtype=f)[:, None] * inv[None, :]
    cos, sin = np.cos(ang).astype(f), np.sin(ang).astype(f)
    rope = np.stack([np.concatenate([cos, cos], 1), np.concatenate([-sin, sin], 1)])
    rope = np.ascontiguousarray(rope.reshape(2, TB, P, HD).transpose(2, 0, 1, 3))
    dist = np.arange(BIAS_W) - (P - 1)
    n = np.maximum(dist, 0)
    big = 16 + (np.log(np.maximum(n, 1).astype(f) / f(16)) / f(np.log(128.0)) * f(16)).astype(np.int32)
    bucket = np.where(n < 16, n, np.minimum(big, BUCKETS - 1))
    times = np.where(dist >= 0, (n <= 128).astype(int) + (n % 4 == 0) + (n % 16 == 0), 0)
    basis = np.zeros((BUCKETS + 3, BIAS_W), f)
    basis[bucket, np.arange(BIAS_W)] = 1
    basis[BUCKETS] = np.where(times > 0, np.log(np.maximum(times, 1)), NEG)
    basis[BUCKETS + 1] = np.where((dist >= 0) & (dist < 128), 0, NEG)
    basis[BUCKETS + 2] = np.where(dist >= 0, 0, NEG)
    pick = np.zeros((3, NREL), f)
    pick[np.arange(NREL) // 4, np.arange(NREL)] = 1
    sign = np.where(np.arange(P) < GP, 1, -1).astype(f)[:, None]
    return {
        "c_ident": np.eye(P, dtype=f), "c_masks": masks, "c_rope": rope, "c_basis": basis, "c_pick": pick,
        "c_sign": sign,
    }


GLU_SLOT, GLU_SLOTS = 0, 8
FFN_SLOT = [8, 61]
FFN_DOWN = [4, 4, 4, 4, 4, 2]
DSA_SLOT = 42
WO_SLOT = 57
HIN_SLOT = 95
HOUT_SLOT = 107
MEM_SLOT = 111
XQ_SLOT = 113
XO_SLOT = 114
MLP_SLOT = [115, 131]
SLOTS = 147
FFN_TILE, HIN_TILE, MEM_TILE, XQ_TILE, MLP_TILE = [0, 22], 44, 52, 53, [54, 62]
GLU_PANEL, FFN_PANEL, DSA_PANEL, WO_PANEL, HIN_PANEL = 0, [4, 16], 6, 14, 18
HOUT_PANEL, MEM_PANEL, XO_PANEL, MLP_PANEL = 20, 22, 23, [25, 27]
FFN_HID, MLP_HID = [0, 22], [44, 52]




def program(nc, w, out):
    with ExitStack() as ctx:
        def sem(name):
            return ctx.enter_context(nc.semaphore(name))

        def fixed(name, shape, dt=F32):
            return ctx.enter_context(nc.sbuf_tensor(name, shape, dt))

        x_res = fixed("x_res", [P, TB, D])
        xT_hi = fixed("xT_hi", [P, KT, S], F32R)
        xT_lo = fixed("xT_lo", [P, KT, S], F32R)
        raw = fixed("raw", [P, 2, SLOT])
        w_hi = fixed("w_hi", [P, 2, SLOT], F32R)
        w_lo = fixed("w_lo", [P, 2, SLOT], F32R)
        arena = fixed("arena", [P, 2 * FT * S])
        spare = fixed("spare", [P, 3072])
        ident = fixed("ident", [P, P])
        masks = fixed("masks", [P, 3, P])
        sign = fixed("sign", [P, 1])
        gain_rows = fixed("gain_rows", [len(GAINS) * KT, P])
        gains = fixed("gains", [P, len(GAINS) * KT])
        half_neg = fixed("half_neg", [P, 64])
        one = fixed("one", [P, 1])
        ssq = fixed("ssq", [P, 64])
        rstd = fixed("rstd", [P, 64])
        r8 = fixed("r8", [P, G])
        neg_max = fixed("neg_max", [P, 4])
        row_sum = fixed("row_sum", [P, 4])
        inv_sum = fixed("inv_sum", [P, 4])
        sinks = fixed("sinks", [P, 4])
        sinks_neg = fixed("sinks_neg", [P, 4])
        rope = fixed("rope", [P, 2, TB, HD])
        rope_q = fixed("rope_q", [P, 2, TB, HD])
        rope_k = fixed("rope_k", [P, 2, TB, HD])
        gain_qk = fixed("gain_qk", [P, 2, HD])
        head_ss = fixed("head_ss", [P, 2, 8])
        head_rs = fixed("head_rs", [P, 2, 8])
        w_idx = fixed("w_idx", [P, TB, NI])
        top = fixed("top", [P, 8])
        above = fixed("above", [P, 1])
        sink_e = fixed("sink_e", [P, 4])
        PS = ctx.enter_context(nc.psum_tensor("PS", [P, 8, 512], F32))

        KB = 1024
        region_at = {n: nc.lookup_mloc(t).addr for n, t in (
            ("arena", arena), ("spare", spare), ("x_hi", xT_hi), ("x_lo", xT_lo), ("w_hi", w_hi), ("w_lo", w_lo),
            ("x_res", x_res))}

        def place(name, where, at, shape, dt=F32):
            return nc.alloc_sbuf_tensor_at(name, shape, dt, offset=region_at[where] + at)

        u = place("u", "arena", 0, [NC, G, CH, GH])
        y = place("y", "arena", 0, [NC, NB, CH, P])
        xp = place("xp", "arena", 32 * KB, [NC, CH, D])
        tab_c = place("tab_c", "arena", 32 * KB, [P, G, NC])
        tab_s = place("tab_s", "arena", 48 * KB, [P, G, NC])
        b_n = place("b_n", "arena", 64 * KB, [P, G, GH])
        b_s = place("b_s", "arena", 68 * KB, [P, G, GH])
        c_n = place("c_n", "arena", 72 * KB, [P, G, GH])
        c_s = place("c_s", "arena", 76 * KB, [P, G, GH])
        decay = place("decay", "arena", 80 * KB, [P, GB, NC])
        tmp_b = place("tmp_b", "arena", 82 * KB, [P, GB, CH, GH])
        pw_r = place("pw_r", "spare", 0, [P, G, CH + 1])
        pw_i = place("pw_i", "spare", 2304, [P, G, CH + 1])
        pw_rs = place("pw_rs", "spare", 4608, [P, G, CH + 1])
        pw_is = place("pw_is", "spare", 6912, [P, G, CH + 1])
        uT = place("uT", "x_hi", 0, [P, G, NC])
        nat_b = place("nat_b", "x_lo", 0, [G, 3, GP, GH])
        nat_c = place("nat_c", "x_hi", 0, [P, NB, 3, GP])
        nat_l = place("nat_l", "x_lo", 12 * KB, [G, 2, 2, GP])
        out_a = place("out_a", "x_lo", 0, [P, GB, CH + 1, GH])
        out_b = place("out_b", "x_lo", 4608, [P, GB, CH, GH])
        in_w = place("in_w", "x_lo", 8704, [P, GB, CH, GH])
        small = place("small", "w_hi", 0, [P, 32, G])
        in_t = place("in_t", "w_hi", 0, [P, GB, 2, GP])
        in_s = place("in_s", "w_hi", 4 * KB, [P, GB, 2, GP])
        taps = place("taps", "w_hi", 8 * KB, [P, GB, CH, GH])
        lag = place("lag", "w_hi", 12 * KB, [GH, GB, CH, GH])
        rot1 = place("rot1", "w_lo", 0, [P, G, NC // 2])
        rot2 = place("rot2", "w_lo", 8 * KB, [P, G, NC // 2])
        v1 = place("v1", "w_lo", 0, [P, GB, NC])
        v2 = place("v2", "w_lo", 2 * KB, [P, GB, NC])
        glu_sg = place("glu_sg", "spare", 0, [P, 2, 256])
        glu_v = place("glu_v", "spare", 2 * KB, [P, 2, 256])
        z = place("z", "w_lo", 4 * KB, [P, GB, NC])
        cz = place("cz", "w_lo", 6 * KB, [P, GB, NC])
        sz = place("sz", "w_lo", 8 * KB, [P, GB, NC])
        du = place("du", "x_res", 12 * KB, [NC, GB, CH, GH])
        d_row = place("d_row", "x_res", 0, [NC, D])
        junk = place("junk", "x_res", 4 * KB, [NC, D])
        g_row = place("g_row", "x_res", 8 * KB, [NC, D])
        tmp_a = place("tmp_a", "x_res", 4 * KB, [P, GB, CH + 1, GH])

        xn = place("xn", "arena", 0, [P, TB, D])
        hT_hi = place("hT_hi", "arena", 0, [P, FT, S], F32R)
        hT_lo = place("hT_lo", "arena", FT * S * 4, [P, FT, S], F32R)
        gbuf = place("gbuf", "spare", 0, [P, 2, 2, 512])
        sq_junk = place("sq_junk", "spare", 8 * KB, [P, D])

        stage = place("stage", "arena", 0, [P, 2, TB, 512])
        o_nat = place("o_nat", "arena", 0, [P, TB, D])
        qT = place("qT", "arena", 16 * KB, [P, KT, S])
        kT = place("kT", "arena", 32 * KB, [P, KT, S])
        v_dsa = place("v_dsa", "arena", 48 * KB, [P, TB, D])
        qiT = place("qiT", "arena", 64 * KB, [P, NI // 2, S])
        kiT = place("kiT", "arena", 72 * KB, [P, S])
        head_sq = place("head_sq", "arena", 74 * KB, [P, 2, 512])
        head_n = place("head_n", "arena", 78 * KB, [P, 2, 512])
        head_c = place("head_c", "arena", 82 * KB, [P, 2, 512])
        head_s = place("head_s", "spare", 0, [P, 512])
        relu_i = place("relu_i", "spare", 2 * KB, [P, 2, 512])
        ki_n = place("ki_n", "spare", 8 * KB, [P, TB, HD])
        ki_c = place("ki_c", "spare", 9 * KB, [P, TB, HD])
        ki_st = place("ki_st", "spare", 10 * KB, [P, TB, 2, HD])
        BLK = [0, 0, 2 * P, 5 * P]
        score = place("score", "spare", 6 * KB, [P, 9 * P])
        ranked = place("ranked", "arena", 74 * KB + 36 * P, [P, 9 * P])
        chosen = place("chosen", "arena", 74 * KB + 72 * P, [P, 9 * P])
        equal = place("equal", "spare", 2 * KB, [P, 512])
        seen = place("seen", "spare", 4 * KB, [P, 512])
        logit = place("logit", "spare", 0, [P, 3, 512])
        probT = place("probT", "spare", 6 * KB, [P, 2, 512])
        soft = [place("soft0", "spare", 10 * KB, [P, 512]), place("soft1", "arena", 86 * KB, [P, 512])]
        hqk = place("hqk", "arena", 16 * KB, [P, 16, S])
        v_ab = place("v_ab", "arena", 48 * KB, [P, TB, 512])
        v_cd = place("v_cd", "arena", 56 * KB, [P, TB, 384])
        bias = place("bias", "arena", 62 * KB, [P, NREL, S])
        basis = place("basis", "spare", 0, [BUCKETS + 3, BIAS_W])
        table = place("table", "spare", 3 * KB, [BUCKETS + 3, NREL])
        bias_v = place("bias_v", "spare", 4 * KB, [NREL, BIAS_W])
        bias_dram = nc.dram_tensor("bias_dram", (NREL, BIAS_W), F32, kind="Internal").ap()
        mem = place("mem", "arena", 16 * KB, [P, 2, D])
        memT_hi = place("memT_hi", "arena", 24 * KB, [P, KT, MEM], F32R)
        memT_lo = place("memT_lo", "arena", 32 * KB, [P, KT, MEM], F32R)
        kxT = place("kxT", "arena", 40 * KB, [P, 2, MEM])
        vx = place("vx", "arena", 42 * KB, [P, 2, MEM])
        qxT = place("qxT", "arena", 44 * KB, [P, 2, S])
        ox = place("ox", "arena", 48 * KB, [P, TB, 256])
        g_last = place("g_last", "arena", 78 * KB, [P, D])

        w_raw = [sem("w_raw0"), sem("w_raw1")]
        w_rounded, w_split, w_used = sem("w_rounded"), sem("w_split"), sem("w_used")
        t_free, t_first = sem("t_free"), sem("t_first")
        n_free, n_ready = sem("n_free"), sem("n_ready")
        hid_act, hid_hi, hid_done = sem("hid_act"), sem("hid_hi"), sem("hid_done")
        row_sq, row_rstd, row_mean, row_norm = sem("row_sq"), sem("row_rstd"), sem("row_mean"), sem("row_norm")
        turned, x_hi_done, x_lo_done = sem("turned"), sem("x_hi_done"), sem("x_lo_done")
        glu_sig, glu_done = sem("glu_sig"), sem("glu_done")
        v_step, a_step, p_step = sem("v_step"), sem("a_step"), sem("p_step")
        ld_x, ld_par, ld_const, ld_res, stored = sem("ld_x"), sem("ld_par"), sem("ld_const"), sem("ld_res"), sem("stored")
        const_set = sem("const_set")
        s5_sq, s5_rstd, s5_u, s5_ut, s5_ut_sb = sem("s5_sq"), sem("s5_rstd"), sem("s5_u"), sem("s5_ut"), sem("s5_ut_sb")
        s5_nat, s5_nat_sb, s5_ang, s5_sin = sem("s5_nat"), sem("s5_nat_sb"), sem("s5_ang"), sem("s5_sin")
        s5_par, s5_outa, s5_outb, s5_inw, s5_dec, s5_du = sem("s5_par"), sem("s5_outa"), sem("s5_outb"), sem("s5_inw"), sem("s5_dec"), sem("s5_du")
        s5_lag, s5_lag_sb, s5_taps, s5_zero = sem("s5_lag"), sem("s5_lag_sb"), sem("s5_taps"), sem("s5_zero")
        s5_int, s5_int_sb, s5_v, s5_rot, s5_cz, s5_y, s5_ysum, s5_gelu = (
            sem("s5_int"), sem("s5_int_sb"), sem("s5_v"), sem("s5_rot"), sem("s5_cz"), sem("s5_y"), sem("s5_ysum"), sem("s5_gelu"))
        x_final = sem("x_final")
        ld_qk, qk_tables = sem("ld_qk"), sem("qk_tables")
        head_sq_done, head_sum, head_rstd, head_norm, head_cos, head_done = (
            sem("head_sq_done"), sem("head_sum"), sem("head_rstd"), sem("head_norm"), sem("head_cos"), sem("head_done"))
        head_t, head_t_sb = sem("head_t"), sem("head_t_sb")
        ki_squared = sem("ki_squared")
        ki_sq, ki_rs, ki_done, ki_t, ki_t_sb = sem("ki_sq"), sem("ki_rs"), sem("ki_done"), sem("ki_t"), sem("ki_t_sb")
        idx_dot, idx_relu, idx_sum, idx_chosen = sem("idx_dot"), sem("idx_relu"), sem("idx_sum"), sem("idx_chosen")
        at_dot, at_ln, at_logit, at_max, at_prob, at_turn, at_turn_sb, at_pv, at_inv, at_out = (
            sem("at_dot"), sem("at_ln"), sem("at_logit"), sem("at_max"), sem("at_prob"), sem("at_turn"),
            sem("at_turn_sb"), sem("at_pv"), sem("at_inv"), sem("at_out"))
        ld_bias, bias_row, bias_row_sb, bias_out, ld_bias_t = (
            sem("ld_bias"), sem("bias_row"), sem("bias_row_sb"), sem("bias_out"), sem("ld_bias_t"))
        grp_sq, grp_rstd, grp_norm = sem("grp_sq"), sem("grp_rstd"), sem("grp_norm")
        ld_mem, mem_sq, mem_rstd, mem_norm, ld_last = sem("ld_mem"), sem("mem_sq"), sem("mem_rstd"), sem("mem_norm"), sem("ld_last")
        gains_t, gains_sb = sem("gains_t"), sem("gains_sb")

        block = ctx.enter_context(nc.Block())

        def f32(ap):
            return ap.bitcast(F32)

        def heads(ap, h):
            return ap[HD * (h % 2):HD * (h % 2) + HD, h // 2, :]

        dsa_units = []
        for b in range(TB):
            for h in range(NH):
                mask = masks[:, 0, :] if b == 0 else chosen[:, BLK[b]:BLK[b] + P * (b + 1)]
                dsa_units.append((heads(qT, h)[:, P * b:P * b + P], heads(kT, h)[:, 0:P * (b + 1)], mask,
                                  [v_dsa[:, k, HD * h:HD * h + HD] for k in range(b + 1)],
                                  o_nat[:, b, HD * h:HD * h + HD], None))

        def hybrid_units(group):
            q_at, k_at, rel, v, v_at = {"a": (0, 2, 0, v_ab, 0), "b": (4, 6, None, v_ab, 256),
                                        "c": (8, 10, 4, v_cd, 0), "d": (12, 14, 8, v_cd, 128)}[group]
            units = []
            for b in range(TB):
                for h in range(4):
                    first = max(0, b - 1) if group == "c" else 0
                    rows = slice(HD * (h % 2), HD * (h % 2) + HD)
                    k_tile = (0, 1, 1, 0)[h] if group == "c" else h // 2
                    v_head = h // 2 if group == "c" else h
                    units.append((hqk[rows, q_at + h // 2, P * b:P * b + P],
                                  hqk[rows, k_at + k_tile, P * first:P * (b + 1)],
                                  None if rel is None else bias[:, rel + h, 0:P * (b + 1 - first)][:, ::-1],
                                  [v[:, k, v_at + HD * v_head:v_at + HD * v_head + HD] for k in range(first, b + 1)],
                                  o_nat[:, b, 256 * "abcd".index(group) + HD * h:256 * "abcd".index(group) + HD * h + HD],
                                  h if group == "c" else None))
            return units

        soft_units = hybrid_units("a") + hybrid_units("c") + hybrid_units("d")
        stick_units = hybrid_units("b")
        mem_units = [(heads(qxT, h)[:, P * b:P * b + P], heads(kxT, h), None,
                      [vx[:, m, HD * h:HD * h + HD] for m in range(2)], ox[:, b, HD * h:HD * h + HD], None)
                     for b in range(TB) for h in range(4)]
        DSA_UNIT, SOFT_UNIT, STICK_UNIT, MEM_UNIT = 0, 64, 112, 128

        @block.sync
        def _(sp):
            sp.dma_start(xp[:, :, :], w["x"].rearrange("(c s) d -> c s d", s=CH)).then_inc(ld_x, 16)
            for j, name in ((0, "s5_lambda_re"), (1, "s5_lambda_im")):
                for half in range(2):
                    sp.dma_start(nat_l[:, j, half, :], w[name][0]).then_inc(ld_par, 16)
            for j, name in ((0, "s5_b_re"), (1, "s5_b_im"), (2, "s5_b_re")):
                sp.dma_start(nat_b[:, j, :, :], w[name][0]).then_inc(ld_par, 16)
            for j, name in ((0, "s5_c_re"), (1, "s5_c_im"), (2, "s5_c_re")):
                sp.dma_start(nat_c[:, :, j, :], w[name][0].rearrange("(b g) h p -> (g h) b p", g=GB)).then_inc(ld_par, 16)
            sp.dma_start(small[:, 0, :], w["s5_log_dt"][0:1, :].broadcast_to([P, G])).then_inc(ld_par, 16)
            sp.dma_start(g_row[:, :], w["norm_mix"][0:1, :].broadcast_to([NC, D])).then_inc(ld_par, 16)
            sp.dma_start(d_row[:, :], w["s5_d"][0:1, :].broadcast_to([NC, D])).then_inc(ld_par, 16)

            def slot_free(g):
                sp.wait_ge(w_split, g - 1)

            def put(par, dst, src):
                sp.dma_start(dst, src).then_inc(w_raw[par], 16)

            def load_pair(par, a, b, n):
                v = raw[:, par, 0:KT * 2 * n].rearrange("p (k t n) -> p k t n", t=2, n=n)
                put(par, v[:, :, 0, :], a)
                put(par, v[:, :, 1, :], b)

            def load_rows(par, src, n):
                m = src.shape[1]
                v = raw[:, par, 0:m * n].rearrange("p (k n) -> p k n", n=n)
                put(par, v[:, 0:m // 2, :], src[:, 0:m // 2, :])
                put(par, v[:, m // 2:m, :], src[:, m // 2:m, :])

            def tiles(ap):
                return ap.rearrange("(k p) n -> p k n", p=P)

            glu = tiles(w["s5_w_glu"][0])
            for j in range(4):
                for k in range(0, KT, 4):
                    g = GLU_SLOT + 2 * j + k // 4
                    if g >= 2:
                        slot_free(g)
                    v = raw[:, g % 2, :].rearrange("p (k t n) -> p k t n", t=2, n=256)
                    put(g % 2, v[:, :, 0, :], glu[:, k:k + 4, 256 * j:256 * j + 256])
                    put(g % 2, v[:, :, 1, :], glu[:, k:k + 4, D + 256 * j:D + 256 * j + 256])
                if j == 0:
                    sp.wait_ge(s5_zero, 1)
                    for b in range(NB):
                        sp.wait_ge(s5_lag_sb, b + 1)
                        if b >= 1:
                            sp.wait_ge(s5_y, b)
                        for s in range(CH):
                            sp.dma_start(taps[GH * s:GH * s + GH, :, s:CH, :].rearrange("p g t h -> p g (t h)"),
                                         lag[:, :, 0:CH - s, :].rearrange("p g t h -> p g (t h)")).then_inc(s5_taps, 16)
                    sp.wait_ge(s5_gelu, NB)
                    sp.dma_start(x_res[:, :, :], w["x"].rearrange("(b p) d -> p b d", p=P)).then_inc(ld_res, 16)

            def ffn_loads(layer):
                up = tiles(w["ffn_w_gate_up"][layer])
                down = tiles(w["ffn_w_down"][layer])
                g0 = FFN_SLOT[layer]
                with sp.Fori(0, FT // 2) as i:
                    for j in range(2):
                        slot_free(i * 2 + (g0 + j))
                        v = raw[:, (g0 + j) % 2, :].rearrange("p (k t n) -> p k t n", t=2, n=P)
                        put((g0 + j) % 2, v[:, :, 0, :], up[:, :, bass.ds(i * (2 * P) + j * P, P)])
                        put((g0 + j) % 2, v[:, :, 1, :], up[:, :, bass.ds(i * (2 * P) + (FF + j * P), P)])
                g0 += FT
                with sp.Fori(0, 2) as i:
                    k = 0
                    for j, m in enumerate(FFN_DOWN):
                        slot_free(i * len(FFN_DOWN) + (g0 + j))
                        load_rows((g0 + j) % 2, down[:, k:k + m, bass.ds(i * 512, 512)], 512)
                        k += m

            ffn_loads(0)

            def panel_loads(g0, src, n, kt=KT):
                for k in range(0, kt, 4):
                    slot_free(g0 + k // 4)
                    load_rows((g0 + k // 4) % 2, src[:, k:k + 4, :], n)

            w_in = tiles(w["dsa_w_in"][0])
            panel_loads(DSA_SLOT, w_in[:, :, 3 * D:3 * D + 512], 512)
            slot_free(DSA_SLOT + 2)
            load_rows((DSA_SLOT + 2) % 2, w_in[:, :, 3 * D + 512:DSA_W], DSA_W - 3 * D - 512)
            for j in range(6):
                panel_loads(DSA_SLOT + 3 + 2 * j, w_in[:, :, 512 * j:512 * j + 512], 512)
            for j in range(2):
                panel_loads(WO_SLOT + 2 * j, tiles(w["dsa_w_o"][0])[:, :, 512 * j:512 * j + 512], 512)
            ffn_loads(1)

            sp.wait_ge(n_free, TB * (FFN_PANEL[1] + 3))
            sp.dma_start(basis[:, :], w["c_basis"]).then_inc(ld_bias, 16)
            sp.dma_start(table[0:BUCKETS, :], w["rel_table_2"]).then_inc(ld_bias, 16)
            sp.dma_start(table[BUCKETS:BUCKETS + 3, :], w["c_pick"]).then_inc(ld_bias, 16)
            w_h = tiles(w["w_in_2"][0])

            def h_slot(g, c):
                slot_free(g)
                load_pair(g % 2, w_h[:, :, c:c + P], w_h[:, :, c + P:c + 2 * P], P)

            h_slot(HIN_SLOT, 0)
            h_slot(HIN_SLOT + 1, 256)
            sp.wait_ge(bias_row_sb, 1)
            sp.dma_start(bias_dram, bias_v[:, :]).then_inc(bias_out, 16)
            sp.wait_ge(bias_out, 16)
            sp.dma_start(bias[:, :, :], bass.AP(tensor=bias_dram.tensor, offset=0, ap=[[1, P], [BIAS_W, NREL], [1, S]]))\
              .then_inc(ld_bias_t, 16)
            for j, c in enumerate((768, 1024, 1536)):
                h_slot(HIN_SLOT + 2 + j, c)
            g = HIN_SLOT + 5
            slot_free(g)
            v = raw[:, g % 2, 0:KT * 192].rearrange("p (k n) -> p k n", n=192)
            put(g % 2, v[:, :, 0:P], w_h[:, :, 1792:1920])
            put(g % 2, v[:, :, P:192], w_h[:, :, 1792:1856])
            for j, c in enumerate((2048, 2304)):
                h_slot(HIN_SLOT + 6 + j, c)
            for k in range(0, KT, 4):
                g = HIN_SLOT + 8 + k // 4
                slot_free(g)
                v = raw[:, g % 2, :].rearrange("p (k t n) -> p k t n", t=2, n=256)
                put(g % 2, v[:, :, 0, :], w_h[:, k:k + 4, 512:768])
                put(g % 2, v[:, :, 1, :], w_h[:, k:k + 4, 1280:1536])
            for k in range(0, KT, 4):
                g = HIN_SLOT + 10 + k // 4
                slot_free(g)
                v = raw[:, g % 2, 0:4 * 384].rearrange("p (k n) -> p k n", n=384)
                put(g % 2, v[:, :, 0:P], w_h[:, k:k + 4, 1920:2048])
                put(g % 2, v[:, :, P:384], w_h[:, k:k + 4, 2560:2816])
            for j in range(2):
                panel_loads(HOUT_SLOT + 2 * j, tiles(w["w_out_2"][0])[:, :, 512 * j:512 * j + 512], 512)
                if j == 0:
                    sp.wait_ge(at_out, MEM_UNIT)
                    sp.dma_start(mem[:, :, :], w["mem_2"].rearrange("(b p) d -> p b d", p=P)).then_inc(ld_mem, 16)

            w_kv, w_q = tiles(w["w_xkv_2"][0]), tiles(w["w_xq_2"][0])
            slot_free(MEM_SLOT)
            load_pair(MEM_SLOT % 2, w_kv[:, :, 0:P], w_kv[:, :, P:2 * P], P)
            slot_free(MEM_SLOT + 1)
            load_rows((MEM_SLOT + 1) % 2, w_kv[:, :, 256:512], 256)
            slot_free(XQ_SLOT)
            load_pair(XQ_SLOT % 2, w_q[:, :, 0:P], w_q[:, :, P:2 * P], P)
            slot_free(XO_SLOT)
            load_rows(XO_SLOT % 2, tiles(w["w_xo_2"][0]), D)
            sp.dma_start(g_last[:, :], w["g_final_2"].rearrange("(a d) -> a d", a=1).broadcast_to([P, D])).then_inc(ld_last, 16)

            up, down = tiles(w["w_up_2"][0]), tiles(w["w_down_2"][0])
            for part in range(MLP_PARTS):
                g0 = MLP_SLOT[part]
                with sp.Fori(0, MT // 4) as i:
                    for j in range(2):
                        slot_free(i * 2 + (g0 + j))
                        c = MT * P * part + 2 * P * j
                        load_pair((g0 + j) % 2, up[:, :, bass.ds(i * (4 * P) + c, P)],
                                  up[:, :, bass.ds(i * (4 * P) + (c + P), P)], P)
                g0 += MT // 2
                with sp.Fori(0, 2) as i:
                    for j in range(MT // 4):
                        slot_free(i * (MT // 4) + (g0 + j))
                        k = MT * part + 4 * j
                        load_rows((g0 + j) % 2, down[:, k:k + 4, bass.ds(i * 512, 512)], 512)

            for tb in range(TB):
                sp.wait_ge(x_final, tb + 1)
                sp.dma_start(out[P * tb:P * tb + P, :], xn[:, tb, :]).then_inc(stored, 16)
            sp.wait_ge(stored, 16 * TB)

        @block.gpsimd
        def _(pool):
            steps = [0]

            def link(ins):
                ins.then_inc(p_step, 1)
                steps[0] += 1
                pool.wait_ge(p_step, steps[0])

            pool.memset(taps[:, :, :, :], 0.0).then_inc(s5_zero, 1)
            link(pool.memset(half_neg[:, :], -0.5))
            link(pool.memset(decay[:, :, 0:1], 0.0))
            pool.memset(one[:, :], 1.0).then_inc(const_set, 1)

            def rsqrt(dst, src, n, scale, parts=P):
                link(pool.tensor_scalar(dst, src, scale, EPS, ALU.mult, ALU.add))
                return pool.tensor_tensor(dst, dst, half_neg[0:parts, 0:n], ALU.pow)

            pool.wait_ge(s5_sq, CH)
            rsqrt(rstd[0:NC, 0:CH], ssq[0:NC, 0:CH], CH, 1.0 / D, NC).then_inc(s5_rstd, 1)

            pool.wait_ge(s5_par, 1)
            pool.wait_ge(s5_u, CH)
            for b in range(NB):
                gs = slice(GB * b, GB * b + GB)
                cn = c_n[:, gs, :].unsqueeze(2).broadcast_to([P, GB, CH, GH])
                cs = c_s[:, gs, :].unsqueeze(2).broadcast_to([P, GB, CH, GH])
                pr = pw_r[:, gs, 1:CH + 1].unsqueeze(3).broadcast_to([P, GB, CH, GH])
                pi = pw_is[:, gs, 1:CH + 1].unsqueeze(3).broadcast_to([P, GB, CH, GH])
                if b >= 1:
                    pool.wait_ge(s5_cz, b)
                pool.tensor_copy(decay[:, :, 1:NC], r8[:, gs].unsqueeze(2).broadcast_to([P, GB, NC - 1])).then_inc(s5_dec, 1)
                if b >= 1:
                    pool.wait_ge(s5_gelu, b)
                pool.tensor_tensor(du[:, :, :, :], u[:, gs, :, :],
                                   d_row[:, P * b:P * b + P].rearrange("p (g h) -> p g h", h=GH).unsqueeze(2).broadcast_to([NC, GB, CH, GH]),
                                   ALU.mult).then_inc(s5_du, 1)
                if b >= 1:
                    pool.wait_ge(s5_y, b)
                link(pool.tensor_tensor(out_b[:, :, :, :], cn, pi, ALU.mult))
                link(pool.tensor_tensor(tmp_b[:, :, :, :], cs, pr, ALU.mult))
                pool.tensor_tensor(out_b[:, :, :, :], out_b[:, :, :, :], tmp_b[:, :, :, :], ALU.subtract).then_inc(s5_outb, 1)

            def split_rest(g, par):
                pool.wait_ge(w_rounded, g + 1)
                pool.tensor_tensor(w_lo[:, par, :], raw[:, par, :], f32(w_hi[:, par, :]), ALU.subtract).then_inc(w_split, 1)

            def split_run(g0, n):
                for g in range(g0, g0 + n):
                    if g < SLOTS:
                        split_rest(g, g % 2)

            def norm_rstd(n):
                pool.wait_ge(row_sq, TB * (n + 1))
                rsqrt(rstd[:, 0:TB], ssq[:, 0:TB], TB, 1.0 / D).then_inc(row_rstd, 1)

            split_run(0, 2 + GLU_SLOTS)
            norm_rstd(0)

            def ffn_split(layer):
                g0 = FFN_SLOT[layer] + 2
                with pool.Fori(0, FT // 2) as i:
                    for j in range(2):
                        split_rest(i * 2 + (g0 + j), (g0 + j) % 2)
                g0 += FT
                split_run(g0, 2 * len(FFN_DOWN))

            ffn_split(0)
            norm_rstd(1)

            def head_rotate(e, table, tb, normed=True):
                if normed:
                    n = e - TB
                    pool.wait_ge(head_sum, n + 1)
                    if n >= 2:
                        pool.wait_ge(head_norm, e - 1)
                    rsqrt(head_rs[:, e % 2, :], head_ss[:, e % 2, :], 8, 1.0 / HD).then_inc(head_rstd, 1)
                pool.wait_ge(head_norm, e + 1)
                if e >= 2:
                    pool.wait_ge(head_done, e - 1)
                pool.tensor_tensor(head_c[:, e % 2, :].rearrange("p (h d) -> p h d", d=HD),
                                   head_n[:, e % 2, :].rearrange("p (h d) -> p h d", d=HD),
                                   table[:, 0, tb, :].unsqueeze(1).broadcast_to([P, 8, HD]), ALU.mult).then_inc(head_cos, 1)

            pool.wait_ge(qk_tables, 1)
            split_run(DSA_SLOT + 2, 1)
            for tb in range(TB):
                head_rotate(tb, rope, tb, False)
            split_run(DSA_SLOT + 3, 1)
            split_run(DSA_SLOT + 4, 1)
            pool.wait_ge(ki_sq, 1)
            rsqrt(head_rs[:, 0, 0:TB], head_ss[:, 0, 0:TB], TB, 1.0 / HD).then_inc(ki_rs, 1)
            for j in range(4):
                split_run(DSA_SLOT + 5 + 2 * j, 1)
                for tb in range(TB):
                    head_rotate(TB * (1 + j) + tb, rope_q if j < 2 else rope_k, tb)
                split_run(DSA_SLOT + 6 + 2 * j, 1)
            split_run(DSA_SLOT + 13, 8)

            norm_rstd(2)
            ffn_split(1)
            norm_rstd(3)
            split_run(HIN_SLOT + 2, 12)
            pool.wait_ge(grp_sq, 4 * TB)
            rsqrt(rstd[:, 16:32], ssq[:, 16:32], 16, 1.0 / 256).then_inc(grp_rstd, 1)
            pool.wait_ge(mem_sq, 2)
            rsqrt(rstd[:, 32:34], ssq[:, 32:34], 2, 1.0 / D).then_inc(mem_rstd, 1)
            split_run(HOUT_SLOT + 2, 4)
            split_run(MEM_SLOT + 2, 2)
            norm_rstd(4)
            split_run(XQ_SLOT + 2, 2)
            norm_rstd(5)
            for part in range(MLP_PARTS):
                g0 = MLP_SLOT[part] + 2
                with pool.Fori(0, MT // 4) as i:
                    for j in range(2):
                        split_rest(i * 2 + (g0 + j), (g0 + j) % 2)
                split_run(g0 + MT // 2, MT // 2)
            norm_rstd(6)

        @block.scalar
        def _(act):
            act.dma_start(ident[:, :], w["c_ident"]).then_inc(ld_const, 16)
            act.dma_start(sign[:, :], w["c_sign"]).then_inc(ld_const, 16)
            act.dma_start(masks[:, :, :], w["c_masks"]).then_inc(ld_const, 16)
            row = 0
            for name in ("norm_mix", "norm_ffn", "g_mix_2", "g_cross_2", "g_mem_2", "g_mlp_2", "g_group_2"):
                n = w[name].shape[0] * KT
                act.dma_start(gain_rows[row:row + n, :], w[name].rearrange("a (k p) -> (a k) p", p=P)).then_inc(ld_const, 16)
                row += n

            act.dma_start(rope[:, :, :, :], w["c_rope"]).then_inc(ld_qk, 16)
            for j, name in enumerate(("dsa_q_norm", "dsa_k_norm")):
                act.dma_start(gain_qk[:, j, :], w[name][0:1, :].broadcast_to([P, HD])).then_inc(ld_qk, 16)
            act.dma_start(sinks[:, :], w["sinks_2"][0:1, :].broadcast_to([P, 4])).then_inc(ld_qk, 16)
            steps = [0]

            def link(ins):
                ins.then_inc(a_step, 1)
                steps[0] += 1
                act.wait_ge(a_step, steps[0])

            act.wait_ge(ld_x, 16)
            for s in range(CH):
                if s >= 1:
                    act.wait_ge(s5_sq, s)
                act.activation(junk[:, :], xp[:, s, :], ACT.Square, accum_out=ssq[0:NC, s:s + 1]).then_inc(s5_sq, 1)
            act.wait_ge(s5_nat, 1)
            act.activation(small[:, 1:3, :].rearrange("p a g -> p (a g)"), PS[:, 0, 0:2 * G], ACT.Copy).then_inc(s5_nat_sb, 1)
            act.wait_ge(s5_nat, 2)
            act.activation(b_n[:, :, :].rearrange("p g h -> p h g"),
                           PS[:, 1:3, :].rearrange("p b (h g) -> p (b h) g", g=G), ACT.Copy).then_inc(s5_nat_sb, 1)
            act.wait_ge(s5_nat, 3)
            act.activation(b_s[:, :, :].rearrange("p g h -> p h g"),
                           PS[:, 3:5, :].rearrange("p b (h g) -> p (b h) g", g=G), ACT.Copy).then_inc(s5_nat_sb, 1)
            act.wait_ge(s5_nat, 4)
            act.activation(c_n[:, :, :].rearrange("p g h -> p (g h)"), PS[:, 5:7, :].rearrange("p b n -> p (b n)"), ACT.Copy).then_inc(s5_nat_sb, 1)
            act.wait_ge(s5_nat, 5)
            act.activation(c_s[:, 0:G // 2, :].rearrange("p g h -> p (g h)"), PS[:, 7, :], ACT.Copy).then_inc(s5_nat_sb, 1)
            act.wait_ge(s5_nat, 6)
            act.activation(c_s[:, G // 2:G, :].rearrange("p g h -> p (g h)"), PS[:, 1, :], ACT.Copy).then_inc(s5_nat_sb, 1)
            act.wait_ge(gains_t, 1)
            act.activation(gains[:, :], PS[:, 0, 0:len(GAINS) * KT], ACT.Copy).then_inc(gains_sb, 1)
            act.wait_ge(s5_ang, 1)
            act.activation(small[:, 12, :], small[:, 11, :], ACT.Sin).then_inc(s5_sin, 1)
            act.activation(small[:, 13, :], small[:, 11, :], ACT.Sin, scale=0.5).then_inc(s5_sin, 1)
            for q in range(8):
                act.wait_ge(s5_ut, q + 1)
                act.activation(uT[:, GB * q:GB * q + GB, :].rearrange("p g c -> p (g c)"), PS[:, q, :], ACT.Copy).then_inc(s5_ut_sb, 1)

            def gelu(b):
                act.wait_ge(s5_ysum, b + 1)
                act.activation(y[:, b, :, :].rearrange("p t (g h) -> p g t h", h=GH), du[:, :, :, :], ACT.Gelu_apprx_tanh).then_inc(s5_gelu, 1)

            for b in range(NB):
                act.wait_ge(s5_lag, b + 1)
                if b >= 1:
                    act.wait_ge(s5_taps, 16 * CH * b)
                act.activation(lag[:, :, :, :].rearrange("p g t h -> p (g t h)"),
                               PS[0:GH, 0:2, :].rearrange("p b n -> p (b n)"), ACT.Copy).then_inc(s5_lag_sb, 1)
                act.wait_ge(s5_int, b + 1)
                if b >= 1:
                    act.wait_ge(s5_v, b)
                pt = PS[:, 2:4, :].rearrange("p b (g r q) -> p (b g) r q", r=2, q=GP)
                act.activation(in_t[:, :, :, :], pt, ACT.Copy)
                act.activation(in_s[:, :, 0, :], pt[:, :, 1, :], ACT.Copy)
                act.activation(in_s[:, :, 1, :], pt[:, :, 0, :], ACT.Copy, scale=-1.0).then_inc(s5_int_sb, 1)
                if b >= 1:
                    gelu(b - 1)
            gelu(NB - 1)

            def turn_hi(j0, n, gain=None, width=S, dst=xT_hi, view=None):
                for k in range(n):
                    act.wait_ge(turned, j0 + k + 1)
                    o, i = dst[:, k, 0:width], PS[:, k % 4, 0:width]
                    if view:
                        o, i = view(o, i)
                    act.activation(o, i, ACT.Copy, scale=1.0 if gain is None else gains[:, gain * KT + k:gain * KT + k + 1]).then_inc(x_hi_done, 1)

            turn_hi(0, KT, view=chunk_view)

            def round_slot(g, par, use):
                act.wait_ge(w_raw[par], use * 32)
                if not isinstance(g, int) or g >= 2:
                    act.wait_ge(w_used, g - 1)
                act.activation(w_hi[:, par, :], raw[:, par, :], ACT.Copy).then_inc(w_rounded, 1)

            def round_run(g0, n):
                for g in range(g0, g0 + n):
                    if g < SLOTS:
                        round_slot(g, g % 2, g // 2 + 1)

            round_run(0, 2)
            act.wait_ge(ld_res, 16)
            for j in range(4):
                round_run(2 + 2 * j, 1)
                for tb in range(TB):
                    e = TB * j + tb
                    if tb < TB - 1:
                        act.wait_ge(n_ready, 3 * (GLU_PANEL + j) + tb + 1)
                    else:
                        act.wait_ge(w_used, GLU_SLOT + 2 * j + 2)
                    if e >= 2:
                        act.wait_ge(n_free, TB + e - 1)
                    act.activation(glu_sg[:, e % 2, :], PS[:, 4 + tb, 256:512], ACT.Sigmoid).then_inc(glu_sig, 1)
                round_run(3 + 2 * j, 1)

            def norm_sq(n, sem_x, value):
                act.wait_ge(sem_x, value)
                for tb in range(TB):
                    if n + tb >= 1:
                        act.wait_ge(row_sq, TB * n + tb)
                    act.activation(sq_junk[:, :], x_res[:, tb, :], ACT.Square, accum_out=ssq[:, tb:tb + 1]).then_inc(row_sq, 1)

            norm_sq(0, glu_done, 4 * TB)
            turn_hi(KT, KT, gain=2)

            def ffn_act(layer):
                g0, t0, h0 = FFN_SLOT[layer], FFN_TILE[layer], FFN_HID[layer]
                with act.Fori(0, FT // 2) as i:
                    for j in range(2):
                        pair = (t0 + j) % 2
                        act.wait_ge(t_first, i * 2 + (t0 + j + 1))
                        act.wait_ge(hid_done, i * 2 + (h0 + j + 1))
                        act.activation(gbuf[:, pair, 0, :], PS[:, 2 * pair, :], ACT.Silu).then_inc(hid_act, 1)
                        g = g0 + j + 2
                        round_slot(i * 2 + g, g % 2, i + (g // 2 + 1))
                round_run(g0 + FT + 2, 2 * len(FFN_DOWN))

            ffn_act(0)
            norm_sq(1, n_free, TB * (FFN_PANEL[0] + 3))
            turn_hi(2 * KT, KT, gain=1)

            def panel_wait(ni, tb, g_last_slot):
                if tb < TB - 1:
                    act.wait_ge(n_ready, 3 * ni + tb + 1)
                else:
                    act.wait_ge(w_used, g_last_slot + 1)

            def head_turned(pi, dst, at):
                for j in range(4):
                    act.wait_ge(head_t, 4 * pi + j + 1)
                    act.activation(dst[:, at + j, :], PS[:, j, :], ACT.Copy).then_inc(head_t_sb, 1)

            g = DSA_SLOT
            round_run(g + 2, 1)
            for tb in range(TB):
                panel_wait(DSA_PANEL, tb, g + 1)
                if tb >= 2:
                    act.wait_ge(head_done, tb - 1)
                act.activation(head_n[:, tb % 2, :], PS[:, 4 + tb, :], ACT.Copy).then_inc(head_norm, 1)
            round_run(g + 3, 1)
            round_run(g + 4, 1)
            act.wait_ge(w_used, g + 3)
            act.wait_ge(head_norm, TB)
            act.activation(ki_c[:, :, :], PS[:, 4:8, 0:HD], ACT.Square).then_inc(ki_squared, 1)
            for j in range(4):
                round_run(g + 5 + 2 * j, 1)
                for tb in range(TB):
                    n = TB * j + tb
                    panel_wait(DSA_PANEL + 2 + j, tb, g + 4 + 2 * j)
                    if n >= 2:
                        act.wait_ge(head_sum, n - 1)
                    act.activation(head_sq[:, n % 2, :], PS[:, 4 + tb, :], ACT.Square).then_inc(head_sq_done, 1)
                round_run(g + 6 + 2 * j, 1)
                if j == 0:
                    head_turned(0, qiT, 0)
                    act.wait_ge(ki_t, 1)
                    act.activation(kiT[:, :], PS[:, 0, :], ACT.Copy).then_inc(ki_t_sb, 1)
                    for e in range(3 * NI):
                        n = P * (e // NI + 2)
                        act.wait_ge(idx_dot, e + 1)
                        if e >= 2:
                            act.wait_ge(idx_sum, e - 1)
                        act.activation(relu_i[:, e % 2, 0:n], PS[:, e % 4, 0:n], ACT.Relu, scale=HD ** -0.5).then_inc(idx_relu, 1)
                else:
                    head_turned(j, qT if j < 3 else kT, (0, 0, 4, 0)[j])
            for j in range(2):
                round_run(g + 13 + 2 * j, 1)
                for tb in range(TB):
                    panel_wait(DSA_PANEL + 6 + j, tb, g + 12 + 2 * j)
                    act.activation(v_dsa[:, tb, 512 * j:512 * j + 512], PS[:, 4 + tb, :], ACT.Copy).then_inc(n_free, 1)
                round_run(g + 14 + 2 * j, 1)
                if j == 0:
                    head_turned(4, kT, 4)

            def attend_act(units, u0, stick=False):
                late = 1 if stick else 0
                n = len(units)
                for t in range(n + 3):
                    if stick and t < n:
                        cols = units[t][1].shape[1]
                        part = soft[t % 2][:, 0:cols]
                        act.wait_ge(at_dot, u0 + t + 1)
                        if t >= 2:
                            act.wait_ge(at_logit, u0 + t - 1)
                        link(act.activation(part, PS[:, t % 3, 0:cols], ACT.Abs))
                        link(act.activation(part, part, ACT.Exp, scale=-1.0))
                        act.activation(part, part, ACT.Ln, bias=1.0).then_inc(at_ln, 1)
                    e = t - late
                    if 0 <= e < n:
                        cols, sink = units[e][1].shape[1], units[e][5]
                        act.wait_ge(at_max, u0 + e + 1)
                        p = logit[:, e % 3, 0:cols]
                        if stick:
                            act.activation(p, p, ACT.Exp).then_inc(at_prob, 1)
                        else:
                            m = neg_max[:, e % 4:e % 4 + 1]
                            if sink is not None:
                                act.activation(sink_e[:, e % 4:e % 4 + 1], sinks[:, sink:sink + 1], ACT.Exp, bias=m)
                            act.activation(p, p, ACT.Exp, bias=m, accum_out=row_sum[:, e % 4:e % 4 + 1]).then_inc(at_prob, 1)
                    e = t - 2
                    if 0 <= e < n:
                        cols = units[e][1].shape[1]
                        act.wait_ge(at_turn, u0 + e + 1)
                        if e >= 2:
                            act.wait_ge(at_pv, u0 + e - 1)
                        act.activation(probT[:, e % 2, 0:cols], PS[:, 3 + e % 2, 0:cols], ACT.Copy).then_inc(at_turn_sb, 1)

            attend_act(dsa_units, DSA_UNIT)
            turn_hi(3 * KT, KT)
            round_run(WO_SLOT + 2, 4)
            norm_sq(2, n_free, TB * (WO_PANEL + 3))
            turn_hi(4 * KT, KT, gain=3)
            ffn_act(1)

            norm_sq(3, n_free, TB * (FFN_PANEL[1] + 3))
            act.wait_ge(bias_row, 1)
            act.activation(bias_v[:, 0:512], PS[0:NREL, 4, :], ACT.Copy)
            act.activation(bias_v[:, 512:BIAS_W], PS[0:NREL, 5, 0:BIAS_W - 512], ACT.Copy).then_inc(bias_row_sb, 1)
            turn_hi(5 * KT, KT, gain=4)

            def tiles_out(g, ti, dst, scale=1.0, width=S):
                pair = ti % 2
                act.wait_ge(t_first, ti + 1)
                act.activation(dst[:, 0, :], PS[:, 2 * pair, 0:width], ACT.Copy, scale=scale)
                act.wait_ge(w_used, g + 1)
                act.activation(dst[:, 1, :], PS[:, 2 * pair + 1, 0:width], ACT.Copy, scale=scale).then_inc(t_free, 1)

            for j in range(8):
                tiles_out(HIN_SLOT + j, HIN_TILE + j, hqk[:, 2 * j:2 * j + 2, :], HD ** -0.5 if j % 2 == 0 else 1.0)
                round_run(HIN_SLOT + j + 2, 1)
            for j, (dst, n) in enumerate(((v_ab, 512), (v_cd, 384))):
                g = HIN_SLOT + 8 + 2 * j
                round_run(g + 2, 1)
                for tb in range(TB):
                    panel_wait(HIN_PANEL + j, tb, g + 1)
                    act.activation(dst[:, tb, :], PS[:, 4 + tb, 0:n], ACT.Copy).then_inc(n_free, 1)
                round_run(g + 3, 1)
            attend_act(soft_units, SOFT_UNIT)
            attend_act(stick_units, STICK_UNIT, stick=True)
            act.wait_ge(at_out, MEM_UNIT)
            for tb in range(TB):
                for j in range(4):
                    e = 4 * tb + j
                    if e >= 1:
                        act.wait_ge(grp_sq, e)
                    act.activation(sq_junk[:, 0:256], o_nat[:, tb, 256 * j:256 * j + 256], ACT.Square,
                                   accum_out=ssq[:, 16 + e:17 + e]).then_inc(grp_sq, 1)
            turn_hi(6 * KT, KT, gain=8)
            act.wait_ge(ld_mem, 16)
            for m in range(2):
                if m == 0:
                    act.wait_ge(grp_sq, 4 * TB)
                else:
                    act.wait_ge(mem_sq, 1)
                act.activation(sq_junk[:, :], mem[:, m, :], ACT.Square, accum_out=ssq[:, 32 + m:33 + m]).then_inc(mem_sq, 1)
            round_run(HOUT_SLOT + 2, 4)

            turn_hi(7 * KT, KT, gain=6, width=MEM, dst=memT_hi)
            tiles_out(MEM_SLOT, MEM_TILE, kxT, width=MEM)
            round_run(MEM_SLOT + 2, 1)
            act.wait_ge(n_ready, 3 * MEM_PANEL + 3)
            act.activation(vx[:, 0, :], PS[:, 4, 0:MEM], ACT.Copy)
            act.wait_ge(w_used, MEM_SLOT + 2)
            act.activation(vx[:, 1, :], PS[:, 5, 0:MEM], ACT.Copy).then_inc(n_free, TB)
            round_run(MEM_SLOT + 3, 1)
            norm_sq(4, n_free, TB * (HOUT_PANEL + 3))
            turn_hi(8 * KT, KT, gain=5)
            tiles_out(XQ_SLOT, XQ_TILE, qxT, HD ** -0.5)
            round_run(XQ_SLOT + 2, 1)
            attend_act(mem_units, MEM_UNIT)
            turn_hi(9 * KT, 2)
            round_run(XO_SLOT + 2, 1)

            norm_sq(5, n_free, TB * (XO_PANEL + 3))
            turn_hi(9 * KT + 2, KT, gain=7)
            for part in range(MLP_PARTS):
                g0, t0, h0 = MLP_SLOT[part], MLP_TILE[part], MLP_HID[part]
                with act.Fori(0, MT // 4) as i:
                    for j in range(2):
                        pair = (t0 + j) % 2
                        act.wait_ge(t_first, i * 2 + (t0 + j + 1))
                        act.wait_ge(hid_done, i * 2 + (h0 + j + 1))
                        act.activation(gbuf[:, pair, 0, :], PS[:, 2 * pair, :], ACT.Relu)
                        act.wait_ge(w_used, i * 2 + (g0 + j + 1))
                        act.activation(gbuf[:, pair, 1, :], PS[:, 2 * pair + 1, :], ACT.Relu).then_inc(t_free, 1)
                        g = g0 + j + 2
                        round_slot(i * 2 + g, g % 2, i + (g // 2 + 1))
                round_run(g0 + MT // 2 + 2, MT // 2)
            norm_sq(6, n_free, TB * (MLP_PANEL[1] + 3))

        @block.vector
        def _(dve):
            steps = [0]

            def link(ins):
                ins.then_inc(v_step, 1)
                steps[0] += 1
                dve.wait_ge(v_step, steps[0])

            def pt(i):
                return small[:, i, :]

            tt, ts, stt = dve.tensor_tensor, dve.tensor_scalar, dve.scalar_tensor_tensor
            dve.memset(neg_max[:, 0:1], 0.0).then_inc(t_free, 2)
            dve.memset(neg_max[:, 1:2], 0.0).then_inc(n_free, TB)
            dve.memset(neg_max[:, 2:3], 0.0).then_inc(hid_done, 2)

            def exp_small(dst, x, a, b, c):
                link(ts(a, x, 88.0, -87.0, ALU.min, ALU.max))
                link(ts(b.bitcast(I32), a, 1.4426950408889634, None, ALU.mult))
                link(dve.tensor_copy(c, b.bitcast(I32)))
                link(stt(a, c, -0.693359375, a, ALU.mult, ALU.add))
                link(stt(a, c, 2.12194440e-4, a, ALU.mult, ALU.add))
                link(ts(b.bitcast(I32), c, 127.0, 8388608.0, ALU.add, ALU.mult))
                link(ts(c, a, 1.0 / 5040, None, ALU.mult))
                for f in (720, 120, 24, 6, 2, 1):
                    link(stt(c, c, 1.0 / f, a, ALU.add, ALU.mult))
                link(stt(dst, c, 1.0, b, ALU.add, ALU.mult))

            dve.wait_ge(ld_par, 16 * 13)
            dve.wait_ge(ld_const, 16 * 10)
            dve.wait_ge(s5_nat_sb, 1)
            exp_small(pt(3), pt(0), pt(4), pt(5), pt(6))
            link(tt(pt(7), pt(1), pt(3), ALU.mult))
            exp_small(pt(8), pt(7), pt(4), pt(5), pt(6))
            link(tt(pt(9), pt(2), pt(3), ALU.mult))
            link(ts(pt(5).bitcast(I32), pt(9), 0.15915494309189535, None, ALU.mult))
            link(dve.tensor_copy(pt(6), pt(5).bitcast(I32)))
            link(stt(pt(9), pt(6), -6.28125, pt(9), ALU.mult, ALU.add))
            link(stt(pt(9), pt(6), -1.9353071795864769e-3, pt(9), ALU.mult, ALU.add))
            ts(pt(11), pt(9), 3.1415925, -3.1415925, ALU.min, ALU.max).then_inc(s5_ang, 1)
            dve.wait_ge(s5_sin, 2)
            link(tt(pt(14), pt(13), pt(13), ALU.mult))
            link(ts(pt(14), pt(14), -2.0, 1.0, ALU.mult, ALU.add))
            link(tt(pw_r[:, :, 1], pt(8), pt(14), ALU.mult))
            link(tt(pw_i[:, :, 1], pt(8), pt(12), ALU.mult))
            link(dve.memset(pw_r[:, :, 0], 1.0))
            link(dve.memset(pw_i[:, :, 0], 0.0))
            link(tt(pt(4), pt(8), pt(8), ALU.mult))
            link(tt(pt(4), pt(4), pt(4), ALU.mult))
            link(tt(r8[:, :], pt(4), pt(4), ALU.mult))
            link(tt(pt(4), pt(1), pt(1), ALU.mult))
            link(tt(pt(5), pt(2), pt(2), ALU.mult))
            link(tt(pt(4), pt(4), pt(5), ALU.add))
            link(dve.reciprocal(pt(4), pt(4)))
            link(ts(pt(5), pw_r[:, :, 1], -1.0, None, ALU.add))
            link(tt(pt(15), pt(5), pt(1), ALU.mult))
            link(tt(pt(16), pw_i[:, :, 1], pt(2), ALU.mult))
            link(tt(pt(15), pt(15), pt(16), ALU.add))
            link(tt(pt(15), pt(15), pt(4), ALU.mult))
            link(tt(pt(16), pw_i[:, :, 1], pt(1), ALU.mult))
            link(tt(pt(17), pt(5), pt(2), ALU.mult))
            link(tt(pt(16), pt(16), pt(17), ALU.subtract))
            link(tt(pt(16), pt(16), pt(4), ALU.mult))
            link(ts(pt(16), pt(16), sign[:, 0:1], None, ALU.mult))
            qr = pt(15).unsqueeze(2).broadcast_to([P, G, GH])
            qi = pt(16).unsqueeze(2).broadcast_to([P, G, GH])

            def rot(buf, k):
                return buf[:, 32 * k:32 * k + 32, :].rearrange("p a b -> p (a b)").rearrange("p (g h) -> p g h", h=GH)

            dve.wait_ge(s5_nat_sb, 6)
            link(tt(rot(rot1, 0), b_n[:, :, :], qr, ALU.mult))
            link(tt(rot(rot1, 1), b_s[:, :, :], qi, ALU.mult))
            link(tt(rot(rot2, 0), b_s[:, :, :], qr, ALU.mult))
            link(tt(rot(rot2, 1), b_n[:, :, :], qi, ALU.mult))
            link(tt(b_n[:, :, :], rot(rot1, 0), rot(rot1, 1), ALU.subtract))
            link(tt(b_s[:, :, :], rot(rot2, 0), rot(rot2, 1), ALU.add))

            def cmul(o_r, o_i, x_r, x_i, y_r, y_i, n):
                y_r, y_i = (y.unsqueeze(2).broadcast_to([P, G, n]) for y in (y_r, y_i))
                s1, s2 = rot1[:, :, 0:n], rot2[:, :, 0:n]
                link(tt(s1, x_r, y_r, ALU.mult))
                link(tt(s2, x_i, y_i, ALU.mult))
                link(tt(o_r, s1, s2, ALU.subtract))
                link(tt(s1, x_r, y_i, ALU.mult))
                link(tt(s2, x_i, y_r, ALU.mult))
                link(tt(o_i, s1, s2, ALU.add))

            for lo, n, e in ((1, 1, 1), (1, 2, 2), (1, 4, 4)):
                cmul(pw_r[:, :, lo + e:lo + e + n], pw_i[:, :, lo + e:lo + e + n],
                     pw_r[:, :, lo:lo + n], pw_i[:, :, lo:lo + n], pw_r[:, :, e], pw_i[:, :, e], n)
            link(ts(pw_rs[:, :, :], pw_r[:, :, :], sign[:, 0:1], None, ALU.mult))
            ts(pw_is[:, :, :], pw_i[:, :, :], sign[:, 0:1], -1.0, ALU.mult, ALU.mult).then_inc(s5_par, 1)
            dve.wait_ge(s5_rstd, 1)
            for s in range(CH):
                stt(u[:, :, s, :], xp[:, s, :].rearrange("p (g h) -> p g h", h=GH), rstd[0:NC, s:s + 1],
                    g_row[:, :].rearrange("p (g h) -> p g h", h=GH), ALU.mult, ALU.mult).then_inc(s5_u, 1)
            turn = [(pt(14), pt(12)), (pt(18), pt(19))]
            for k in range(3 + 6):
                (c0, s0), (c1, s1) = turn[k % 2], turn[(k + 1) % 2]
                if k >= 3:
                    n = 1 << (k - 3)
                    if k == 3:
                        link(dve.memset(tab_c[:, :, 0:1], 1.0))
                        link(dve.memset(tab_s[:, :, 0:1], 0.0))
                    cmul(tab_c[:, :, n:2 * n], tab_s[:, :, n:2 * n], tab_c[:, :, 0:n], tab_s[:, :, 0:n], c0, s0, n)
                link(tt(pt(20), c0, c0, ALU.mult))
                link(tt(pt(21), s0, s0, ALU.mult))
                link(tt(c1, pt(20), pt(21), ALU.subtract))
                link(tt(pt(20), c0, s0, ALU.mult))
                link(ts(s1, pt(20), 2.0, None, ALU.mult))

            def ysum(b):
                dve.wait_ge(s5_y, b + 1)
                dve.wait_ge(s5_du, b + 1)
                flat = du[:, :, :, :].rearrange("p g t h -> p (g t h)")
                tt(flat, PS[0:NC, 6:8, :].rearrange("p b n -> p (b n)"), flat, ALU.add).then_inc(s5_ysum, 1)

            dve.wait_ge(s5_ut_sb, 8)
            for b in range(NB):
                gs = slice(GB * b, GB * b + GB)

                def over_k(ap, n):
                    return ap[:, gs, :].unsqueeze(2).broadcast_to([P, GB, n, GH])

                def over_h(ap, n):
                    return ap[:, gs, 0:n].unsqueeze(3).broadcast_to([P, GB, n, GH])

                if b >= 1:
                    dve.wait_ge(s5_y, b)
                link(tt(out_a[:, :, :, :], over_k(c_n, CH + 1), over_h(pw_rs, CH + 1), ALU.mult))
                link(tt(tmp_a[:, :, :, :], over_k(c_s, CH + 1), over_h(pw_i, CH + 1), ALU.mult))
                tt(out_a[:, :, :, :], out_a[:, :, :, :], tmp_a[:, :, :, :], ALU.subtract).then_inc(s5_outa, 1)
                if b >= 1:
                    dve.wait_ge(s5_int, b)
                back = [t[:, gs, 0:CH][:, :, ::-1] for t in (pw_r, pw_is)]
                back = [t.unsqueeze(3).broadcast_to([P, GB, CH, GH]) for t in back]
                dve.wait_ge(s5_outa, b + 1)
                link(tt(in_w[:, :, :, :], over_k(b_n, CH), back[0], ALU.mult))
                link(tt(tmp_a[:, :, 0:CH, :], over_k(b_s, CH), back[1], ALU.mult))
                tt(in_w[:, :, :, :], in_w[:, :, :, :], tmp_a[:, :, 0:CH, :], ALU.add).then_inc(s5_inw, 1)
                if b >= 1:
                    ysum(b - 1)
                dve.wait_ge(s5_v, b + 1)
                ps_v = PS[:, 4, :].rearrange("p (g c) -> p g c", c=NC)
                ps_s = PS[:, 5, :].rearrange("p (g c) -> p g c", c=NC)
                link(tt(v1[:, :, :], ps_v, tab_c[:, gs, :], ALU.mult))
                tt(v2[:, :, :], ps_s, tab_s[:, gs, :], ALU.mult).then_inc(s5_rot, 1)
                dve.wait_ge(s5_rot, b + 1)
                link(tt(v1[:, :, :], v1[:, :, :], v2[:, :, :], ALU.add))
                dve.wait_ge(s5_dec, b + 1)
                link(dve.tensor_tensor_scan(z[:, :, :].rearrange("p g c -> p (g c)"),
                                            decay[:, :, :].rearrange("p g c -> p (g c)"),
                                            v1[:, :, :].rearrange("p g c -> p (g c)"), 0.0, ALU.mult, ALU.add))
                if b == 0:
                    link(dve.memset(cz[:, :, 0:1], 0.0))
                    link(dve.memset(sz[:, :, 0:1], 0.0))
                if b >= 1:
                    dve.wait_ge(s5_y, b)
                link(tt(cz[:, :, 1:NC], z[:, :, 0:NC - 1], tab_c[:, gs, 0:NC - 1], ALU.mult))
                tt(sz[:, :, 1:NC], z[:, :, 0:NC - 1], tab_s[:, gs, 0:NC - 1], ALU.mult).then_inc(s5_cz, 1)
            ysum(NB - 1)

            def turn_lo(j0, n, gain=None, width=S, hi=xT_hi, lo=xT_lo, view=None):
                for k in range(n):
                    dve.wait_ge(x_hi_done, j0 + k + 1)
                    o, h, i = lo[:, k, 0:width], f32(hi[:, k, 0:width]), PS[:, k % 4, 0:width]
                    if view:
                        (o, i), (h, i) = view(o, i), view(h, i)
                        tt(o, i, h, ALU.subtract).then_inc(x_lo_done, 1)
                    else:
                        s = 1.0 if gain is None else gains[:, gain * KT + k:gain * KT + k + 1]
                        stt(o, i, s, h, ALU.mult, ALU.subtract).then_inc(x_lo_done, 1)

            turn_lo(0, KT, view=chunk_view)
            dve.wait_ge(ld_res, 16)
            for e in range(4 * TB):
                j, tb = divmod(e, TB)
                dve.wait_ge(glu_sig, e + 1)
                tt(glu_v[:, e % 2, :], PS[:, 4 + tb, 0:256], glu_sg[:, e % 2, :], ALU.mult).then_inc(n_free, 1)
                dve.wait_ge(n_free, TB + e + 1)
                xs = x_res[:, tb, 256 * j:256 * j + 256]
                tt(xs, xs, glu_v[:, e % 2, :], ALU.add).then_inc(glu_done, 1)

            def norm_x(n, sem_x, value):
                dve.wait_ge(sem_x, value)
                dve.wait_ge(row_rstd, n + 1)
                for tb in range(TB):
                    ts(xn[:, tb, :], x_res[:, tb, :], rstd[:, tb:tb + 1], None, ALU.mult).then_inc(row_norm, 1)

            dve.wait_ge(gains_sb, 1)
            norm_x(0, glu_done, 4 * TB)
            turn_lo(KT, KT, gain=2)

            def add_panel(ni, g_done, cols, extra=0):
                for tb in range(TB):
                    if tb < TB - 1:
                        dve.wait_ge(n_ready, ni * 3 + (tb + 1 + extra))
                    else:
                        dve.wait_ge(w_used, g_done)
                    tt(x_res[:, tb, cols], x_res[:, tb, cols], PS[:, 4 + tb, :], ALU.add).then_inc(n_free, 1)

            def ffn_dve(layer):
                t0, h0 = FFN_TILE[layer], FFN_HID[layer]
                g0 = FFN_SLOT[layer]
                with dve.Fori(0, FT // 2) as i:
                    for j in range(2):
                        pair = (t0 + j) % 2
                        dve.wait_ge(w_used, i * 2 + (g0 + j + 1))
                        dve.wait_ge(hid_act, i * 2 + (h0 + j + 1))
                        tt(gbuf[:, pair, 1, :], gbuf[:, pair, 0, :], PS[:, 2 * pair + 1, :], ALU.mult).then_inc(t_free, 1)
                        dve.wait_ge(t_free, i * 2 + (t0 + j + 3))
                        dve.tensor_copy(hT_hi[:, bass.ds(i * 2 + j, 1), :], gbuf[:, pair, 1:2, :]).then_inc(hid_hi, 1)
                        dve.wait_ge(hid_hi, i * 2 + (h0 + j + 1))
                        tt(hT_lo[:, bass.ds(i * 2 + j, 1), :], gbuf[:, pair, 1:2, :], f32(hT_hi[:, bass.ds(i * 2 + j, 1), :]),
                           ALU.subtract).then_inc(hid_done, 1)
                m = len(FFN_DOWN)
                with dve.Fori(0, 2) as i:
                    add_panel(i + FFN_PANEL[layer], i * m + (g0 + FT + m), bass.ds(i * 512, 512))

            ffn_dve(0)
            dve.wait_ge(ld_qk, 16 * 4)
            for j, (dst, scale) in enumerate(((rope_q, HD ** -0.5), (rope_k, 1.0))):
                g = gain_qk[:, j, :].unsqueeze(1).broadcast_to([P, TB, HD])
                link(tt(dst[:, 0, :, :], rope[:, 0, :, :], g, ALU.mult))
                for half in range(2):
                    to, of = slice(32 * half, 32 * half + 32), slice(32 - 32 * half, 64 - 32 * half)
                    g = gain_qk[:, j, of].unsqueeze(1).broadcast_to([P, TB, 32])
                    link(tt(dst[:, 1, :, to], rope[:, 1, :, to], g, ALU.mult))
                if scale != 1.0:
                    link(ts(dst[:, :, :, :], dst[:, :, :, :], scale, None, ALU.mult))
            ts(sinks_neg[:, :], sinks[:, :], -1.0, None, ALU.mult).then_inc(qk_tables, 1)
            norm_x(1, n_free, TB * (FFN_PANEL[0] + 3))
            turn_lo(2 * KT, KT, gain=1)

            def swap_halves(ap):
                return ap.rearrange("p (h t d) -> p h t d", t=2, d=HD // 2)[:, :, ::-1, :]

            def head_rotate(e, table, tb):
                pi = e // TB
                dve.wait_ge(head_norm, e + 1)
                sin = table[:, 1, tb, :].rearrange("p (t d) -> p t d", t=2).unsqueeze(1).broadcast_to([P, 8, 2, HD // 2])
                if e >= 1:
                    dve.wait_ge(head_done, e)
                link(tt(head_s[:, :].rearrange("p (h t d) -> p h t d", t=2, d=HD // 2),
                        swap_halves(head_n[:, e % 2, :]), sin, ALU.mult))
                dve.wait_ge(head_cos, e + 1)
                if pi >= 2:
                    dve.wait_ge(head_t, 4 * (pi - 1))
                tt(stage[:, pi % 2, tb, :], head_c[:, e % 2, :], head_s[:, :], ALU.add).then_inc(head_done, 1)

            for tb in range(TB):
                head_rotate(tb, rope, tb)
                if tb == TB - 1:
                    dve.memset(above[:, :], 0.0).then_inc(n_free, TB)
            dve.wait_ge(ki_squared, 1)
            dve.tensor_reduce(head_ss[:, 0, 0:TB], ki_c[:, :, :], AX.X, ALU.add).then_inc(ki_sq, 1)
            dve.wait_ge(ki_rs, 1)
            link(tt(ki_n[:, :, :], PS[:, 4:8, 0:HD], head_rs[:, 0, 0:TB].unsqueeze(2).broadcast_to([P, TB, HD]), ALU.mult))
            ts(w_idx[:, :, :], PS[:, 4:8, HD:HD + NI], NI ** -0.5, None, ALU.mult).then_inc(n_free, TB)
            for half in range(2):
                to, of = slice(32 * half, 32 * half + 32), slice(32 - 32 * half, 64 - 32 * half)
                link(tt(ki_c[:, :, to], ki_n[:, :, of], rope[:, 1, :, to], ALU.mult))
            link(tt(ki_n[:, :, :], ki_n[:, :, :], rope[:, 0, :, :], ALU.mult))
            for twice in range(2):
                tt(ki_st[:, :, twice, :], ki_n[:, :, :], ki_c[:, :, :], ALU.add).then_inc(ki_done, 1)

            def index_scores():
                for e in range(3 * NI):
                    b, h = e // NI + 1, e % NI
                    n = P * (b + 1)
                    sc = score[:, BLK[b]:BLK[b] + n]
                    dve.wait_ge(idx_relu, e + 1)
                    if h == 0:
                        if e:
                            dve.wait_ge(idx_sum, e)
                        ts(sc, relu_i[:, e % 2, 0:n], w_idx[:, b, h:h + 1], None, ALU.mult).then_inc(idx_sum, 1)
                    else:
                        dve.wait_ge(idx_sum, e)
                        stt(sc, relu_i[:, e % 2, 0:n], w_idx[:, b, h:h + 1], sc, ALU.mult, ALU.add).then_inc(idx_sum, 1)

            def choose(b):
                n = P * (b + 1)
                cols = slice(BLK[b], BLK[b] + n)
                sc, rk = score[:, cols], ranked[:, cols]
                link(tt(sc[:, n - P:n], sc[:, n - P:n], masks[:, 0, :], ALU.add))
                for r in range(TOPK // 8):
                    link(dve.max(top[:, :], sc if r == 0 else rk))
                    if r < TOPK // 8 - 1:
                        link(dve.match_replace(rk, top[:, :], sc if r == 0 else rk, 3 * NEG))
                least = top[:, 7:8]
                link(ts(rk, sc, least, None, ALU.is_gt))
                link(dve.tensor_reduce(above[:, :], rk, AX.X, ALU.add))
                link(ts(equal[:, 0:n], sc, least, None, ALU.is_equal))
                link(dve.tensor_tensor_scan(seen[:, 0:n], one[:, 0:1].broadcast_to([P, n]), equal[:, 0:n], 0.0, ALU.mult, ALU.add))
                link(ts(seen[:, 0:n], seen[:, 0:n], above[:, 0:1], float(TOPK), ALU.add, ALU.is_le))
                link(tt(seen[:, 0:n], seen[:, 0:n], equal[:, 0:n], ALU.mult))
                link(tt(rk, rk, seen[:, 0:n], ALU.add))
                ts(chosen[:, cols], rk, -1.0, -NEG, ALU.add, ALU.mult).then_inc(idx_chosen, 1)

            for j in range(4):
                for tb in range(TB):
                    n, e = TB * j + tb, TB * (1 + j) + tb
                    dve.wait_ge(head_sq_done, n + 1)
                    dve.tensor_reduce(head_ss[:, e % 2, :], head_sq[:, n % 2, :].rearrange("p (h d) -> p h d", d=HD),
                                      AX.X, ALU.add).then_inc(head_sum, 1)
                    dve.wait_ge(head_rstd, n + 1)
                    if e >= 2:
                        dve.wait_ge(head_cos, e - 1)
                    tt(head_n[:, e % 2, :].rearrange("p (h d) -> p h d", d=HD),
                       PS[:, 4 + tb, :].rearrange("p (h d) -> p h d", d=HD),
                       head_rs[:, e % 2, :].unsqueeze(2).broadcast_to([P, 8, HD]), ALU.mult).then_inc(head_norm, 1)
                    head_rotate(e, rope_q if j < 2 else rope_k, tb)
                dve.memset(above[:, :], 0.0).then_inc(n_free, TB)
                if j == 0:
                    index_scores()
            for b in range(1, TB):
                choose(b)

            def attend_dve(units, u0, stick=False):
                n = len(units)
                for t in range(n + 3):
                    if t < n:
                        cols, add, sink = units[t][1].shape[1], units[t][2], units[t][5]
                        lg, s, m = logit[:, t % 3, 0:cols], PS[:, t % 3, 0:cols], neg_max[:, t % 4:t % 4 + 1]
                        dve.wait_ge(at_dot, u0 + t + 1)
                        if t >= 3:
                            dve.wait_ge(at_turn, u0 + t - 2)
                        if stick:
                            dve.wait_ge(at_ln, t + 1)
                            sp = soft[t % 2][:, 0:cols]
                            link(stt(sp, s, 0.0, sp, ALU.max, ALU.add))
                            link(tt(sp[:, cols - P:cols], sp[:, cols - P:cols], masks[:, 2, :], ALU.mult))
                            link(dve.tensor_tensor_scan(lg[:, ::-1], one[:, 0:1].broadcast_to([P, cols]), sp[:, ::-1], 0.0,
                                                        ALU.mult, ALU.add))
                            tt(lg, s, lg, ALU.subtract).then_inc(at_logit, 1)
                            dve.wait_ge(at_logit, u0 + t + 1)
                            tt(lg[:, cols - P:cols], lg[:, cols - P:cols], masks[:, 1, :], ALU.add).then_inc(at_max, 1)
                        else:
                            if add is None:
                                dve.tensor_copy(lg, s).then_inc(at_logit, 1)
                            else:
                                tt(lg, s, add, ALU.add).then_inc(at_logit, 1)
                            dve.wait_ge(at_logit, u0 + t + 1)
                            ins = dve.tensor_reduce(m, lg, AX.X, ALU.max, negate=True)
                            if sink is not None:
                                link(ins)
                                ins = tt(m, m, sinks_neg[:, sink:sink + 1], ALU.min)
                            ins.then_inc(at_max, 1)
                    e = t - 3
                    if e >= 0:
                        o, sink = units[e][4], units[e][5]
                        c = slice(e % 4, e % 4 + 1)
                        dve.wait_ge(at_pv, u0 + e + 1)
                        if stick:
                            dve.tensor_copy(o, PS[:, 5 + e % 2, 0:HD]).then_inc(at_out, 1)
                            continue
                        if sink is not None:
                            link(tt(row_sum[:, c], row_sum[:, c], sink_e[:, c], ALU.add))
                        link(dve.reciprocal(inv_sum[:, c], row_sum[:, c]))
                        ts(o, PS[:, 5 + e % 2, 0:HD], inv_sum[:, c], None, ALU.mult).then_inc(at_out, 1)

            attend_dve(dsa_units, DSA_UNIT)
            turn_lo(3 * KT, KT)
            for j in range(2):
                add_panel(WO_PANEL + j, WO_SLOT + 2 * j + 2, slice(512 * j, 512 * j + 512))
            norm_x(2, n_free, TB * (WO_PANEL + 3))
            turn_lo(4 * KT, KT, gain=3)
            ffn_dve(1)

            norm_x(3, n_free, TB * (FFN_PANEL[1] + 3))
            turn_lo(5 * KT, KT, gain=4)
            dve.wait_ge(ld_bias_t, 16)
            attend_dve(soft_units, SOFT_UNIT)
            attend_dve(stick_units, STICK_UNIT, stick=True)
            dve.wait_ge(grp_rstd, 1)
            for tb in range(TB):
                y4 = o_nat[:, tb, :].rearrange("p (g n) -> p g n", g=4)
                tt(y4, y4, rstd[:, 16 + 4 * tb:20 + 4 * tb].unsqueeze(2).broadcast_to([P, 4, 256]), ALU.mult).then_inc(grp_norm, 1)
            turn_lo(6 * KT, KT, gain=8)
            dve.wait_ge(mem_rstd, 1)
            for m in range(2):
                ts(mem[:, m, :], mem[:, m, :], rstd[:, 32 + m:33 + m], None, ALU.mult).then_inc(mem_norm, 1)
            for j in range(2):
                add_panel(HOUT_PANEL + j, HOUT_SLOT + 2 * j + 2, slice(512 * j, 512 * j + 512))

            turn_lo(7 * KT, KT, gain=6, width=MEM, hi=memT_hi, lo=memT_lo)
            norm_x(4, n_free, TB * (HOUT_PANEL + 3))
            turn_lo(8 * KT, KT, gain=5)
            attend_dve(mem_units, MEM_UNIT)
            turn_lo(9 * KT, 2)
            for j in range(2):
                for tb in range(TB):
                    if j == 1 and tb == TB - 1:
                        dve.wait_ge(w_used, XO_SLOT + 1)
                    else:
                        dve.wait_ge(n_ready, 3 * XO_PANEL + TB * j + tb + 1)
                    xs = x_res[:, tb, 512 * j:512 * j + 512]
                    tt(xs, xs, PS[:, 4 + tb, :], ALU.add).then_inc(n_free, 1)

            norm_x(5, n_free, TB * (XO_PANEL + 3))
            turn_lo(9 * KT + 2, KT, gain=7)
            for part in range(MLP_PARTS):
                g0, t0, h0 = MLP_SLOT[part], MLP_TILE[part], MLP_HID[part]
                with dve.Fori(0, MT // 4) as i:
                    for j in range(2):
                        pair = (t0 + j) % 2
                        gb = gbuf[:, pair, :, :]
                        hi = hT_hi[:, bass.ds(i * 4 + 2 * j, 2), :]
                        dve.wait_ge(t_free, i * 2 + (t0 + j + 3))
                        tt(gb, gb, gb, ALU.mult).then_inc(hid_act, 1)
                        dve.wait_ge(hid_act, i * 2 + (h0 + j + 1))
                        dve.tensor_copy(hi, gb).then_inc(hid_hi, 1)
                        dve.wait_ge(hid_hi, i * 2 + (h0 + j + 1))
                        tt(hT_lo[:, bass.ds(i * 4 + 2 * j, 2), :], gb, f32(hi), ALU.subtract).then_inc(hid_done, 1)
                m = MT // 4
                with dve.Fori(0, 2) as i:
                    add_panel(i + MLP_PANEL[part], i * m + (g0 + MT // 2 + m), bass.ds(i * 512, 512), 1)
            dve.wait_ge(row_rstd, 7)
            dve.wait_ge(ld_last, 16)
            for tb in range(TB):
                stt(xn[:, tb, :], x_res[:, tb, :], rstd[:, tb:tb + 1], g_last[:, :], ALU.mult, ALU.mult).then_inc(x_final, 1)

        @block.tensor
        def _(pe):
            mm, tr = pe.matmul, pe.transpose
            id64 = ident[0:64, 0:64]
            pe.wait_ge(ld_const, 16 * 10)
            pe.wait_ge(ld_par, 16 * 13)
            for j in range(2):
                ins = tr(PS[:, 0, G * j:G * j + G], nat_l[:, j, :, :].rearrange("g a p -> g (a p)"), id64)
            ins.then_inc(s5_nat, 1)
            for order, bank in ((0, 1), (1, 3)):
                for h in range(GH):
                    ins = tr(PS[:, bank + h // 8, G * (h % 8):G * (h % 8) + G],
                             nat_b[:, order:order + 2, :, h].rearrange("g a p -> g (a p)"), id64)
                ins.then_inc(s5_nat, 1)
            for b in range(NB):
                ins = tr(PS[:, 5 + b // 4, P * (b % 4):P * (b % 4) + P], nat_c[:, b, 0:2, :].rearrange("g a p -> g (a p)"), ident[:, :])
            ins.then_inc(s5_nat, 1)
            for b in range(NB // 2):
                ins = tr(PS[:, 7, P * b:P * b + P], nat_c[:, b, 1:3, :].rearrange("g a p -> g (a p)"), ident[:, :])
            ins.then_inc(s5_nat, 1)
            pe.wait_ge(s5_nat_sb, 2)
            for b in range(NB // 2):
                ins = tr(PS[:, 1, P * b:P * b + P], nat_c[:, NB // 2 + b, 1:3, :].rearrange("g a p -> g (a p)"), ident[:, :])
            ins.then_inc(s5_nat, 1)
            tr(PS[:, 0, 0:len(GAINS) * KT], gain_rows[:, :], ident[0:len(GAINS) * KT, 0:len(GAINS) * KT]).then_inc(gains_t, 1)
            pe.wait_ge(s5_u, CH)
            pe.wait_ge(s5_nat_sb, 6)
            pe.wait_ge(gains_sb, 1)
            for q in range(8):
                for g in range(GB):
                    ins = tr(PS[:, q, NC * g:NC * g + NC], u[:, GB * q + g, :, :].rearrange("p t h -> p (t h)"), id64)
                ins.then_inc(s5_ut, 1)
            pe.wait_ge(s5_ut_sb, 8)

            def s5_out(b):
                pe.wait_ge(s5_cz, b + 1)
                pe.wait_ge(s5_outb, b + 1)
                pe.wait_ge(s5_taps, 16 * CH * (b + 1))
                if b >= 1:
                    pe.wait_ge(s5_ysum, b)
                for g in range(GB):
                    o = PS[0:NC, 6 + g // 4, P * (g % 4):P * (g % 4) + P]
                    mm(o, uT[:, GB * b + g, :], taps[:, g, :, :].rearrange("p t h -> p (t h)"), start=True, stop=False)
                    mm(o, cz[:, g, :], out_a[:, g, 1:CH + 1, :].rearrange("p t h -> p (t h)"), start=False, stop=False)
                    ins = mm(o, sz[:, g, :], out_b[:, g, :, :].rearrange("p t h -> p (t h)"), start=False, stop=True)
                ins.then_inc(s5_y, 1)

            for b in range(NB):
                pe.wait_ge(s5_outa, b + 1)
                if b >= 1:
                    pe.wait_ge(s5_lag_sb, b)
                for g in range(GB):
                    ins = mm(PS[0:GH, g // 4, P * (g % 4):P * (g % 4) + P], b_n[:, GB * b + g, :],
                             out_a[:, g, 0:CH, :].rearrange("p t h -> p (t h)"), start=True, stop=True)
                ins.then_inc(s5_lag, 1)
                pe.wait_ge(s5_inw, b + 1)
                if b >= 1:
                    pe.wait_ge(s5_int_sb, b)
                for g in range(GB):
                    ins = tr(PS[:, 2 + g // 4, P * (g % 4):P * (g % 4) + P], in_w[:, g, :, :].rearrange("p s h -> p (s h)"), ident[:, :])
                ins.then_inc(s5_int, 1)
                pe.wait_ge(s5_int_sb, b + 1)
                if b >= 1:
                    pe.wait_ge(s5_rot, b)
                for g in range(GB):
                    mm(PS[:, 4, NC * g:NC * g + NC], in_t[:, g, :, :].rearrange("p r q -> p (r q)"), uT[:, GB * b + g, :], start=True, stop=True)
                    ins = mm(PS[:, 5, NC * g:NC * g + NC], in_s[:, g, :, :].rearrange("p r q -> p (r q)"), uT[:, GB * b + g, :], start=True, stop=True)
                ins.then_inc(s5_v, 1)
                s5_out(b)
            for b in range(NB):
                pe.wait_ge(s5_gelu, b + 1)
                if b >= 4:
                    pe.wait_ge(x_lo_done, b - 3)
                for s in range(CH):
                    ins = tr(PS[:, b % 4, NC * s:NC * s + NC], y[:, b, s, :], id64)
                ins.then_inc(turned, 1)

            def three(o, wgt_hi, wgt_lo, x_hi, x_lo, weights_stay, first, last):
                for n, (a, c) in enumerate(((wgt_hi, x_hi), (wgt_lo, x_hi), (wgt_hi, x_lo))):
                    ins = mm(o, a if weights_stay else c, c if weights_stay else a,
                             start=first and n == 0, stop=last and n == 2)
                return ins

            def n_slot(g, par, ni, ks, hi, lo, first, last, n=512, tbs=TB, inc=1):
                pe.wait_ge(w_split, g + 1)
                for tb in range(tbs):
                    if first:
                        pe.wait_ge(n_free, ni * TB + (tb + 1))
                    for j, k in enumerate(ks):
                        cols = slice(n * j, n * j + n)
                        ins = three(PS[:, 4 + tb, 0:n], w_hi[:, par, cols], w_lo[:, par, cols],
                                    hi[:, k, P * tb:P * tb + P], lo[:, k, P * tb:P * tb + P], False,
                                    first and j == 0, last and j == len(ks) - 1)
                    if tb == tbs - 1:
                        ins.then_inc(w_used, 1)
                    elif last:
                        ins.then_inc(n_ready, inc)

            def t_slot(g, par, ti, pair, hi, lo, width=S, step=(2 * P, P)):
                pe.wait_ge(w_split, g + 1)
                pe.wait_ge(t_free, ti + 1)
                for t in range(2):
                    for k in range(KT):
                        at = step[0] * k + step[1] * t
                        cols = slice(at, at + P)
                        ins = three(PS[:, 2 * pair + t, 0:width], w_hi[:, par, cols], w_lo[:, par, cols],
                                    hi[:, k, 0:width], lo[:, k, 0:width], True, k == 0, k == KT - 1)
                    ins.then_inc(w_used if t else t_first, 1)

            def turn_rows(j0, n, src, tbs=TB):
                for k in range(n):
                    if k >= 4:
                        pe.wait_ge(x_lo_done, j0 + k - 3)
                    for tb in range(tbs):
                        ins = tr(PS[:, k % 4, P * tb:P * tb + P], src[:, tb, P * k:P * k + P], ident[:, :])
                    ins.then_inc(turned, 1)

            pe.wait_ge(x_lo_done, KT)
            for j in range(4):
                for k in range(2):
                    g = GLU_SLOT + 2 * j + k
                    n_slot(g, g % 2, GLU_PANEL + j, range(4 * k, 4 * k + 4), xT_hi, xT_lo, k == 0, k == 1)
            pe.wait_ge(row_norm, TB)
            turn_rows(KT, KT, xn)

            def ffn_pe(layer, turns):
                g0, t0, h0 = FFN_SLOT[layer], FFN_TILE[layer], FFN_HID[layer]
                pe.wait_ge(x_lo_done, turns)
                with pe.Fori(0, FT // 2) as i:
                    for j in range(2):
                        t_slot(i * 2 + (g0 + j), (g0 + j) % 2, i * 2 + (t0 + j), (t0 + j) % 2, xT_hi, xT_lo)
                g0 += FT
                m = len(FFN_DOWN)
                with pe.Fori(0, 2) as i:
                    k = 0
                    for j, n in enumerate(FFN_DOWN):
                        pe.wait_ge(hid_done, h0 + k + n + 2)
                        n_slot(i * m + (g0 + j), (g0 + j) % 2, i + FFN_PANEL[layer], range(k, k + n), hT_hi, hT_lo,
                               j == 0, j == m - 1)
                        k += n

            ffn_pe(0, 2 * KT)
            pe.wait_ge(row_norm, 2 * TB)
            turn_rows(2 * KT, KT, xn)
            pe.wait_ge(x_lo_done, 3 * KT)

            def panel(g0, ni, n=512):
                for k in range(2):
                    n_slot(g0 + k, (g0 + k) % 2, ni, range(4 * k, 4 * k + 4), xT_hi, xT_lo, k == 0, k == 1, n)

            def turn_heads(pi):
                pe.wait_ge(head_done, TB * (pi + 1))
                for j in range(4):
                    if pi >= 1:
                        pe.wait_ge(head_t_sb, 4 * (pi - 1) + j + 1)
                    for tb in range(TB):
                        ins = tr(PS[:, j, P * tb:P * tb + P], stage[:, pi % 2, tb, P * j:P * j + P], ident[:, :])
                    ins.then_inc(head_t, 1)

            g = DSA_SLOT
            panel(g, DSA_PANEL)
            n_slot(g + 2, (g + 2) % 2, DSA_PANEL + 1, range(KT), xT_hi, xT_lo, True, True, DSA_W - 3 * D - 512)
            panel(g + 3, DSA_PANEL + 2)
            turn_heads(0)
            pe.wait_ge(ki_done, 2)
            pe.wait_ge(head_t_sb, 1)
            for tb in range(TB):
                ins = tr(PS[:, 0, P * tb:P * tb + P], ki_st[:, tb, :, :].rearrange("p a d -> p (a d)"), ident[:, :])
            ins.then_inc(ki_t, 1)
            pe.wait_ge(head_t_sb, 4)
            pe.wait_ge(ki_t_sb, 1)
            for e in range(3 * NI):
                b, h = e // NI + 1, e % NI
                if e >= 4:
                    pe.wait_ge(idx_relu, e - 3)
                rows = slice(HD * (h % 2), HD * (h % 2) + HD)
                mm(PS[:, e % 4, 0:P * (b + 1)], qiT[rows, h // 2, P * b:P * b + P], kiT[rows, 0:P * (b + 1)],
                   start=True, stop=True).then_inc(idx_dot, 1)
            for j in range(1, 6):
                panel(g + 3 + 2 * j, DSA_PANEL + 2 + j)
                if j == 1:
                    pe.wait_ge(idx_relu, 3 * NI)
                if j < 5:
                    turn_heads(j)

            def attend_pe(units, u0):
                n = len(units)
                for t in range(n + 3):
                    if t < n:
                        q, k = units[t][0], units[t][1]
                        if t >= 3:
                            pe.wait_ge(at_logit, u0 + t - 2)
                        mm(PS[:, t % 3, 0:k.shape[1]], q, k, start=True, stop=True).then_inc(at_dot, 1)
                    e = t - 2
                    if 0 <= e < n:
                        pe.wait_ge(at_prob, u0 + e + 1)
                        if e >= 2:
                            pe.wait_ge(at_turn_sb, u0 + e - 1)
                        for j in range(len(units[e][3])):
                            ins = tr(PS[:, 3 + e % 2, P * j:P * j + P], logit[:, e % 3, P * j:P * j + P], ident[:, :])
                        ins.then_inc(at_turn, 1)
                    e = t - 3
                    if e >= 0:
                        v = units[e][3]
                        pe.wait_ge(at_turn_sb, u0 + e + 1)
                        if e >= 2:
                            pe.wait_ge(at_out, u0 + e - 1)
                        for j in range(len(v)):
                            ins = mm(PS[:, 5 + e % 2, 0:HD], probT[:, e % 2, P * j:P * j + P], v[j],
                                     start=j == 0, stop=j == len(v) - 1)
                        ins.then_inc(at_pv, 1)

            pe.wait_ge(head_t_sb, 20)
            pe.wait_ge(n_free, TB * (DSA_PANEL + 9))
            pe.wait_ge(idx_chosen, 3)
            attend_pe(dsa_units, DSA_UNIT)
            pe.wait_ge(at_out, SOFT_UNIT)
            turn_rows(3 * KT, KT, o_nat)
            pe.wait_ge(x_lo_done, 4 * KT)
            for j in range(2):
                panel(WO_SLOT + 2 * j, WO_PANEL + j)
            pe.wait_ge(row_norm, 3 * TB)
            turn_rows(4 * KT, KT, xn)
            ffn_pe(1, 5 * KT)

            pe.wait_ge(ld_bias, 48)
            pe.wait_ge(n_free, TB * (FFN_PANEL[1] + 3))
            mm(PS[0:NREL, 4, :], table[:, :], basis[:, 0:512], start=True, stop=True)
            mm(PS[0:NREL, 5, 0:BIAS_W - 512], table[:, :], basis[:, 512:BIAS_W], start=True, stop=True).then_inc(bias_row, 1)
            pe.wait_ge(row_norm, 4 * TB)
            turn_rows(5 * KT, KT, xn)
            pe.wait_ge(x_lo_done, 6 * KT)
            for j in range(8):
                g = HIN_SLOT + j
                t_slot(g, g % 2, HIN_TILE + j, (HIN_TILE + j) % 2, xT_hi, xT_lo, step=(192, 64) if j == 5 else (256, P))
            pe.wait_ge(bias_row_sb, 1)
            panel(HIN_SLOT + 8, HIN_PANEL)
            panel(HIN_SLOT + 10, HIN_PANEL + 1, 384)
            pe.wait_ge(t_free, HIN_TILE + 10)
            pe.wait_ge(n_free, TB * (HIN_PANEL + 3))
            attend_pe(soft_units, SOFT_UNIT)
            attend_pe(stick_units, STICK_UNIT)
            pe.wait_ge(grp_norm, TB)
            turn_rows(6 * KT, KT, o_nat)
            pe.wait_ge(x_lo_done, 7 * KT)
            for j in range(2):
                panel(HOUT_SLOT + 2 * j, HOUT_PANEL + j)

            pe.wait_ge(mem_norm, 2)
            turn_rows(7 * KT, KT, mem, 2)
            pe.wait_ge(x_lo_done, 8 * KT)
            t_slot(MEM_SLOT, MEM_SLOT % 2, MEM_TILE, MEM_TILE % 2, memT_hi, memT_lo, MEM)
            n_slot(MEM_SLOT + 1, (MEM_SLOT + 1) % 2, MEM_PANEL, range(KT), memT_hi, memT_lo, True, True, 256, 2, 3)
            pe.wait_ge(t_free, MEM_TILE + 3)
            pe.wait_ge(row_norm, 5 * TB)
            turn_rows(8 * KT, KT, xn)
            pe.wait_ge(x_lo_done, 9 * KT)
            t_slot(XQ_SLOT, XQ_SLOT % 2, XQ_TILE, XQ_TILE % 2, xT_hi, xT_lo)
            pe.wait_ge(t_free, XQ_TILE + 3)
            pe.wait_ge(n_free, TB * (MEM_PANEL + 2))
            attend_pe(mem_units, MEM_UNIT)
            pe.wait_ge(at_out, MEM_UNIT + 16)
            turn_rows(9 * KT, 2, ox)
            pe.wait_ge(x_lo_done, 9 * KT + 2)
            par = XO_SLOT % 2
            pe.wait_ge(w_split, XO_SLOT + 1)
            for j in range(2):
                for tb in range(TB):
                    pe.wait_ge(n_free, TB * (XO_PANEL + j) + tb + 1)
                    for k in range(2):
                        cols = slice(D * k + 512 * j, D * k + 512 * j + 512)
                        ins = three(PS[:, 4 + tb, :], w_hi[:, par, cols], w_lo[:, par, cols],
                                    xT_hi[:, k, P * tb:P * tb + P], xT_lo[:, k, P * tb:P * tb + P], False, k == 0, k == 1)
                    ins.then_inc(w_used if j == 1 and tb == TB - 1 else n_ready, 1)

            pe.wait_ge(row_norm, 6 * TB)
            turn_rows(9 * KT + 2, KT, xn)
            pe.wait_ge(x_lo_done, 10 * KT + 2)
            for part in range(MLP_PARTS):
                g0, t0, h0 = MLP_SLOT[part], MLP_TILE[part], MLP_HID[part]
                with pe.Fori(0, MT // 4) as i:
                    for j in range(2):
                        t_slot(i * 2 + (g0 + j), (g0 + j) % 2, i * 2 + (t0 + j), (t0 + j) % 2, xT_hi, xT_lo)
                g0 += MT // 2
                m = MT // 4
                with pe.Fori(0, 2) as i:
                    for j in range(m):
                        pe.wait_ge(hid_done, h0 + 2 * j + 4)
                        n_slot(i * m + (g0 + j), (g0 + j) % 2, i + MLP_PANEL[part], range(4 * j, 4 * j + 4), hT_hi, hT_lo,
                               j == 0, j == m - 1)


def chunk_view(o, i):
    return o.rearrange("p (c s) -> p s c", s=CH), i.rearrange("p (s c) -> p s c", s=CH)


_INS = ["x", "s5_lambda_re", "s5_lambda_im", "s5_log_dt", "s5_b_re", "s5_b_im", "s5_c_re", "s5_c_im", "s5_d", "s5_w_glu",
        "dsa_w_in", "dsa_q_norm", "dsa_k_norm", "dsa_w_o", "ffn_w_gate_up", "ffn_w_down", "norm_mix", "norm_ffn",
        "mem_2", "rel_table_2", "g_mix_2", "w_in_2", "g_group_2", "sinks_2", "w_out_2", "g_cross_2", "g_mem_2",
        "w_xq_2", "w_xkv_2", "w_xo_2", "g_mlp_2", "w_up_2", "w_down_2", "g_final_2"]


def kernel(**inputs):
    import concourse.bacc as bacc
    from concourse.bass_utils import run_bass_kernel_spmd

    nc = bacc.Bacc("TRN2", target_bir_lowering=False, num_devices=1)
    arrays, w = {}, {}
    for name, value in {**{n: inputs[n] for n in _INS}, **shape_constants()}.items():
        a = np.ascontiguousarray(value)
        if name in ("x", "mem_2"):
            a = a[0]
        arrays[f"in_{name}"] = a
        w[name] = nc.dram_tensor(f"in_{name}", a.shape, mybir.dt.from_np(a.dtype), kind="ExternalInput").ap()
    out = nc.dram_tensor("out_x", (S, D), F32, kind="ExternalOutput").ap()
    program(nc, w, out)
    r = run_bass_kernel_spmd(nc, [arrays], core_ids=[0])
    return r.results[0]["out_x"][None]
```

```python
from contextlib import ExitStack

import numpy as np

import concourse.bass as bass
from concourse import mybir

F32 = mybir.dt.float32
F32R = mybir.dt.float32r
I32 = mybir.dt.int32
ALU = mybir.AluOpType
ACT = mybir.ActivationFunctionType
AX = mybir.AxisListType

P = 128
S = 512
D = 1024
TB = S // P
KT = D // P
EPS = 1e-6
NEG = -1e30

G, GH, GP = 64, 16, 64
CH = P // GH
NC = S // CH
GB = P // GH
NB = G // GB

HD = 64
NH = 16
NI = 8
TOPK = min(256, S // 4)
ROUNDS = TOPK // 8
DSA_W = 3 * D + NI * HD + HD + NI

FF = 2816
FT = FF // P
FF2 = 4096
MLP_PARTS = 2
MT = FF2 // P // MLP_PARTS

MEM = 256
NREL = 12
BUCKETS = 32
BIAS_W = S + P - 1

SLOT = 2048

GAINS = ["norm_mix0", "norm_mix1", "norm_ffn0", "norm_ffn1", "g_mix", "g_cross", "g_mem", "g_mlp", "g_group"]


def shape_constants():
    f = np.float32
    row, col = np.arange(P)[:, None], np.arange(P)[None, :]
    masks = np.stack([np.where(col <= row, 0, NEG), col >= row, col < row], 1).astype(f)
    inv = f(10000.0) ** (-np.arange(0, HD, 2, dtype=f) / f(HD))
    ang = np.arange(S, dtype=f)[:, None] * inv[None, :]
    cos, sin = np.cos(ang).astype(f), np.sin(ang).astype(f)
    rope = np.stack([np.concatenate([cos, cos], 1), np.concatenate([-sin, sin], 1)])
    rope = np.ascontiguousarray(rope.reshape(2, TB, P, HD).transpose(2, 0, 1, 3))
    dist = np.arange(BIAS_W) - (P - 1)
    n = np.maximum(dist, 0)
    big = 16 + (np.log(np.maximum(n, 1).astype(f) / f(16)) / f(np.log(128.0)) * f(16)).astype(np.int32)
    bucket = np.where(n < 16, n, np.minimum(big, BUCKETS - 1))
    times = np.where(dist >= 0, (n <= 128).astype(int) + (n % 4 == 0) + (n % 16 == 0), 0)
    basis = np.zeros((BUCKETS + 3, BIAS_W), f)
    basis[bucket, np.arange(BIAS_W)] = 1
    basis[BUCKETS] = np.where(times > 0, np.log(np.maximum(times, 1)), NEG)
    basis[BUCKETS + 1] = np.where((dist >= 0) & (dist < 128), 0, NEG)
    basis[BUCKETS + 2] = np.where(dist >= 0, 0, NEG)
    pick = np.zeros((3, NREL), f)
    pick[np.arange(NREL) // 4, np.arange(NREL)] = 1
    sign = np.where(np.arange(P) < GP, 1, -1).astype(f)[:, None]
    return {
        "c_ident": np.eye(P, dtype=f), "c_masks": masks, "c_rope": rope, "c_basis": basis, "c_pick": pick,
        "c_sign": sign,
    }


GLU_SLOT, GLU_SLOTS = 0, 8
FFN_SLOT = [8, 61]
FFN_DOWN = [4, 4, 4, 4, 4, 2]
DSA_SLOT = 42
WO_SLOT = 57
HIN_SLOT = 95
MEM_SLOT = 107
HOUT_SLOT = 109
XQ_SLOT = 113
XO_SLOT = 114
MLP_SLOT = [115, 131]
SLOTS = 147
FFN_TILE, HIN_TILE, MEM_TILE, XQ_TILE, MLP_TILE = [0, 22], 44, 52, 53, [54, 62]
GLU_PANEL, FFN_PANEL, DSA_PANEL, WO_PANEL, HIN_PANEL = 0, [4, 16], 6, 14, 18
MEM_PANEL, HOUT_PANEL, XO_PANEL, MLP_PANEL = 20, 21, 23, [25, 27]
FFN_HID, MLP_HID = [0, 22], [44, 52]




def program(nc, w, out):
    with ExitStack() as ctx:
        def sem(name):
            return ctx.enter_context(nc.semaphore(name))

        def fixed(name, shape, dt=F32):
            return ctx.enter_context(nc.sbuf_tensor(name, shape, dt))

        x_res = fixed("x_res", [P, TB, D])
        xT_hi = fixed("xT_hi", [P, KT, S], F32R)
        xT_lo = fixed("xT_lo", [P, KT, S], F32R)
        raw = fixed("raw", [P, 2, SLOT])
        w_hi = fixed("w_hi", [P, 2, SLOT], F32R)
        w_lo = fixed("w_lo", [P, 2, SLOT], F32R)
        arena = fixed("arena", [P, 2 * FT * S])
        spare = fixed("spare", [P, 3072])
        ident = fixed("ident", [P, P])
        masks = fixed("masks", [P, 3, P])
        sign = fixed("sign", [P, 1])
        gain_rows = fixed("gain_rows", [len(GAINS) * KT, P])
        gains = fixed("gains", [P, len(GAINS) * KT])
        half_neg = fixed("half_neg", [P, 64])
        half_mask = fixed("half_mask", [P, 2])
        one = fixed("one", [P, 1])
        ssq = fixed("ssq", [P, 64])
        rstd = fixed("rstd", [P, 64])
        r8 = fixed("r8", [P, G])
        neg_max = fixed("neg_max", [P, 4])
        row_sum = fixed("row_sum", [P, 4])
        inv_sum = fixed("inv_sum", [P, 4])
        sinks = fixed("sinks", [P, 4])
        sinks_neg = fixed("sinks_neg", [P, 4])
        rope = fixed("rope", [P, 2, TB, HD])
        rope_q = fixed("rope_q", [P, 2, TB, HD])
        rope_k = fixed("rope_k", [P, 2, TB, HD])
        gain_qk = fixed("gain_qk", [P, 2, HD])
        head_ss = fixed("head_ss", [P, 3, 8])
        head_rs = fixed("head_rs", [P, 3, 8])
        w_idx = fixed("w_idx", [P, TB, NI])
        top = fixed("top", [P, 8])
        above = fixed("above", [P, 1])
        sink_e = fixed("sink_e", [P, 4])
        PS = ctx.enter_context(nc.psum_tensor("PS", [P, 8, 512], F32))

        KB = 1024
        region_at = {n: nc.lookup_mloc(t).addr for n, t in (
            ("arena", arena), ("spare", spare), ("x_hi", xT_hi), ("x_lo", xT_lo), ("w_hi", w_hi), ("w_lo", w_lo),
            ("x_res", x_res), ("rope_q", rope_q), ("rope_k", rope_k))}

        def place(name, where, at, shape, dt=F32):
            return nc.alloc_sbuf_tensor_at(name, shape, dt, offset=region_at[where] + at)

        u = place("u", "arena", 0, [NC, G, CH, GH])
        y = place("y", "arena", 0, [NC, NB, CH, P])
        xp = place("xp", "arena", 32 * KB, [NC, CH, D])
        tab_c = place("tab_c", "arena", 32 * KB, [P, G, NC])
        tab_s = place("tab_s", "arena", 48 * KB, [P, G, NC])
        b_n = place("b_n", "arena", 64 * KB, [P, G, GH])
        b_s = place("b_s", "arena", 68 * KB, [P, G, GH])
        c_n = place("c_n", "arena", 72 * KB, [P, G, GH])
        c_s = place("c_s", "arena", 76 * KB, [P, G, GH])
        decay = place("decay", "arena", 80 * KB, [P, GB, NC])
        tmp_b = place("tmp_b", "arena", 82 * KB, [P, GB, CH, GH])
        pw_r = place("pw_r", "spare", 0, [P, G, CH + 1])
        pw_i = place("pw_i", "spare", 2304, [P, G, CH + 1])
        pw_rs = place("pw_rs", "spare", 4608, [P, G, CH + 1])
        pw_is = place("pw_is", "spare", 6912, [P, G, CH + 1])
        uT = place("uT", "x_hi", 0, [P, G, NC])
        nat_b = place("nat_b", "x_lo", 0, [G, 3, GP, GH])
        nat_c = place("nat_c", "x_hi", 0, [P, NB, 3, GP])
        nat_l = place("nat_l", "x_lo", 12 * KB, [G, 2, 2, GP])
        out_a = [place("out_a0", "x_lo", 0, [P, GB, CH + 1, GH]), place("out_a1", "w_lo", 10 * KB, [P, GB, CH + 1, GH])]
        out_b = place("out_b", "x_lo", 4608, [P, GB, CH, GH])
        in_w = place("in_w", "x_lo", 8704, [P, GB, CH, GH])
        small = place("small", "w_hi", 0, [P, 32, G])
        in_t = place("in_t", "w_hi", 0, [P, GB, 2, GP])
        in_s = place("in_s", "w_hi", 4 * KB, [P, GB, 2, GP])
        taps = place("taps", "w_hi", 8 * KB, [P, GB, CH, GH])
        lag = place("lag", "w_hi", 12 * KB, [GH, GB, CH, GH])
        rot1 = place("rot1", "w_lo", 0, [P, G, NC // 2])
        rot2 = place("rot2", "w_lo", 8 * KB, [P, G, NC // 2])
        v1 = place("v1", "w_lo", 0, [P, GB, NC])
        v2 = place("v2", "w_lo", 2 * KB, [P, GB, NC])
        glu_sg = place("glu_sg", "spare", 0, [P, 2, 256])
        glu_v = place("glu_v", "spare", 2 * KB, [P, 2, 256])
        z = place("z", "w_lo", 4 * KB, [P, GB, NC])
        cz = place("cz", "w_lo", 6 * KB, [P, GB, NC])
        sz = place("sz", "w_lo", 8 * KB, [P, GB, NC])
        du = place("du", "x_res", 12 * KB, [NC, GB, CH, GH])
        d_row = place("d_row", "x_res", 0, [NC, D])
        junk = place("junk", "x_res", 4 * KB, [NC, D])
        g_row = place("g_row", "x_res", 8 * KB, [NC, D])
        tmp_a = place("tmp_a", "x_res", 4 * KB, [P, GB, CH + 1, GH])

        diag = place("diag", "rope_q", 0, [P, TB, P])
        x_out = place("x_out", "x_lo", 0, [P, TB, D])
        hT_hi = place("hT_hi", "arena", 0, [P, FT, S], F32R)
        hT_lo = place("hT_lo", "arena", FT * S * 4, [P, FT, S], F32R)
        gbuf = place("gbuf", "spare", 0, [P, 2, 2, 512])
        sq_junk = place("sq_junk", "spare", 8 * KB, [P, D])

        stage = place("stage", "arena", 0, [P, 2, TB, 512])
        o_nat = place("o_nat", "arena", 0, [P, TB, D])
        qT = place("qT", "arena", 16 * KB, [P, KT, S])
        kT = place("kT", "arena", 32 * KB, [P, KT, S])
        v_dsa = place("v_dsa", "arena", 48 * KB, [P, TB, D])
        qiT = place("qiT", "arena", 64 * KB, [P, NI // 2, S])
        kiT = [place("kiT0", "arena", 72 * KB, [P, S]), place("kiT1", "arena", 48 * KB, [P, S])]
        head_n = place("head_n", "arena", 74 * KB, [P, 3, 512])
        head_sq = place("head_sq", "arena", 80 * KB, [P, 2, 512])
        head_c = place("head_c", "arena", 84 * KB, [P, 2, 512])
        ki_raw = place("ki_raw", "spare", 0, [P, TB, HD + NI])
        relu_i = place("relu_i", "spare", 2 * KB, [P, 2, 512])
        ki_n = place("ki_n", "spare", 8 * KB, [P, TB, HD])
        ki_c = place("ki_c", "spare", 1152, [P, TB, HD])
        ki_st = place("ki_st", "spare", 9 * KB, [P, TB, 3, HD])
        BLK = [0, 0, 2 * P, 5 * P]
        score = place("score", "spare", 6 * KB, [P, 9 * P])
        ranked = place("ranked", "arena", 64 * KB, [P, 9 * P])
        chosen = place("chosen", "arena", 64 * KB + 36 * P, [P, 9 * P])
        equal = place("equal", "spare", 2 * KB, [P, 512])
        seen = place("seen", "spare", 4 * KB, [P, 512])
        q_pad = place("q_pad", "rope_k", 0, [P, 4, P])
        logit = place("logit", "spare", 0, [P, 3, 512])
        probT = place("probT", "spare", 6 * KB, [P, 2, 512])
        stay = [place("stay0", "spare", 10 * KB, [P, 512]), place("stay1", "arena", 86 * KB, [P, 512])]
        hqk = place("hqk", "arena", 16 * KB, [P, 16, S])
        v_ab = place("v_ab", "arena", 48 * KB, [P, TB, 512])
        v_cd = place("v_cd", "arena", 56 * KB, [P, TB, 384])
        bias = place("bias", "arena", 62 * KB, [P, NREL, S])
        basis = place("basis", "spare", 0, [BUCKETS + 3, BIAS_W])
        table = place("table", "spare", 3 * KB, [BUCKETS + 3, NREL])
        bias_v = place("bias_v", "spare", 4 * KB, [NREL, BIAS_W])
        bias_dram = nc.dram_tensor("bias_dram", (NREL, BIAS_W), F32, kind="Internal").ap()
        mem = place("mem", "x_hi", 8 * KB, [P, 2, D])
        memT_hi = place("memT_hi", "x_hi", 0, [P, KT, MEM], F32R)
        memT_lo = place("memT_lo", "x_lo", 0, [P, KT, MEM], F32R)
        kxT = place("kxT", "arena", 62 * KB, [P, 2, MEM])
        vx = place("vx", "arena", 64 * KB, [P, 2, MEM])
        qxT = place("qxT", "arena", 66 * KB, [P, 2, S])
        late_junk = place("late_junk", "arena", 72 * KB, [P, D])
        ox = place("ox", "arena", 48 * KB, [P, TB, 256])
        g_last = place("g_last", "arena", 78 * KB, [P, D])

        w_raw = [sem("w_raw0"), sem("w_raw1")]
        w_rounded, w_split, w_used = sem("w_rounded"), sem("w_split"), sem("w_used")
        t_free, t_first = sem("t_free"), sem("t_first")
        n_free, n_ready = sem("n_free"), sem("n_ready")
        hid_act, hid_hi, hid_done = sem("hid_act"), sem("hid_hi"), sem("hid_done")
        row_sq, row_rstd, row_mean, row_norm = sem("row_sq"), sem("row_rstd"), sem("row_mean"), sem("row_norm")
        turned, x_hi_done, x_lo_done = sem("turned"), sem("x_hi_done"), sem("x_lo_done")
        glu_sig, glu_done = sem("glu_sig"), sem("glu_done")
        v_step, a_step, p_step = sem("v_step"), sem("a_step"), sem("p_step")
        ld_x, ld_par, ld_const, ld_res, stored = sem("ld_x"), sem("ld_par"), sem("ld_const"), sem("ld_res"), sem("stored")
        const_set = sem("const_set")
        s5_sq, s5_rstd, s5_u, s5_ut, s5_ut_sb = sem("s5_sq"), sem("s5_rstd"), sem("s5_u"), sem("s5_ut"), sem("s5_ut_sb")
        s5_nat, s5_nat_sb, s5_ang, s5_sin = sem("s5_nat"), sem("s5_nat_sb"), sem("s5_ang"), sem("s5_sin")
        s5_par, s5_outa, s5_outb, s5_inw, s5_dec, s5_du = sem("s5_par"), sem("s5_outa"), sem("s5_outb"), sem("s5_inw"), sem("s5_dec"), sem("s5_du")
        s5_lag, s5_lag_sb, s5_taps, s5_zero = sem("s5_lag"), sem("s5_lag_sb"), sem("s5_taps"), sem("s5_zero")
        s5_int, s5_int_sb, s5_v, s5_rot, s5_cz, s5_y, s5_ysum, s5_gelu = (
            sem("s5_int"), sem("s5_int_sb"), sem("s5_v"), sem("s5_rot"), sem("s5_cz"), sem("s5_y"), sem("s5_ysum"), sem("s5_gelu"))
        x_final = sem("x_final")
        ld_qk, qk_tables = sem("ld_qk"), sem("qk_tables")
        head_sq_done, head_sum, head_rstd, head_norm, head_sin, head_cos, head_done = (
            sem("head_sq_done"), sem("head_sum"), sem("head_rstd"), sem("head_norm"), sem("head_sin"), sem("head_cos"), sem("head_done"))
        head_t, head_t_sb = sem("head_t"), sem("head_t_sb")
        ki_squared = sem("ki_squared")
        ki_sq, ki_rs, ki_done, ki_t, ki_t_sb = sem("ki_sq"), sem("ki_rs"), sem("ki_done"), sem("ki_t"), sem("ki_t_sb")
        idx_dot, idx_relu, idx_sum, idx_chosen = sem("idx_dot"), sem("idx_relu"), sem("idx_sum"), sem("idx_chosen")
        q_padded, at_dot, at_logit, at_max, at_prob, at_turn, at_turn_sb, at_pv, at_inv, at_out = (
            sem("q_padded"), sem("at_dot"), sem("at_logit"), sem("at_max"), sem("at_prob"), sem("at_turn"),
            sem("at_turn_sb"), sem("at_pv"), sem("at_inv"), sem("at_out"))
        ld_bias, bias_row, bias_row_sb, bias_out, ld_bias_t = (
            sem("ld_bias"), sem("bias_row"), sem("bias_row_sb"), sem("bias_out"), sem("ld_bias_t"))
        grp_sq, grp_rstd, grp_norm = sem("grp_sq"), sem("grp_rstd"), sem("grp_norm")
        ld_mem, mem_sq, mem_rstd, mem_norm, ld_last = sem("ld_mem"), sem("mem_sq"), sem("mem_rstd"), sem("mem_norm"), sem("ld_last")
        gains_t, gains_sb = sem("gains_t"), sem("gains_sb")

        block = ctx.enter_context(nc.Block())

        def f32(ap):
            return ap.bitcast(F32)

        dsa_units = []
        for b in range(TB):
            for h in range(NH):
                mask = masks[:, 0, :] if b == 0 else chosen[:, BLK[b]:BLK[b] + P * (b + 1)]
                dsa_units.append((qT[:, h // 2, P * b:P * b + P], kT[:, h // 2, 0:P * (b + 1)], mask,
                                  [v_dsa[:, k, P * (h // 2):P * (h // 2) + P] for k in range(b + 1)], h % 2,
                                  o_nat[:, b, HD * h:HD * h + HD], None))

        def hybrid_units(group):
            q_at, k_at, rel, v, v_at = {"a": (0, 2, 0, v_ab, 0), "b": (4, 6, None, v_ab, 256),
                                        "c": (8, 10, 4, v_cd, 0), "d": (12, 14, 8, v_cd, 128)}[group]
            units = []
            for b in range(TB):
                for h in range(4):
                    first = max(0, b - 1) if group == "c" else 0
                    k_tile = (0, 1, 1, 0)[h] if group == "c" else h // 2
                    v_head = h // 2 if group == "c" else h
                    v_cols = slice(v_at + P * (v_head // 2), v_at + P * (v_head // 2) + P)
                    o_at = 256 * "abcd".index(group) + HD * h
                    units.append((hqk[:, q_at + h // 2, P * b:P * b + P],
                                  hqk[:, k_at + k_tile, P * first:P * (b + 1)],
                                  None if rel is None else bias[:, rel + h, 0:P * (b + 1 - first)][:, ::-1],
                                  [v[:, k, v_cols] for k in range(first, b + 1)], v_head % 2,
                                  o_nat[:, b, o_at:o_at + HD], h if group == "c" else None))
            return units

        soft_units = hybrid_units("a") + hybrid_units("c") + hybrid_units("d")
        stick_units = hybrid_units("b")
        mem_units = [(qxT[:, h // 2, P * b:P * b + P], kxT[:, h // 2, :], None,
                      [vx[:, m, P * (h // 2):P * (h // 2) + P] for m in range(2)], h % 2,
                      ox[:, b, HD * h:HD * h + HD], None)
                     for b in range(TB) for h in range(4)]
        DSA_UNIT, SOFT_UNIT, STICK_UNIT, MEM_UNIT = 0, 64, 112, 128

        def head_copied(e):
            return TB * (DSA_PANEL + 1 + (e >= TB)) + e + 1

        @block.sync
        def _(sp):
            sp.dma_start(xp[:, :, :], w["x"].rearrange("(c s) d -> c s d", s=CH)).then_inc(ld_x, 16)
            for j, name in ((0, "s5_lambda_re"), (1, "s5_lambda_im")):
                for half in range(2):
                    sp.dma_start(nat_l[:, j, half, :], w[name][0]).then_inc(ld_par, 16)
            for j, name in ((0, "s5_b_re"), (1, "s5_b_im"), (2, "s5_b_re")):
                sp.dma_start(nat_b[:, j, :, :], w[name][0]).then_inc(ld_par, 16)
            for j, name in ((0, "s5_c_re"), (1, "s5_c_im"), (2, "s5_c_re")):
                sp.dma_start(nat_c[:, :, j, :], w[name][0].rearrange("(b g) h p -> (g h) b p", g=GB)).then_inc(ld_par, 16)
            sp.dma_start(small[:, 0, :], w["s5_log_dt"][0:1, :].broadcast_to([P, G])).then_inc(ld_par, 16)
            sp.dma_start(g_row[:, :], w["norm_mix"][0:1, :].broadcast_to([NC, D])).then_inc(ld_par, 16)
            sp.dma_start(d_row[:, :], w["s5_d"][0:1, :].broadcast_to([NC, D])).then_inc(ld_par, 16)

            def slot_free(g):
                sp.wait_ge(w_split, g - 1)

            def put(par, dst, src):
                sp.dma_start(dst, src).then_inc(w_raw[par], 16)

            def load_pair(par, a, b, n):
                v = raw[:, par, 0:KT * 2 * n].rearrange("p (k t n) -> p k t n", t=2, n=n)
                put(par, v[:, :, 0, :], a)
                put(par, v[:, :, 1, :], b)

            def load_rows(par, src, n):
                m = src.shape[1]
                v = raw[:, par, 0:m * n].rearrange("p (k n) -> p k n", n=n)
                put(par, v[:, 0:m // 2, :], src[:, 0:m // 2, :])
                put(par, v[:, m // 2:m, :], src[:, m // 2:m, :])

            def tiles(ap):
                return ap.rearrange("(k p) n -> p k n", p=P)

            glu = tiles(w["s5_w_glu"][0])
            for j in range(4):
                for k in range(0, KT, 4):
                    g = GLU_SLOT + 2 * j + k // 4
                    if g >= 2:
                        slot_free(g)
                    v = raw[:, g % 2, :].rearrange("p (k t n) -> p k t n", t=2, n=256)
                    put(g % 2, v[:, :, 0, :], glu[:, k:k + 4, 256 * j:256 * j + 256])
                    put(g % 2, v[:, :, 1, :], glu[:, k:k + 4, D + 256 * j:D + 256 * j + 256])
                if j == 0:
                    sp.wait_ge(s5_zero, 1)
                    for b in range(NB):
                        sp.wait_ge(s5_lag_sb, b + 1)
                        if b >= 1:
                            sp.wait_ge(s5_y, b)
                        for s in range(CH):
                            sp.dma_start(taps[GH * s:GH * s + GH, :, s:CH, :].rearrange("p g t h -> p g (t h)"),
                                         lag[:, :, 0:CH - s, :].rearrange("p g t h -> p g (t h)")).then_inc(s5_taps, 16)
                    sp.wait_ge(s5_gelu, NB)
                    sp.dma_start(x_res[:, :, :], w["x"].rearrange("(b p) d -> p b d", p=P)).then_inc(ld_res, 16)

            def ffn_loads(layer):
                up = tiles(w["ffn_w_gate_up"][layer])
                down = tiles(w["ffn_w_down"][layer])
                g0 = FFN_SLOT[layer]
                with sp.Fori(0, FT // 2) as i:
                    for j in range(2):
                        slot_free(i * 2 + (g0 + j))
                        v = raw[:, (g0 + j) % 2, :].rearrange("p (k t n) -> p k t n", t=2, n=P)
                        put((g0 + j) % 2, v[:, :, 0, :], up[:, :, bass.ds(i * (2 * P) + j * P, P)])
                        put((g0 + j) % 2, v[:, :, 1, :], up[:, :, bass.ds(i * (2 * P) + (FF + j * P), P)])
                g0 += FT
                with sp.Fori(0, 2) as i:
                    k = 0
                    for j, m in enumerate(FFN_DOWN):
                        slot_free(i * len(FFN_DOWN) + (g0 + j))
                        load_rows((g0 + j) % 2, down[:, k:k + m, bass.ds(i * 512, 512)], 512)
                        k += m

            ffn_loads(0)

            def panel_loads(g0, src, n, kt=KT):
                for k in range(0, kt, 4):
                    slot_free(g0 + k // 4)
                    load_rows((g0 + k // 4) % 2, src[:, k:k + 4, :], n)

            w_in = tiles(w["dsa_w_in"][0])
            panel_loads(DSA_SLOT, w_in[:, :, 3 * D:3 * D + 512], 512)
            slot_free(DSA_SLOT + 2)
            load_rows((DSA_SLOT + 2) % 2, w_in[:, :, 3 * D + 512:DSA_W], DSA_W - 3 * D - 512)
            for j in range(6):
                panel_loads(DSA_SLOT + 3 + 2 * j, w_in[:, :, 512 * j:512 * j + 512], 512)
            for j in range(2):
                panel_loads(WO_SLOT + 2 * j, tiles(w["dsa_w_o"][0])[:, :, 512 * j:512 * j + 512], 512)
            ffn_loads(1)

            sp.wait_ge(hid_done, FFN_HID[1] + FT + 2)
            sp.dma_start(basis[:, :], w["c_basis"]).then_inc(ld_bias, 16)
            sp.dma_start(table[0:BUCKETS, :], w["rel_table_2"]).then_inc(ld_bias, 16)
            sp.dma_start(table[BUCKETS:BUCKETS + 3, :], w["c_pick"]).then_inc(ld_bias, 16)
            w_h = tiles(w["w_in_2"][0])

            def h_slot(g, c):
                slot_free(g)
                load_pair(g % 2, w_h[:, :, c:c + P], w_h[:, :, c + P:c + 2 * P], P)

            h_slot(HIN_SLOT, 0)
            h_slot(HIN_SLOT + 1, 256)
            for j, c in enumerate((768, 1024, 1536)):
                h_slot(HIN_SLOT + 2 + j, c)
            g = HIN_SLOT + 5
            slot_free(g)
            v = raw[:, g % 2, 0:KT * 192].rearrange("p (k n) -> p k n", n=192)
            put(g % 2, v[:, :, 0:P], w_h[:, :, 1792:1920])
            put(g % 2, v[:, :, P:192], w_h[:, :, 1792:1856])
            for j, c in enumerate((2048, 2304)):
                h_slot(HIN_SLOT + 6 + j, c)
            for k in range(0, KT, 4):
                g = HIN_SLOT + 8 + k // 4
                slot_free(g)
                v = raw[:, g % 2, :].rearrange("p (k t n) -> p k t n", t=2, n=256)
                put(g % 2, v[:, :, 0, :], w_h[:, k:k + 4, 512:768])
                put(g % 2, v[:, :, 1, :], w_h[:, k:k + 4, 1280:1536])
            for k in range(0, KT, 4):
                g = HIN_SLOT + 10 + k // 4
                slot_free(g)
                v = raw[:, g % 2, 0:4 * 384].rearrange("p (k n) -> p k n", n=384)
                put(g % 2, v[:, :, 0:P], w_h[:, k:k + 4, 1920:2048])
                put(g % 2, v[:, :, P:384], w_h[:, k:k + 4, 2560:2816])
            w_kv, w_q = tiles(w["w_xkv_2"][0]), tiles(w["w_xq_2"][0])
            slot_free(MEM_SLOT)
            load_pair(MEM_SLOT % 2, w_kv[:, :, 0:P], w_kv[:, :, P:2 * P], P)
            slot_free(MEM_SLOT + 1)
            load_rows((MEM_SLOT + 1) % 2, w_kv[:, :, 256:512], 256)
            sp.wait_ge(w_used, HIN_SLOT + 12)
            sp.dma_start(mem[:, :, :], w["mem_2"].rearrange("(b p) d -> p b d", p=P)).then_inc(ld_mem, 16)
            for j in range(2):
                panel_loads(HOUT_SLOT + 2 * j, tiles(w["w_out_2"][0])[:, :, 512 * j:512 * j + 512], 512)
            slot_free(XQ_SLOT)
            load_pair(XQ_SLOT % 2, w_q[:, :, 0:P], w_q[:, :, P:2 * P], P)
            slot_free(XO_SLOT)
            load_rows(XO_SLOT % 2, tiles(w["w_xo_2"][0]), D)
            sp.dma_start(g_last[:, :], w["g_final_2"].rearrange("(a d) -> a d", a=1).broadcast_to([P, D])).then_inc(ld_last, 16)

            up, down = tiles(w["w_up_2"][0]), tiles(w["w_down_2"][0])
            for part in range(MLP_PARTS):
                g0 = MLP_SLOT[part]
                with sp.Fori(0, MT // 4) as i:
                    for j in range(2):
                        slot_free(i * 2 + (g0 + j))
                        c = MT * P * part + 2 * P * j
                        load_pair((g0 + j) % 2, up[:, :, bass.ds(i * (4 * P) + c, P)],
                                  up[:, :, bass.ds(i * (4 * P) + (c + P), P)], P)
                g0 += MT // 2
                with sp.Fori(0, 2) as i:
                    for j in range(MT // 4):
                        slot_free(i * (MT // 4) + (g0 + j))
                        k = MT * part + 4 * j
                        load_rows((g0 + j) % 2, down[:, k:k + 4, bass.ds(i * 512, 512)], 512)

            for tb in range(TB):
                sp.wait_ge(x_final, tb + 1)
                sp.dma_start(out[P * tb:P * tb + P, :], x_out[:, tb, :]).then_inc(stored, 16)
            sp.wait_ge(stored, 16 * TB)

        @block.gpsimd
        def _(pool):
            steps = [0]

            def link(ins):
                ins.then_inc(p_step, 1)
                steps[0] += 1
                pool.wait_ge(p_step, steps[0])

            pool.memset(taps[:, :, :, :], 0.0).then_inc(s5_zero, 1)
            link(pool.memset(half_neg[:, :], -0.5))
            link(pool.memset(decay[:, :, 0:1], 0.0))
            pool.memset(one[:, :], 1.0).then_inc(const_set, 1)
            pool.wait_ge(ld_const, 16 * 10)
            for half in range(2):
                link(pool.tensor_scalar(half_mask[:, half:half + 1], sign[:, :], 1.0 - 2 * half, 0.0, ALU.mult, ALU.max))

            def rsqrt(dst, src, n, scale, parts=P):
                link(pool.tensor_scalar(dst, src, scale, EPS, ALU.mult, ALU.add))
                return pool.tensor_tensor(dst, dst, half_neg[0:parts, 0:n], ALU.pow)

            pool.wait_ge(s5_sq, CH)
            rsqrt(rstd[0:NC, 0:CH], ssq[0:NC, 0:CH], CH, 1.0 / D, NC).then_inc(s5_rstd, 1)

            pool.wait_ge(s5_par, 1)
            pool.wait_ge(s5_u, CH)
            for b in range(NB):
                gs = slice(GB * b, GB * b + GB)
                cn = c_n[:, gs, :].unsqueeze(2).broadcast_to([P, GB, CH, GH])
                cs = c_s[:, gs, :].unsqueeze(2).broadcast_to([P, GB, CH, GH])
                pr = pw_r[:, gs, 1:CH + 1].unsqueeze(3).broadcast_to([P, GB, CH, GH])
                pi = pw_is[:, gs, 1:CH + 1].unsqueeze(3).broadcast_to([P, GB, CH, GH])
                if b >= 1:
                    pool.wait_ge(s5_cz, b)
                pool.tensor_copy(decay[:, :, 1:NC], r8[:, gs].unsqueeze(2).broadcast_to([P, GB, NC - 1])).then_inc(s5_dec, 1)
                if b >= 1:
                    pool.wait_ge(s5_y, b)
                link(pool.tensor_tensor(out_b[:, :, :, :], cn, pi, ALU.mult))
                link(pool.tensor_tensor(tmp_b[:, :, :, :], cs, pr, ALU.mult))
                pool.tensor_tensor(out_b[:, :, :, :], out_b[:, :, :, :], tmp_b[:, :, :, :], ALU.subtract).then_inc(s5_outb, 1)
                if b >= 1:
                    pool.wait_ge(s5_gelu, b)
                pool.tensor_tensor(du[:, :, :, :], u[:, gs, :, :],
                                   d_row[:, P * b:P * b + P].rearrange("p (g h) -> p g h", h=GH).unsqueeze(2).broadcast_to([NC, GB, CH, GH]),
                                   ALU.mult).then_inc(s5_du, 1)

            def split_rest(g, par):
                pool.wait_ge(w_rounded, g + 1)
                pool.tensor_tensor(w_lo[:, par, :], raw[:, par, :], f32(w_hi[:, par, :]), ALU.subtract).then_inc(w_split, 1)

            def split_run(g0, n):
                for g in range(g0, g0 + n):
                    if g < SLOTS:
                        split_rest(g, g % 2)

            def norm_rstd(n):
                for tb in range(TB):
                    pool.wait_ge(row_sq, TB * n + tb + 1)
                    rsqrt(rstd[:, tb:tb + 1], ssq[:, tb:tb + 1], 1, 1.0 / D).then_inc(row_rstd, 1)

            split_run(0, 1 + GLU_SLOTS)
            norm_rstd(0)
            split_run(1 + GLU_SLOTS, 1)

            def ffn_split(layer):
                g0 = FFN_SLOT[layer] + 2
                with pool.Fori(0, FT // 2) as i:
                    for j in range(2):
                        split_rest(i * 2 + (g0 + j), (g0 + j) % 2)
                g0 += FT
                split_run(g0, 2 * len(FFN_DOWN) - 1)
                norm_rstd(1 + 2 * layer)
                split_run(g0 + 2 * len(FFN_DOWN) - 1, 1)

            ffn_split(0)

            def head_rsqrt(n):
                pool.wait_ge(head_sum, n + 1)
                if n >= 2:
                    pool.wait_ge(head_norm, n - 1)
                rsqrt(head_rs[:, n % 2, :], head_ss[:, n % 2, :], 8, 1.0 / HD).then_inc(head_rstd, 1)

            def head_cosine(e, table, tb):
                if e < TB:
                    pool.wait_ge(n_free, head_copied(e))
                else:
                    pool.wait_ge(head_norm, e - TB + 1)
                if e >= 2:
                    pool.wait_ge(head_done, e - 1)
                pool.tensor_tensor(head_c[:, e % 2, :].rearrange("p (h d) -> p h d", d=HD),
                                   head_n[:, e % 3, :].rearrange("p (h d) -> p h d", d=HD),
                                   table[:, 0, tb, :].unsqueeze(1).broadcast_to([P, 8, HD]), ALU.mult).then_inc(head_cos, 1)

            pool.wait_ge(qk_tables, 1)
            split_run(DSA_SLOT + 2, 1)
            for tb in range(TB):
                if tb == TB - 1:
                    split_run(DSA_SLOT + 3, 1)
                head_cosine(tb, rope, tb)
            split_run(DSA_SLOT + 4, 1)
            pool.wait_ge(ki_sq, 1)
            rsqrt(head_rs[:, 2, 0:TB], head_ss[:, 2, 0:TB], TB, 1.0 / HD).then_inc(ki_rs, 1)
            for j in range(4):
                split_run(DSA_SLOT + 5 + 2 * j, 1)
                for t in range(TB + 1):
                    if t == TB - 1:
                        split_run(DSA_SLOT + 6 + 2 * j, 1)
                    if t < TB:
                        head_rsqrt(TB * j + t)
                    if t >= 1:
                        head_cosine(TB * (1 + j) + t - 1, rope_q if j < 2 else rope_k, t - 1)
            split_run(DSA_SLOT + 13, 2)

            def pad_queries(units, u0, first=0, last=None):
                for t, unit in list(enumerate(units))[first:last]:
                    if u0 + t >= 4:
                        pool.wait_ge(at_dot, u0 + t - 3)
                    pool.tensor_scalar(q_pad[:, (u0 + t) % 4, :], unit[0], half_mask[:, t % 2:t % 2 + 1], None, ALU.mult).then_inc(q_padded, 1)

            pool.wait_ge(head_done, 5 * TB)
            pool.wait_ge(head_t_sb, 20)
            pad_queries(dsa_units, DSA_UNIT, 0, 4)
            split_run(DSA_SLOT + 15, 2)
            pad_queries(dsa_units, DSA_UNIT, 4)
            split_run(WO_SLOT + 2, 3)
            norm_rstd(2)
            split_run(WO_SLOT + 5, 1)
            ffn_split(1)
            split_run(HIN_SLOT + 2, 10)
            pool.wait_ge(t_free, HIN_TILE + 10)
            pad_queries(soft_units, SOFT_UNIT, 0, 4)
            split_run(MEM_SLOT, 2)
            pad_queries(soft_units, SOFT_UNIT, 4)
            pool.wait_ge(mem_sq, 2)
            rsqrt(rstd[:, 32:34], ssq[:, 32:34], 2, 1.0 / D).then_inc(mem_rstd, 1)
            pad_queries(stick_units, STICK_UNIT)
            pool.wait_ge(grp_sq, 4 * TB)
            rsqrt(rstd[:, 16:32], ssq[:, 16:32], 16, 1.0 / 256).then_inc(grp_rstd, 1)
            split_run(MEM_SLOT + 2, 2)
            split_run(HOUT_SLOT + 2, 3)
            norm_rstd(4)
            split_run(HOUT_SLOT + 5, 1)
            pool.wait_ge(t_free, XQ_TILE + 3)
            pad_queries(mem_units, MEM_UNIT)
            split_run(XQ_SLOT + 2, 1)
            norm_rstd(5)
            split_run(XO_SLOT + 2, 1)
            for part in range(MLP_PARTS):
                g0 = MLP_SLOT[part] + 2
                with pool.Fori(0, MT // 4) as i:
                    for j in range(2):
                        split_rest(i * 2 + (g0 + j), (g0 + j) % 2)
                split_run(g0 + MT // 2, MT // 2)
            norm_rstd(6)

        @block.scalar
        def _(act):
            act.dma_start(ident[:, :], w["c_ident"]).then_inc(ld_const, 16)
            act.dma_start(sign[:, :], w["c_sign"]).then_inc(ld_const, 16)
            act.dma_start(masks[:, :, :], w["c_masks"]).then_inc(ld_const, 16)
            row = 0
            for name in ("norm_mix", "norm_ffn", "g_mix_2", "g_cross_2", "g_mem_2", "g_mlp_2", "g_group_2"):
                n = w[name].shape[0] * KT
                act.dma_start(gain_rows[row:row + n, :], w[name].rearrange("a (k p) -> (a k) p", p=P)).then_inc(ld_const, 16)
                row += n

            act.dma_start(rope[:, :, :, :], w["c_rope"]).then_inc(ld_qk, 16)
            for j, name in enumerate(("dsa_q_norm", "dsa_k_norm")):
                act.dma_start(gain_qk[:, j, :], w[name][0:1, :].broadcast_to([P, HD])).then_inc(ld_qk, 16)
            act.dma_start(sinks[:, :], w["sinks_2"][0:1, :].broadcast_to([P, 4])).then_inc(ld_qk, 16)
            steps = [0]

            def link(ins):
                ins.then_inc(a_step, 1)
                steps[0] += 1
                act.wait_ge(a_step, steps[0])

            act.wait_ge(ld_x, 16)
            for s in range(CH):
                if s >= 1:
                    act.wait_ge(s5_sq, s)
                act.activation(junk[:, :], xp[:, s, :], ACT.Square, accum_out=ssq[0:NC, s:s + 1]).then_inc(s5_sq, 1)
            act.wait_ge(s5_nat, 1)
            act.activation(small[:, 1:3, :].rearrange("p a g -> p (a g)"), PS[:, 0, 0:2 * G], ACT.Copy).then_inc(s5_nat_sb, 1)
            act.wait_ge(s5_nat, 2)
            act.activation(b_n[:, :, :].rearrange("p g h -> p h g"),
                           PS[:, 1:3, :].rearrange("p b (h g) -> p (b h) g", g=G), ACT.Copy).then_inc(s5_nat_sb, 1)
            act.wait_ge(s5_nat, 3)
            act.activation(b_s[:, :, :].rearrange("p g h -> p h g"),
                           PS[:, 3:5, :].rearrange("p b (h g) -> p (b h) g", g=G), ACT.Copy).then_inc(s5_nat_sb, 1)
            act.wait_ge(s5_nat, 4)
            act.activation(c_n[:, :, :].rearrange("p g h -> p (g h)"), PS[:, 5:7, :].rearrange("p b n -> p (b n)"), ACT.Copy).then_inc(s5_nat_sb, 1)
            act.wait_ge(s5_nat, 5)
            act.activation(c_s[:, 0:G // 2, :].rearrange("p g h -> p (g h)"), PS[:, 7, :], ACT.Copy).then_inc(s5_nat_sb, 1)
            act.wait_ge(s5_nat, 6)
            act.activation(c_s[:, G // 2:G, :].rearrange("p g h -> p (g h)"), PS[:, 1, :], ACT.Copy).then_inc(s5_nat_sb, 1)
            act.wait_ge(gains_t, 1)
            act.activation(gains[:, :], PS[:, 0, 0:len(GAINS) * KT], ACT.Copy).then_inc(gains_sb, 1)
            act.wait_ge(s5_ang, 1)
            act.activation(small[:, 12, :], small[:, 11, :], ACT.Sin).then_inc(s5_sin, 1)
            act.activation(small[:, 13, :], small[:, 11, :], ACT.Sin, scale=0.5).then_inc(s5_sin, 1)
            for q in range(8):
                act.wait_ge(s5_ut, q + 1)
                act.activation(uT[:, GB * q:GB * q + GB, :].rearrange("p g c -> p (g c)"), PS[:, q, :], ACT.Copy).then_inc(s5_ut_sb, 1)

            def gelu(b):
                act.wait_ge(s5_ysum, b + 1)
                act.activation(y[:, b, :, :].rearrange("p t (g h) -> p g t h", h=GH), du[:, :, :, :], ACT.Gelu_apprx_tanh).then_inc(s5_gelu, 1)

            for b in range(NB):
                act.wait_ge(s5_int, b + 1)
                if b >= 1:
                    act.wait_ge(s5_v, b)
                pt = PS[:, 2:4, :].rearrange("p b (g r q) -> p (b g) r q", r=2, q=GP)
                act.activation(in_t[:, :, :, :], pt, ACT.Copy)
                act.activation(in_s[:, :, 0, :], pt[:, :, 1, :], ACT.Copy)
                act.activation(in_s[:, :, 1, :], pt[:, :, 0, :], ACT.Copy, scale=-1.0).then_inc(s5_int_sb, 1)
                act.wait_ge(s5_lag, b + 1)
                if b >= 1:
                    act.wait_ge(s5_taps, 16 * CH * b)
                act.activation(lag[:, :, :, :].rearrange("p g t h -> p (g t h)"),
                               PS[0:GH, 0:2, :].rearrange("p b n -> p (b n)"), ACT.Copy).then_inc(s5_lag_sb, 1)
                if b >= 1:
                    gelu(b - 1)
            gelu(NB - 1)

            def turn_hi(j0, n, gain=None, width=S, dst=xT_hi, view=None, banks=4):
                for k in range(n):
                    act.wait_ge(turned, j0 + k + 1)
                    o, i = dst[:, k, 0:width], PS[:, k % banks, 0:width]
                    if view:
                        o, i = view(o, i)
                    act.activation(o, i, ACT.Copy, scale=1.0 if gain is None else gains[:, gain * KT + k:gain * KT + k + 1]).then_inc(x_hi_done, 1)

            turn_hi(0, KT, view=chunk_view)

            def round_slot(g, par, use):
                act.wait_ge(w_raw[par], use * 32)
                if not isinstance(g, int) or g >= 2:
                    act.wait_ge(w_used, g - 1)
                act.activation(w_hi[:, par, :], raw[:, par, :], ACT.Copy).then_inc(w_rounded, 1)

            def round_run(g0, n):
                for g in range(g0, g0 + n):
                    if g < SLOTS:
                        round_slot(g, g % 2, g // 2 + 1)

            round_run(0, 2)
            act.wait_ge(ld_res, 16)
            for j in range(4):
                round_run(2 + 2 * j, 1)
                for tb in range(TB):
                    e = TB * j + tb
                    if tb < TB - 1:
                        act.wait_ge(n_ready, 3 * (GLU_PANEL + j) + tb + 1)
                    else:
                        act.wait_ge(w_used, GLU_SLOT + 2 * j + 2)
                    if e >= 2:
                        act.wait_ge(n_free, TB + e - 1)
                    act.activation(glu_sg[:, e % 2, :], PS[:, 4 + tb, 256:512], ACT.Sigmoid).then_inc(glu_sig, 1)
                if j < 3:
                    round_run(3 + 2 * j, 1)

            def norm_sq(n, sem_x, value):
                for tb in range(TB):
                    act.wait_ge(sem_x, value - (TB - 1 - tb))
                    if n + tb >= 1:
                        act.wait_ge(row_sq, TB * n + tb)
                    act.activation(sq_junk[:, :], x_res[:, tb, :], ACT.Square, accum_out=ssq[:, tb:tb + 1]).then_inc(row_sq, 1)

            norm_sq(0, glu_done, 4 * TB)
            round_run(9, 1)
            turn_hi(KT, KT, gain=2, banks=8)

            def ffn_act(layer):
                g0, t0, h0 = FFN_SLOT[layer], FFN_TILE[layer], FFN_HID[layer]
                with act.Fori(0, FT // 2) as i:
                    for j in range(2):
                        pair = (t0 + j) % 2
                        act.wait_ge(t_first, i * 2 + (t0 + j + 1))
                        act.wait_ge(hid_done, i * 2 + (h0 + j + 1))
                        act.activation(gbuf[:, pair, 0, :], PS[:, 2 * pair, :], ACT.Silu).then_inc(hid_act, 1)
                        g = g0 + j + 2
                        round_slot(i * 2 + g, g % 2, i + (g // 2 + 1))
                round_run(g0 + FT + 2, 2 * len(FFN_DOWN) - 1)
                norm_sq(1 + 2 * layer, n_free, TB * (FFN_PANEL[layer] + 3))
                round_run(g0 + FT + 1 + 2 * len(FFN_DOWN), 1)

            ffn_act(0)
            turn_hi(2 * KT, KT, gain=1, banks=8)

            def panel_wait(ni, tb, g_last_slot):
                if tb < TB - 1:
                    act.wait_ge(n_ready, 3 * ni + tb + 1)
                else:
                    act.wait_ge(w_used, g_last_slot + 1)

            def head_turned(pi, dst, at):
                for j in range(4):
                    act.wait_ge(head_t, 4 * pi + j + 1)
                    act.activation(dst[:, at + j, :], PS[:, j, :], ACT.Copy).then_inc(head_t_sb, 1)

            g = DSA_SLOT
            round_run(g + 2, 1)
            for tb in range(TB):
                if tb == TB - 1:
                    round_run(g + 3, 1)
                panel_wait(DSA_PANEL, tb, g + 1)
                if tb >= 3:
                    act.wait_ge(head_done, tb - 2)
                act.activation(head_n[:, tb % 3, :], PS[:, 4 + tb, :], ACT.Copy).then_inc(n_free, 1)
            round_run(g + 4, 1)
            act.wait_ge(w_used, g + 3)
            act.activation(ki_raw[:, :, :], PS[:, 4:8, 0:HD + NI], ACT.Copy).then_inc(n_free, TB)
            act.wait_ge(n_free, TB * (DSA_PANEL + 3))
            act.activation(ki_c[:, :, :], ki_raw[:, :, 0:HD], ACT.Square).then_inc(ki_squared, 1)
            for j in range(4):
                round_run(g + 5 + 2 * j, 1)
                for tb in range(TB):
                    if tb == TB - 1:
                        round_run(g + 6 + 2 * j, 1)
                    n, e = TB * j + tb, TB * (1 + j) + tb
                    panel_wait(DSA_PANEL + 2 + j, tb, g + 4 + 2 * j)
                    if n >= 2:
                        act.wait_ge(head_sum, n - 1)
                    act.activation(head_sq[:, n % 2, :], PS[:, 4 + tb, :], ACT.Square).then_inc(head_sq_done, 1)
                    act.wait_ge(head_done, e - 2)
                    act.activation(head_n[:, e % 3, :], PS[:, 4 + tb, :], ACT.Copy).then_inc(n_free, 1)
                if j == 0:
                    head_turned(0, qiT, 0)
                    for head in range(2):
                        act.wait_ge(ki_t, head + 1)
                        act.activation(kiT[head][:, :], PS[:, head, :], ACT.Copy).then_inc(ki_t_sb, 1)
                    for e in range(3 * NI):
                        n = P * (e // NI + 2)
                        act.wait_ge(idx_dot, e + 1)
                        if e >= 2:
                            act.wait_ge(idx_sum, e - 1)
                        act.activation(relu_i[:, e % 2, 0:n], PS[:, e % 4, 0:n], ACT.Relu, scale=HD ** -0.5).then_inc(idx_relu, 1)
                else:
                    head_turned(j, qT if j < 3 else kT, (0, 0, 4, 0)[j])
            for j in range(2):
                round_run(g + 13 + 2 * j, 1)
                for tb in range(TB):
                    if tb == TB - 1:
                        round_run(g + 14 + 2 * j, 1)
                    panel_wait(DSA_PANEL + 6 + j, tb, g + 12 + 2 * j)
                    act.activation(v_dsa[:, tb, 512 * j:512 * j + 512], PS[:, 4 + tb, :], ACT.Copy).then_inc(n_free, 1)
                if j == 0:
                    head_turned(4, kT, 4)

            def attend_act(units, u0, stick=False):
                n = len(units)
                for t in range(n + 3):
                    if stick and t < n:
                        cols = units[t][1].shape[1]
                        act.wait_ge(at_dot, u0 + t + 1)
                        if t >= 2:
                            act.wait_ge(at_prob, u0 + t - 1)
                        if t >= 3:
                            act.wait_ge(at_turn, u0 + t - 2)
                        act.activation(stay[t % 2][:, 0:cols], PS[:, t % 3, 0:cols], ACT.Sigmoid, scale=-1.0)
                        act.activation(logit[:, t % 3, 0:cols], PS[:, t % 3, 0:cols], ACT.Sigmoid).then_inc(at_logit, 1)
                        if 4 <= t < 16:
                            group_sq(t - 4, (0, 2, 3))
                    e = t - 2
                    if 0 <= e < n:
                        cols = units[e][1].shape[1]
                        act.wait_ge(at_turn, u0 + e + 1)
                        if e >= 2:
                            act.wait_ge(at_pv, u0 + e - 1)
                        act.activation(probT[:, e % 2, 0:cols], PS[:, 3 + e % 2, 0:cols], ACT.Copy).then_inc(at_turn_sb, 1)
                    if not stick and t < n:
                        cols, sink = units[t][1].shape[1], units[t][6]
                        act.wait_ge(at_max, u0 + t + 1)
                        p = logit[:, t % 3, 0:cols]
                        m = neg_max[:, t % 4:t % 4 + 1]
                        if sink is not None:
                            act.activation(sink_e[:, t % 4:t % 4 + 1], sinks[:, sink:sink + 1], ACT.Exp, bias=m)
                        act.activation(p, p, ACT.Exp, bias=m, accum_out=row_sum[:, t % 4:t % 4 + 1]).then_inc(at_prob, 1)

            def group_sq(e, groups):
                tb, j = divmod(e, len(groups))
                j = groups[j]
                if e >= 1 or j == 1:
                    act.wait_ge(grp_sq, e + (12 if j == 1 else 0))
                else:
                    act.wait_ge(at_out, STICK_UNIT)
                c = 16 + 4 * tb + j
                act.activation(late_junk[:, 0:256], o_nat[:, tb, 256 * j:256 * j + 256], ACT.Square,
                               accum_out=ssq[:, c:c + 1]).then_inc(grp_sq, 1)

            attend_act(dsa_units, DSA_UNIT)
            turn_hi(3 * KT, KT)
            round_run(WO_SLOT + 2, 3)
            norm_sq(2, n_free, TB * (WO_PANEL + 3))
            round_run(WO_SLOT + 5, 1)
            turn_hi(4 * KT, KT, gain=3, banks=8)
            ffn_act(1)

            turn_hi(5 * KT, KT, gain=4, banks=8)

            def tiles_out(g, ti, dst, scale=1.0, width=S):
                pair = ti % 2
                act.wait_ge(t_first, ti + 1)
                act.activation(dst[:, 0, :], PS[:, 2 * pair, 0:width], ACT.Copy, scale=scale)
                act.wait_ge(w_used, g + 1)
                act.activation(dst[:, 1, :], PS[:, 2 * pair + 1, 0:width], ACT.Copy, scale=scale).then_inc(t_free, 1)

            for j in range(8):
                tiles_out(HIN_SLOT + j, HIN_TILE + j, hqk[:, 2 * j:2 * j + 2, :], HD ** -0.5 if j % 2 == 0 else 1.0)
                round_run(HIN_SLOT + j + 2, 1)
                if j == 0:
                    act.wait_ge(bias_row, 1)
                    act.activation(bias_v[:, 0:512], PS[0:NREL, 4, :], ACT.Copy)
                    act.activation(bias_v[:, 512:BIAS_W], PS[0:NREL, 5, 0:BIAS_W - 512], ACT.Copy).then_inc(bias_row_sb, 1)
                    act.wait_ge(bias_row_sb, 1)
                    act.dma_start(bias_dram, bias_v[:, :]).then_inc(bias_out, 16)
                if j == 1:
                    act.wait_ge(bias_out, 16)
                    act.dma_start(bias[:, :, :], bass.AP(tensor=bias_dram.tensor, offset=0, ap=[[1, P], [BIAS_W, NREL], [1, S]]))\
                       .then_inc(ld_bias_t, 16)
            for j, (dst, n) in enumerate(((v_ab, 512), (v_cd, 384))):
                g = HIN_SLOT + 8 + 2 * j
                round_run(g + 2, 1)
                for tb in range(TB):
                    panel_wait(HIN_PANEL + j, tb, g + 1)
                    act.activation(dst[:, tb, :], PS[:, 4 + tb, 0:n], ACT.Copy).then_inc(n_free, 1)
                round_run(g + 3, 1)
            attend_act(soft_units, SOFT_UNIT)
            act.wait_ge(ld_mem, 16)
            for m in range(2):
                if m:
                    act.wait_ge(mem_sq, 1)
                act.activation(late_junk[:, :], mem[:, m, :], ACT.Square, accum_out=ssq[:, 32 + m:33 + m]).then_inc(mem_sq, 1)
            act.wait_ge(mem_sq, 2)
            attend_act(stick_units, STICK_UNIT, stick=True)
            act.wait_ge(at_out, MEM_UNIT)
            for tb in range(TB):
                group_sq(tb, (1,))

            turn_hi(6 * KT, KT, gain=6, width=MEM, dst=memT_hi)
            tiles_out(MEM_SLOT, MEM_TILE, kxT, width=MEM)
            round_run(MEM_SLOT + 2, 1)
            act.wait_ge(n_ready, 3 * MEM_PANEL + 3)
            act.activation(vx[:, 0, :], PS[:, 4, 0:MEM], ACT.Copy)
            act.wait_ge(w_used, MEM_SLOT + 2)
            act.activation(vx[:, 1, :], PS[:, 5, 0:MEM], ACT.Copy).then_inc(n_free, TB)
            round_run(MEM_SLOT + 3, 1)
            turn_hi(7 * KT, KT, gain=8)
            round_run(HOUT_SLOT + 2, 3)

            norm_sq(4, n_free, TB * (HOUT_PANEL + 3))
            round_run(HOUT_SLOT + 5, 1)
            turn_hi(8 * KT, KT, gain=5, banks=8)
            tiles_out(XQ_SLOT, XQ_TILE, qxT, HD ** -0.5)
            attend_act(mem_units, MEM_UNIT)
            turn_hi(9 * KT, 2)
            round_run(XQ_SLOT + 2, 1)

            norm_sq(5, n_free, TB * (XO_PANEL + 3))
            round_run(XO_SLOT + 2, 1)
            turn_hi(9 * KT + 2, KT, gain=7, banks=8)
            for part in range(MLP_PARTS):
                g0, t0, h0 = MLP_SLOT[part], MLP_TILE[part], MLP_HID[part]
                with act.Fori(0, MT // 4) as i:
                    for j in range(2):
                        pair = (t0 + j) % 2
                        act.wait_ge(t_first, i * 2 + (t0 + j + 1))
                        act.wait_ge(hid_done, i * 2 + (h0 + j + 1))
                        act.activation(gbuf[:, pair, 0, :], PS[:, 2 * pair, :], ACT.Relu)
                        act.wait_ge(w_used, i * 2 + (g0 + j + 1))
                        act.activation(gbuf[:, pair, 1, :], PS[:, 2 * pair + 1, :], ACT.Relu).then_inc(t_free, 1)
                        g = g0 + j + 2
                        round_slot(i * 2 + g, g % 2, i + (g // 2 + 1))
                round_run(g0 + MT // 2 + 2, MT // 2)
            norm_sq(6, n_free, TB * (MLP_PANEL[1] + 3))

        @block.vector
        def _(dve):
            steps = [0]

            def link(ins):
                ins.then_inc(v_step, 1)
                steps[0] += 1
                dve.wait_ge(v_step, steps[0])

            def pt(i):
                return small[:, i, :]

            tt, ts, stt = dve.tensor_tensor, dve.tensor_scalar, dve.scalar_tensor_tensor
            dve.memset(neg_max[:, 0:1], 0.0).then_inc(t_free, 2)
            dve.memset(neg_max[:, 1:2], 0.0).then_inc(n_free, TB)
            dve.memset(neg_max[:, 2:3], 0.0).then_inc(hid_done, 2)

            def exp_small(dst, x, a, b, c):
                link(ts(a, x, 88.0, -87.0, ALU.min, ALU.max))
                link(ts(b.bitcast(I32), a, 1.4426950408889634, None, ALU.mult))
                link(dve.tensor_copy(c, b.bitcast(I32)))
                link(stt(a, c, -0.693359375, a, ALU.mult, ALU.add))
                link(stt(a, c, 2.12194440e-4, a, ALU.mult, ALU.add))
                link(ts(b.bitcast(I32), c, 127.0, 8388608.0, ALU.add, ALU.mult))
                link(ts(c, a, 1.0 / 5040, None, ALU.mult))
                for f in (720, 120, 24, 6, 2, 1):
                    link(stt(c, c, 1.0 / f, a, ALU.add, ALU.mult))
                link(stt(dst, c, 1.0, b, ALU.add, ALU.mult))

            dve.wait_ge(ld_par, 16 * 13)
            dve.wait_ge(ld_const, 16 * 10)
            dve.wait_ge(s5_nat_sb, 1)
            exp_small(pt(3), pt(0), pt(4), pt(5), pt(6))
            link(tt(pt(7), pt(1), pt(3), ALU.mult))
            exp_small(pt(8), pt(7), pt(4), pt(5), pt(6))
            link(tt(pt(9), pt(2), pt(3), ALU.mult))
            link(ts(pt(5).bitcast(I32), pt(9), 0.15915494309189535, None, ALU.mult))
            link(dve.tensor_copy(pt(6), pt(5).bitcast(I32)))
            link(stt(pt(9), pt(6), -6.28125, pt(9), ALU.mult, ALU.add))
            link(stt(pt(9), pt(6), -1.9353071795864769e-3, pt(9), ALU.mult, ALU.add))
            ts(pt(11), pt(9), 3.1415925, -3.1415925, ALU.min, ALU.max).then_inc(s5_ang, 1)
            dve.wait_ge(s5_sin, 2)
            link(tt(pt(14), pt(13), pt(13), ALU.mult))
            link(ts(pt(14), pt(14), -2.0, 1.0, ALU.mult, ALU.add))
            link(tt(pw_r[:, :, 1], pt(8), pt(14), ALU.mult))
            link(tt(pw_i[:, :, 1], pt(8), pt(12), ALU.mult))
            link(dve.memset(pw_r[:, :, 0], 1.0))
            link(dve.memset(pw_i[:, :, 0], 0.0))
            link(tt(pt(4), pt(8), pt(8), ALU.mult))
            link(tt(pt(4), pt(4), pt(4), ALU.mult))
            link(tt(r8[:, :], pt(4), pt(4), ALU.mult))
            link(tt(pt(4), pt(1), pt(1), ALU.mult))
            link(tt(pt(5), pt(2), pt(2), ALU.mult))
            link(tt(pt(4), pt(4), pt(5), ALU.add))
            link(dve.reciprocal(pt(4), pt(4)))
            link(ts(pt(5), pw_r[:, :, 1], -1.0, None, ALU.add))
            link(tt(pt(15), pt(5), pt(1), ALU.mult))
            link(tt(pt(16), pw_i[:, :, 1], pt(2), ALU.mult))
            link(tt(pt(15), pt(15), pt(16), ALU.add))
            link(tt(pt(15), pt(15), pt(4), ALU.mult))
            link(tt(pt(16), pw_i[:, :, 1], pt(1), ALU.mult))
            link(tt(pt(17), pt(5), pt(2), ALU.mult))
            link(tt(pt(16), pt(16), pt(17), ALU.subtract))
            link(tt(pt(16), pt(16), pt(4), ALU.mult))
            link(ts(pt(16), pt(16), sign[:, 0:1], None, ALU.mult))
            qr = pt(15).unsqueeze(2).broadcast_to([P, G, GH])
            qi = pt(16).unsqueeze(2).broadcast_to([P, G, GH])

            def rot(buf, k):
                return buf[:, 32 * k:32 * k + 32, :].rearrange("p a b -> p (a b)").rearrange("p (g h) -> p g h", h=GH)

            dve.wait_ge(s5_nat_sb, 6)
            link(tt(rot(rot1, 0), b_n[:, :, :], qr, ALU.mult))
            link(tt(rot(rot1, 1), b_s[:, :, :], qi, ALU.mult))
            link(tt(rot(rot2, 0), b_s[:, :, :], qr, ALU.mult))
            link(tt(rot(rot2, 1), b_n[:, :, :], qi, ALU.mult))
            link(tt(b_n[:, :, :], rot(rot1, 0), rot(rot1, 1), ALU.subtract))
            link(tt(b_s[:, :, :], rot(rot2, 0), rot(rot2, 1), ALU.add))

            def cmul(o_r, o_i, x_r, x_i, y_r, y_i, n):
                y_r, y_i = (y.unsqueeze(2).broadcast_to([P, G, n]) for y in (y_r, y_i))
                s1, s2 = rot1[:, :, 0:n], rot2[:, :, 0:n]
                link(tt(s1, x_r, y_r, ALU.mult))
                link(tt(s2, x_i, y_i, ALU.mult))
                link(tt(o_r, s1, s2, ALU.subtract))
                link(tt(s1, x_r, y_i, ALU.mult))
                link(tt(s2, x_i, y_r, ALU.mult))
                link(tt(o_i, s1, s2, ALU.add))

            for lo, n, e in ((1, 1, 1), (1, 2, 2), (1, 4, 4)):
                cmul(pw_r[:, :, lo + e:lo + e + n], pw_i[:, :, lo + e:lo + e + n],
                     pw_r[:, :, lo:lo + n], pw_i[:, :, lo:lo + n], pw_r[:, :, e], pw_i[:, :, e], n)
            link(ts(pw_rs[:, :, :], pw_r[:, :, :], sign[:, 0:1], None, ALU.mult))
            ts(pw_is[:, :, :], pw_i[:, :, :], sign[:, 0:1], -1.0, ALU.mult, ALU.mult).then_inc(s5_par, 1)
            dve.wait_ge(s5_rstd, 1)
            for s in range(CH):
                stt(u[:, :, s, :], xp[:, s, :].rearrange("p (g h) -> p g h", h=GH), rstd[0:NC, s:s + 1],
                    g_row[:, :].rearrange("p (g h) -> p g h", h=GH), ALU.mult, ALU.mult).then_inc(s5_u, 1)
            turn = [(pt(14), pt(12)), (pt(18), pt(19))]
            for k in range(3 + 6):
                (c0, s0), (c1, s1) = turn[k % 2], turn[(k + 1) % 2]
                if k >= 3:
                    n = 1 << (k - 3)
                    if k == 3:
                        link(dve.memset(tab_c[:, :, 0:1], 1.0))
                        link(dve.memset(tab_s[:, :, 0:1], 0.0))
                    cmul(tab_c[:, :, n:2 * n], tab_s[:, :, n:2 * n], tab_c[:, :, 0:n], tab_s[:, :, 0:n], c0, s0, n)
                link(tt(pt(20), c0, c0, ALU.mult))
                link(tt(pt(21), s0, s0, ALU.mult))
                link(tt(c1, pt(20), pt(21), ALU.subtract))
                link(tt(pt(20), c0, s0, ALU.mult))
                link(ts(s1, pt(20), 2.0, None, ALU.mult))

            def ysum(b):
                dve.wait_ge(s5_y, b + 1)
                dve.wait_ge(s5_du, b + 1)
                flat = du[:, :, :, :].rearrange("p g t h -> p (g t h)")
                tt(flat, PS[0:NC, 6:8, :].rearrange("p b n -> p (b n)"), flat, ALU.add).then_inc(s5_ysum, 1)

            dve.wait_ge(s5_ut_sb, 8)
            def over_k(ap, b, n):
                return ap[:, GB * b:GB * b + GB, :].unsqueeze(2).broadcast_to([P, GB, n, GH])

            def output_map(b):
                o = out_a[b % 2]
                gs = slice(GB * b, GB * b + GB)
                p_re, p_im = (t[:, gs, 0:CH + 1].unsqueeze(3).broadcast_to([P, GB, CH + 1, GH]) for t in (pw_rs, pw_i))
                if b >= 2:
                    dve.wait_ge(s5_y, b - 1)
                dve.wait_ge(s5_inw, min(b + 1, NB))
                link(tt(o[:, :, :, :], over_k(c_n, b, CH + 1), p_re, ALU.mult))
                link(tt(tmp_a[:, :, :, :], over_k(c_s, b, CH + 1), p_im, ALU.mult))
                tt(o[:, :, :, :], o[:, :, :, :], tmp_a[:, :, :, :], ALU.subtract).then_inc(s5_outa, 1)

            def input_map(b):
                gs = slice(GB * b, GB * b + GB)
                p_re, p_im = (t[:, gs, 0:CH][:, :, ::-1].unsqueeze(3).broadcast_to([P, GB, CH, GH]) for t in (pw_r, pw_is))
                if b >= 1:
                    dve.wait_ge(s5_int, b)
                    dve.wait_ge(s5_outa, b)
                link(tt(in_w[:, :, :, :], over_k(b_n, b, CH), p_re, ALU.mult))
                link(tt(tmp_a[:, :, 0:CH, :], over_k(b_s, b, CH), p_im, ALU.mult))
                tt(in_w[:, :, :, :], in_w[:, :, :, :], tmp_a[:, :, 0:CH, :], ALU.add).then_inc(s5_inw, 1)

            def chunk_scan(b):
                gs = slice(GB * b, GB * b + GB)
                dve.wait_ge(s5_v, b + 1)
                ps_v = PS[:, 4, :].rearrange("p (g c) -> p g c", c=NC)
                ps_s = PS[:, 5, :].rearrange("p (g c) -> p g c", c=NC)
                link(tt(v1[:, :, :], ps_v, tab_c[:, gs, :], ALU.mult))
                tt(v2[:, :, :], ps_s, tab_s[:, gs, :], ALU.mult).then_inc(s5_rot, 1)
                dve.wait_ge(s5_rot, b + 1)
                link(tt(v1[:, :, :], v1[:, :, :], v2[:, :, :], ALU.add))
                dve.wait_ge(s5_dec, b + 1)
                if b >= 1:
                    dve.wait_ge(s5_cz, b)
                link(dve.tensor_tensor_scan(z[:, :, :].rearrange("p g c -> p (g c)"),
                                            decay[:, :, :].rearrange("p g c -> p (g c)"),
                                            v1[:, :, :].rearrange("p g c -> p (g c)"), 0.0, ALU.mult, ALU.add))
                if b == 0:
                    link(dve.memset(cz[:, :, 0:1], 0.0))
                    link(dve.memset(sz[:, :, 0:1], 0.0))
                if b >= 1:
                    dve.wait_ge(s5_y, b)
                link(tt(cz[:, :, 1:NC], z[:, :, 0:NC - 1], tab_c[:, gs, 0:NC - 1], ALU.mult))
                tt(sz[:, :, 1:NC], z[:, :, 0:NC - 1], tab_s[:, gs, 0:NC - 1], ALU.mult).then_inc(s5_cz, 1)

            for b in range(2):
                input_map(b)
                output_map(b)
            for b in range(NB):
                chunk_scan(b)
                if b + 2 < NB:
                    input_map(b + 2)
                ysum(b)
                if b + 2 < NB:
                    output_map(b + 2)

            def turn_lo(j0, n, gain=None, width=S, hi=xT_hi, lo=xT_lo, view=None, banks=4):
                for k in range(n):
                    dve.wait_ge(x_hi_done, j0 + k + 1)
                    o, h, i = lo[:, k, 0:width], f32(hi[:, k, 0:width]), PS[:, k % banks, 0:width]
                    if view:
                        (o, i), (h, i) = view(o, i), view(h, i)
                        tt(o, i, h, ALU.subtract).then_inc(x_lo_done, 1)
                    else:
                        s = 1.0 if gain is None else gains[:, gain * KT + k:gain * KT + k + 1]
                        stt(o, i, s, h, ALU.mult, ALU.subtract).then_inc(x_lo_done, 1)

            turn_lo(0, KT, view=chunk_view)
            def norm_row(n, tb):
                dve.wait_ge(row_rstd, TB * n + tb + 1)
                if n == 6:
                    dve.wait_ge(ld_last, 16)
                    stt(x_out[:, tb, :], x_res[:, tb, :], rstd[:, tb:tb + 1], g_last[:, :], ALU.mult, ALU.mult).then_inc(x_final, 1)
                    return
                ts(diag[:, tb, :], ident[:, :], rstd[:, tb:tb + 1], None, ALU.mult).then_inc(row_norm, 1)

            def norm_after(n, tb):
                if tb >= 1:
                    norm_row(n, tb - 1)
                if tb == TB - 1:
                    norm_row(n, tb)

            dve.wait_ge(ld_res, 16)
            dve.wait_ge(gains_sb, 1)
            for e in range(4 * TB):
                j, tb = divmod(e, TB)
                dve.wait_ge(glu_sig, e + 1)
                tt(glu_v[:, e % 2, :], PS[:, 4 + tb, 0:256], glu_sg[:, e % 2, :], ALU.mult).then_inc(n_free, 1)
                dve.wait_ge(n_free, TB + e + 1)
                xs = x_res[:, tb, 256 * j:256 * j + 256]
                tt(xs, xs, glu_v[:, e % 2, :], ALU.add).then_inc(glu_done, 1)
                if j == 3:
                    norm_after(0, tb)
            turn_lo(KT, KT, gain=2, banks=8)

            def add_panel(ni, g_done, cols, extra=0, norm=None):
                for tb in range(TB):
                    if tb < TB - 1:
                        dve.wait_ge(n_ready, ni * 3 + (tb + 1 + extra))
                    else:
                        dve.wait_ge(w_used, g_done)
                    tt(x_res[:, tb, cols], x_res[:, tb, cols], PS[:, 4 + tb, :], ALU.add).then_inc(n_free, 1)
                    if norm is not None:
                        norm_after(norm, tb)

            def ffn_dve(layer):
                t0, h0 = FFN_TILE[layer], FFN_HID[layer]
                g0 = FFN_SLOT[layer]
                with dve.Fori(0, FT // 2) as i:
                    for j in range(2):
                        pair = (t0 + j) % 2
                        dve.wait_ge(w_used, i * 2 + (g0 + j + 1))
                        dve.wait_ge(hid_act, i * 2 + (h0 + j + 1))
                        tt(gbuf[:, pair, 1, :], gbuf[:, pair, 0, :], PS[:, 2 * pair + 1, :], ALU.mult).then_inc(t_free, 1)
                        dve.wait_ge(t_free, i * 2 + (t0 + j + 3))
                        dve.tensor_copy(hT_hi[:, bass.ds(i * 2 + j, 1), :], gbuf[:, pair, 1:2, :]).then_inc(hid_hi, 1)
                        dve.wait_ge(hid_hi, i * 2 + (h0 + j + 1))
                        tt(hT_lo[:, bass.ds(i * 2 + j, 1), :], gbuf[:, pair, 1:2, :], f32(hT_hi[:, bass.ds(i * 2 + j, 1), :]),
                           ALU.subtract).then_inc(hid_done, 1)
                m = len(FFN_DOWN)
                for i in range(2):
                    add_panel(i + FFN_PANEL[layer], i * m + (g0 + FT + m), slice(512 * i, 512 * i + 512),
                              norm=(None, 1 + 2 * layer)[i])

            ffn_dve(0)
            turn_lo(2 * KT, KT, gain=1, banks=8)
            dve.wait_ge(ld_qk, 16 * 4)
            for j, (dst, scale) in enumerate(((rope_q, HD ** -0.5), (rope_k, 1.0))):
                g = gain_qk[:, j, :].unsqueeze(1).broadcast_to([P, TB, HD])
                link(tt(dst[:, 0, :, :], rope[:, 0, :, :], g, ALU.mult))
                for half in range(2):
                    to, of = slice(32 * half, 32 * half + 32), slice(32 - 32 * half, 64 - 32 * half)
                    g = gain_qk[:, j, of].unsqueeze(1).broadcast_to([P, TB, 32])
                    link(tt(dst[:, 1, :, to], rope[:, 1, :, to], g, ALU.mult))
                if scale != 1.0:
                    link(ts(dst[:, :, :, :], dst[:, :, :, :], scale, None, ALU.mult))
            ts(sinks_neg[:, :], sinks[:, :], -1.0, None, ALU.mult).then_inc(qk_tables, 1)

            def swap_halves(ap):
                return ap.rearrange("p (h t d) -> p h t d", t=2, d=HD // 2)[:, :, ::-1, :]

            def head_sums(n):
                dve.wait_ge(head_sq_done, n + 1)
                if n >= 2:
                    dve.wait_ge(head_rstd, n - 1)
                dve.tensor_reduce(head_ss[:, n % 2, :], head_sq[:, n % 2, :].rearrange("p (h d) -> p h d", d=HD),
                                  AX.X, ALU.add).then_inc(head_sum, 1)

            def head_scale(n):
                e = n + TB
                dve.wait_ge(n_free, head_copied(e))
                dve.wait_ge(head_rstd, n + 1)
                hn = head_n[:, e % 3, :].rearrange("p (h d) -> p h d", d=HD)
                tt(hn, hn, head_rs[:, n % 2, :].unsqueeze(2).broadcast_to([P, 8, HD]), ALU.mult).then_inc(head_norm, 1)

            def head_sine(e, table, tb):
                pi = e // TB
                if pi == 0:
                    dve.wait_ge(n_free, head_copied(e))
                else:
                    dve.wait_ge(head_norm, e - TB + 1)
                if pi >= 2:
                    dve.wait_ge(head_t, 4 * (pi - 1))
                sin = table[:, 1, tb, :].rearrange("p (t d) -> p t d", t=2).unsqueeze(1).broadcast_to([P, 8, 2, HD // 2])
                tt(stage[:, pi % 2, tb, :].rearrange("p (h t d) -> p h t d", t=2, d=HD // 2),
                   swap_halves(head_n[:, e % 3, :]), sin, ALU.mult).then_inc(head_sin, 1)

            def head_add(e, tb):
                st = stage[:, (e // TB) % 2, tb, :]
                dve.wait_ge(head_cos, e + 1)
                dve.wait_ge(head_sin, e + 1)
                tt(st, st, head_c[:, e % 2, :], ALU.add).then_inc(head_done, 1)

            for t in range(TB + 1):
                if t < TB:
                    head_sine(t, rope, t)
                if t >= 1:
                    head_add(t - 1, t - 1)
            dve.wait_ge(ki_squared, 1)
            dve.tensor_reduce(head_ss[:, 2, 0:TB], ki_c[:, :, :], AX.X, ALU.add).then_inc(ki_sq, 1)
            ts(w_idx[:, :, :], ki_raw[:, :, HD:HD + NI], NI ** -0.5, None, ALU.mult)
            dve.wait_ge(ki_rs, 1)
            link(tt(ki_n[:, :, :], ki_raw[:, :, 0:HD], head_rs[:, 2, 0:TB].unsqueeze(2).broadcast_to([P, TB, HD]), ALU.mult))
            for half in range(2):
                to, of = slice(32 * half, 32 * half + 32), slice(32 - 32 * half, 64 - 32 * half)
                link(tt(ki_c[:, :, to], ki_n[:, :, of], rope[:, 1, :, to], ALU.mult))
            link(tt(ki_n[:, :, :], ki_n[:, :, :], rope[:, 0, :, :], ALU.mult))
            tt(ki_st[:, :, 1, :], ki_n[:, :, :], ki_c[:, :, :], ALU.add).then_inc(ki_done, 1)
            for side in (0, 2):
                dve.memset(ki_st[:, :, side, :], 0.0).then_inc(ki_done, 1)

            def index_scores():
                for e in range(3 * NI):
                    b, h = e // NI + 1, e % NI
                    n = P * (b + 1)
                    sc = score[:, BLK[b]:BLK[b] + n]
                    dve.wait_ge(idx_relu, e + 1)
                    if h == 0:
                        if e:
                            dve.wait_ge(idx_sum, e)
                        ts(sc, relu_i[:, e % 2, 0:n], w_idx[:, b, h:h + 1], None, ALU.mult).then_inc(idx_sum, 1)
                    else:
                        dve.wait_ge(idx_sum, e)
                        stt(sc, relu_i[:, e % 2, 0:n], w_idx[:, b, h:h + 1], sc, ALU.mult, ALU.add).then_inc(idx_sum, 1)

            def choose_rounds(b, first, last):
                n = P * (b + 1)
                cols = slice(BLK[b], BLK[b] + n)
                sc, rk = score[:, cols], ranked[:, cols]
                if first == 0:
                    link(tt(sc[:, n - P:n], sc[:, n - P:n], masks[:, 0, :], ALU.add))
                for r in range(first, last):
                    link(dve.max(top[:, :], sc if r == 0 else rk))
                    if r < ROUNDS - 1:
                        link(dve.match_replace(rk, top[:, :], sc if r == 0 else rk, 3 * NEG))

            def choose(b):
                n = P * (b + 1)
                cols = slice(BLK[b], BLK[b] + n)
                sc, rk = score[:, cols], ranked[:, cols]
                least = top[:, 7:8]
                link(ts(rk, sc, least, None, ALU.is_gt))
                link(dve.tensor_reduce(above[:, :], rk, AX.X, ALU.add))
                link(ts(equal[:, 0:n], sc, least, None, ALU.is_equal))
                link(dve.tensor_tensor_scan(seen[:, 0:n], one[:, 0:1].broadcast_to([P, n]), equal[:, 0:n], 0.0, ALU.mult, ALU.add))
                link(ts(seen[:, 0:n], seen[:, 0:n], above[:, 0:1], float(TOPK), ALU.add, ALU.is_le))
                link(tt(seen[:, 0:n], seen[:, 0:n], equal[:, 0:n], ALU.mult))
                link(tt(rk, rk, seen[:, 0:n], ALU.add))
                ts(chosen[:, cols], rk, -1.0, -NEG, ALU.add, ALU.mult).then_inc(idx_chosen, 1)

            for j in range(4):
                table = rope_q if j < 2 else rope_k
                for t in range(TB + 2):
                    n, e = TB * j + t, TB * (1 + j) + t
                    if t < TB:
                        head_sums(n)
                    if 1 <= t <= TB:
                        head_scale(n - 1)
                        head_sine(e - 1, table, t - 1)
                    if t >= 2:
                        head_add(e - 2, t - 2)
                if j == 0:
                    index_scores()
                if j == 1:
                    choose_rounds(1, 0, 10)
                if j == 2:
                    choose_rounds(1, 10, ROUNDS)
                    choose(1)
            for b in (2, 3):
                choose_rounds(b, 0, ROUNDS)
                choose(b)

            def attend_dve(units, u0, stick=False):
                n = len(units)
                for t in range(n + 3):
                    if t < n:
                        cols, add, sink = units[t][1].shape[1], units[t][2], units[t][6]
                        lg, s, m = logit[:, t % 3, 0:cols], PS[:, t % 3, 0:cols], neg_max[:, t % 4:t % 4 + 1]
                        dve.wait_ge(at_dot, u0 + t + 1)
                        if t >= 3 and not stick:
                            dve.wait_ge(at_turn, u0 + t - 2)
                        if stick:
                            dve.wait_ge(at_logit, u0 + t + 1)
                            rest, diagonal = stay[t % 2][:, 0:cols], slice(cols - P, cols)
                            link(tt(rest[:, diagonal], rest[:, diagonal], masks[:, 1, :], ALU.max))
                            link(tt(lg[:, diagonal], lg[:, diagonal], masks[:, 2, :], ALU.mult))
                            dve.tensor_tensor_scan(rest[:, ::-1], rest[:, ::-1], one[:, 0:1].broadcast_to([P, cols]), 1.0,
                                                   ALU.mult, ALU.mult).then_inc(at_max, 1)
                            dve.wait_ge(at_max, u0 + t + 1)
                            tt(lg[:, 0:cols - 1], lg[:, 0:cols - 1], rest[:, 1:cols], ALU.mult).then_inc(at_prob, 1)
                        else:
                            if add is None:
                                dve.tensor_copy(lg, s).then_inc(at_logit, 1)
                            else:
                                tt(lg, s, add, ALU.add).then_inc(at_logit, 1)
                            dve.wait_ge(at_logit, u0 + t + 1)
                            ins = dve.tensor_reduce(m, lg, AX.X, ALU.max, negate=True)
                            if sink is not None:
                                link(ins)
                                ins = tt(m, m, sinks_neg[:, sink:sink + 1], ALU.min)
                            ins.then_inc(at_max, 1)
                    e = t - 3
                    if e >= 0:
                        half, o, sink = units[e][4:7]
                        c = slice(e % 4, e % 4 + 1)
                        dve.wait_ge(at_pv, u0 + e + 1)
                        if stick:
                            dve.tensor_copy(o, PS[:, 5 + e % 2, HD * half:HD * half + HD]).then_inc(at_out, 1)
                            continue
                        if sink is not None:
                            link(tt(row_sum[:, c], row_sum[:, c], sink_e[:, c], ALU.add))
                        link(dve.reciprocal(inv_sum[:, c], row_sum[:, c]))
                        ts(o, PS[:, 5 + e % 2, HD * half:HD * half + HD], inv_sum[:, c], None, ALU.mult).then_inc(at_out, 1)

            attend_dve(dsa_units, DSA_UNIT)
            turn_lo(3 * KT, KT)
            for j in range(2):
                add_panel(WO_PANEL + j, WO_SLOT + 2 * j + 2, slice(512 * j, 512 * j + 512), norm=(None, 2)[j])
            turn_lo(4 * KT, KT, gain=3, banks=8)
            ffn_dve(1)

            turn_lo(5 * KT, KT, gain=4, banks=8)
            dve.wait_ge(ld_bias_t, 16)
            attend_dve(soft_units, SOFT_UNIT)
            dve.wait_ge(mem_rstd, 1)
            for m in range(2):
                ts(mem[:, m, :], mem[:, m, :], rstd[:, 32 + m:33 + m], None, ALU.mult).then_inc(mem_norm, 1)
            attend_dve(stick_units, STICK_UNIT, stick=True)
            turn_lo(6 * KT, KT, gain=6, width=MEM, hi=memT_hi, lo=memT_lo)
            dve.wait_ge(grp_rstd, 1)
            for tb in range(TB):
                y4 = o_nat[:, tb, :].rearrange("p (g n) -> p g n", g=4)
                tt(y4, y4, rstd[:, 16 + 4 * tb:20 + 4 * tb].unsqueeze(2).broadcast_to([P, 4, 256]), ALU.mult).then_inc(grp_norm, 1)
            turn_lo(7 * KT, KT, gain=8)
            for j in range(2):
                add_panel(HOUT_PANEL + j, HOUT_SLOT + 2 * j + 2, slice(512 * j, 512 * j + 512), norm=(None, 4)[j])

            turn_lo(8 * KT, KT, gain=5, banks=8)
            attend_dve(mem_units, MEM_UNIT)
            turn_lo(9 * KT, 2)
            for j in range(2):
                for tb in range(TB):
                    if j == 1 and tb == TB - 1:
                        dve.wait_ge(w_used, XO_SLOT + 1)
                    else:
                        dve.wait_ge(n_ready, 3 * XO_PANEL + TB * j + tb + 1)
                    xs = x_res[:, tb, 512 * j:512 * j + 512]
                    tt(xs, xs, PS[:, 4 + tb, :], ALU.add).then_inc(n_free, 1)
                    if j == 1:
                        norm_after(5, tb)

            turn_lo(9 * KT + 2, KT, gain=7, banks=8)
            for part in range(MLP_PARTS):
                g0, t0, h0 = MLP_SLOT[part], MLP_TILE[part], MLP_HID[part]
                with dve.Fori(0, MT // 4) as i:
                    for j in range(2):
                        pair = (t0 + j) % 2
                        gb = gbuf[:, pair, :, :]
                        hi = hT_hi[:, bass.ds(i * 4 + 2 * j, 2), :]
                        dve.wait_ge(t_free, i * 2 + (t0 + j + 3))
                        tt(gb, gb, gb, ALU.mult).then_inc(hid_act, 1)
                        dve.wait_ge(hid_act, i * 2 + (h0 + j + 1))
                        dve.tensor_copy(hi, gb).then_inc(hid_hi, 1)
                        dve.wait_ge(hid_hi, i * 2 + (h0 + j + 1))
                        tt(hT_lo[:, bass.ds(i * 4 + 2 * j, 2), :], gb, f32(hi), ALU.subtract).then_inc(hid_done, 1)
                m = MT // 4
                for i in range(2):
                    add_panel(i + MLP_PANEL[part], i * m + (g0 + MT // 2 + m), slice(512 * i, 512 * i + 512), 1,
                              norm=6 if part and i else None)

        @block.tensor
        def _(pe):
            mm, tr = pe.matmul, pe.transpose
            id64 = ident[0:64, 0:64]
            pe.wait_ge(ld_const, 16 * 10)
            pe.wait_ge(ld_par, 16 * 13)
            for j in range(2):
                ins = tr(PS[:, 0, G * j:G * j + G], nat_l[:, j, :, :].rearrange("g a p -> g (a p)"), id64)
            ins.then_inc(s5_nat, 1)
            for order, bank in ((0, 1), (1, 3)):
                for h in range(GH):
                    ins = tr(PS[:, bank + h // 8, G * (h % 8):G * (h % 8) + G],
                             nat_b[:, order:order + 2, :, h].rearrange("g a p -> g (a p)"), id64)
                ins.then_inc(s5_nat, 1)
            for b in range(NB):
                ins = tr(PS[:, 5 + b // 4, P * (b % 4):P * (b % 4) + P], nat_c[:, b, 0:2, :].rearrange("g a p -> g (a p)"), ident[:, :])
            ins.then_inc(s5_nat, 1)
            for b in range(NB // 2):
                ins = tr(PS[:, 7, P * b:P * b + P], nat_c[:, b, 1:3, :].rearrange("g a p -> g (a p)"), ident[:, :])
            ins.then_inc(s5_nat, 1)
            pe.wait_ge(s5_nat_sb, 2)
            for b in range(NB // 2):
                ins = tr(PS[:, 1, P * b:P * b + P], nat_c[:, NB // 2 + b, 1:3, :].rearrange("g a p -> g (a p)"), ident[:, :])
            ins.then_inc(s5_nat, 1)
            tr(PS[:, 0, 0:len(GAINS) * KT], gain_rows[:, :], ident[0:len(GAINS) * KT, 0:len(GAINS) * KT]).then_inc(gains_t, 1)
            pe.wait_ge(s5_u, CH)
            pe.wait_ge(s5_nat_sb, 6)
            pe.wait_ge(gains_sb, 1)
            for q in range(8):
                for g in range(GB):
                    ins = tr(PS[:, q, NC * g:NC * g + NC], u[:, GB * q + g, :, :].rearrange("p t h -> p (t h)"), id64)
                ins.then_inc(s5_ut, 1)
            pe.wait_ge(s5_ut_sb, 8)

            def s5_out(b):
                pe.wait_ge(s5_cz, b + 1)
                pe.wait_ge(s5_outb, b + 1)
                pe.wait_ge(s5_taps, 16 * CH * (b + 1))
                if b >= 1:
                    pe.wait_ge(s5_ysum, b)
                for g in range(GB):
                    o = PS[0:NC, 6 + g // 4, P * (g % 4):P * (g % 4) + P]
                    mm(o, uT[:, GB * b + g, :], taps[:, g, :, :].rearrange("p t h -> p (t h)"), start=True, stop=False)
                    mm(o, cz[:, g, :], out_a[b % 2][:, g, 1:CH + 1, :].rearrange("p t h -> p (t h)"), start=False, stop=False)
                    ins = mm(o, sz[:, g, :], out_b[:, g, :, :].rearrange("p t h -> p (t h)"), start=False, stop=True)
                ins.then_inc(s5_y, 1)

            def s5_maps(b):
                pe.wait_ge(s5_inw, b + 1)
                if b >= 1:
                    pe.wait_ge(s5_int_sb, b)
                for g in range(GB):
                    ins = tr(PS[:, 2 + g // 4, P * (g % 4):P * (g % 4) + P], in_w[:, g, :, :].rearrange("p s h -> p (s h)"), ident[:, :])
                ins.then_inc(s5_int, 1)
                pe.wait_ge(s5_outa, b + 1)
                if b >= 1:
                    pe.wait_ge(s5_lag_sb, b)
                for g in range(GB):
                    ins = mm(PS[0:GH, g // 4, P * (g % 4):P * (g % 4) + P], b_n[:, GB * b + g, :],
                             out_a[b % 2][:, g, 0:CH, :].rearrange("p t h -> p (t h)"), start=True, stop=True)
                ins.then_inc(s5_lag, 1)

            def s5_in(b):
                pe.wait_ge(s5_int_sb, b + 1)
                if b >= 1:
                    pe.wait_ge(s5_rot, b)
                for g in range(GB):
                    mm(PS[:, 4, NC * g:NC * g + NC], in_t[:, g, :, :].rearrange("p r q -> p (r q)"), uT[:, GB * b + g, :], start=True, stop=True)
                    ins = mm(PS[:, 5, NC * g:NC * g + NC], in_s[:, g, :, :].rearrange("p r q -> p (r q)"), uT[:, GB * b + g, :], start=True, stop=True)
                ins.then_inc(s5_v, 1)

            s5_maps(0)
            s5_in(0)
            for b in range(NB):
                if b + 1 < NB:
                    s5_maps(b + 1)
                s5_out(b)
                if b + 1 < NB:
                    s5_in(b + 1)
            for b in range(NB):
                pe.wait_ge(s5_gelu, b + 1)
                if b >= 4:
                    pe.wait_ge(x_lo_done, b - 3)
                for s in range(CH):
                    ins = tr(PS[:, b % 4, NC * s:NC * s + NC], y[:, b, s, :], id64)
                ins.then_inc(turned, 1)

            def three(o, wgt_hi, wgt_lo, x_hi, x_lo, weights_stay, first, last):
                for n, (a, c) in enumerate(((wgt_hi, x_hi), (wgt_lo, x_hi), (wgt_hi, x_lo))):
                    ins = mm(o, a if weights_stay else c, c if weights_stay else a,
                             start=first and n == 0, stop=last and n == 2)
                return ins

            def n_slot(g, par, ni, ks, hi, lo, first, last, n=512, tbs=TB, inc=1):
                pe.wait_ge(w_split, g + 1)
                for tb in range(tbs):
                    if first:
                        pe.wait_ge(n_free, ni * TB + (tb + 1))
                    for j, k in enumerate(ks):
                        cols = slice(n * j, n * j + n)
                        ins = three(PS[:, 4 + tb, 0:n], w_hi[:, par, cols], w_lo[:, par, cols],
                                    hi[:, k, P * tb:P * tb + P], lo[:, k, P * tb:P * tb + P], False,
                                    first and j == 0, last and j == len(ks) - 1)
                    if tb == tbs - 1:
                        ins.then_inc(w_used, 1)
                    elif last:
                        ins.then_inc(n_ready, inc)

            def t_slot(g, par, ti, pair, hi, lo, width=S, step=(2 * P, P), turns=None):
                pe.wait_ge(w_split, g + 1)
                pe.wait_ge(t_free, ti + 1)
                for t in range(2):
                    for k in range(KT):
                        if turns is not None and t == 0:
                            pe.wait_ge(x_lo_done, turns - KT + k + 1)
                        at = step[0] * k + step[1] * t
                        cols = slice(at, at + P)
                        ins = three(PS[:, 2 * pair + t, 0:width], w_hi[:, par, cols], w_lo[:, par, cols],
                                    hi[:, k, 0:width], lo[:, k, 0:width], True, k == 0, k == KT - 1)
                    ins.then_inc(w_used if t else t_first, 1)

            def turn_rows(j0, n, src, tbs=TB):
                for k in range(n):
                    if k >= 4:
                        pe.wait_ge(x_lo_done, j0 + k - 3)
                    for tb in range(tbs):
                        ins = tr(PS[:, k % 4, P * tb:P * tb + P], src[:, tb, P * k:P * k + P], ident[:, :])
                    ins.then_inc(turned, 1)

            pe.wait_ge(x_lo_done, KT)
            for j in range(4):
                for k in range(2):
                    g = GLU_SLOT + 2 * j + k
                    n_slot(g, g % 2, GLU_PANEL + j, range(4 * k, 4 * k + 4), xT_hi, xT_lo, k == 0, k == 1)
            def turn_normed(n, j0):
                def turn(k, tb):
                    ins = mm(PS[:, k, P * tb:P * tb + P], x_res[:, tb, P * k:P * k + P], diag[:, tb, :], start=True, stop=True)
                    if tb == TB - 1:
                        ins.then_inc(turned, 1)

                for tb in range(TB):
                    pe.wait_ge(row_norm, TB * n + tb + 1)
                    for k in range(4):
                        turn(k, tb)
                    if tb == TB - 2:
                        for k in range(4, 7):
                            for t in range(TB - 1):
                                turn(k, t)
                for k in range(4, 7):
                    turn(k, TB - 1)
                for t in range(TB):
                    turn(7, t)

            turn_normed(0, KT)

            def ffn_pe(layer, turns):
                g0, t0, h0 = FFN_SLOT[layer], FFN_TILE[layer], FFN_HID[layer]
                with pe.Fori(0, FT // 2) as i:
                    for j in range(2):
                        t_slot(i * 2 + (g0 + j), (g0 + j) % 2, i * 2 + (t0 + j), (t0 + j) % 2, xT_hi, xT_lo,
                               turns=(turns, None)[j])
                g0 += FT
                m = len(FFN_DOWN)
                with pe.Fori(0, 2) as i:
                    k = 0
                    for j, n in enumerate(FFN_DOWN):
                        pe.wait_ge(hid_done, h0 + k + n + 2)
                        n_slot(i * m + (g0 + j), (g0 + j) % 2, i + FFN_PANEL[layer], range(k, k + n), hT_hi, hT_lo,
                               j == 0, j == m - 1)
                        k += n

            ffn_pe(0, 2 * KT)
            turn_normed(1, 2 * KT)
            pe.wait_ge(x_lo_done, 3 * KT)

            def panel(g0, ni, n=512):
                for k in range(2):
                    n_slot(g0 + k, (g0 + k) % 2, ni, range(4 * k, 4 * k + 4), xT_hi, xT_lo, k == 0, k == 1, n)

            def turn_heads(pi):
                pe.wait_ge(head_done, TB * (pi + 1))
                for j in range(4):
                    if pi >= 1:
                        pe.wait_ge(head_t_sb, 4 * (pi - 1) + j + 1)
                    for tb in range(TB):
                        ins = tr(PS[:, j, P * tb:P * tb + P], stage[:, pi % 2, tb, P * j:P * j + P], ident[:, :])
                    ins.then_inc(head_t, 1)

            g = DSA_SLOT
            panel(g, DSA_PANEL)
            n_slot(g + 2, (g + 2) % 2, DSA_PANEL + 1, range(KT), xT_hi, xT_lo, True, True, DSA_W - 3 * D - 512)
            panel(g + 3, DSA_PANEL + 2)
            turn_heads(0)
            pe.wait_ge(ki_done, 3)
            for head in range(2):
                pe.wait_ge(head_t_sb, head + 1)
                for tb in range(TB):
                    ins = tr(PS[:, head, P * tb:P * tb + P],
                             ki_st[:, tb, 1 - head:3 - head, :].rearrange("p a d -> p (a d)"), ident[:, :])
                ins.then_inc(ki_t, 1)
            pe.wait_ge(head_t_sb, 4)
            pe.wait_ge(ki_t_sb, 2)
            for e in range(3 * NI):
                b, h = e // NI + 1, e % NI
                if e >= 4:
                    pe.wait_ge(idx_relu, e - 3)
                mm(PS[:, e % 4, 0:P * (b + 1)], qiT[:, h // 2, P * b:P * b + P], kiT[h % 2][:, 0:P * (b + 1)],
                   start=True, stop=True).then_inc(idx_dot, 1)
            for j in range(1, 6):
                panel(g + 3 + 2 * j, DSA_PANEL + 2 + j)
                if j == 1:
                    pe.wait_ge(idx_relu, 3 * NI)
                if j < 5:
                    turn_heads(j)

            def attend_pe(units, u0):
                n = len(units)
                for t in range(n + 3):
                    if t < n:
                        k = units[t][1]
                        pe.wait_ge(q_padded, u0 + t + 1)
                        if t >= 3:
                            pe.wait_ge(at_logit, u0 + t - 2)
                        mm(PS[:, t % 3, 0:k.shape[1]], q_pad[:, (u0 + t) % 4, :], k, start=True, stop=True).then_inc(at_dot, 1)
                    e = t - 2
                    if 0 <= e < n:
                        pe.wait_ge(at_prob, u0 + e + 1)
                        if e >= 2:
                            pe.wait_ge(at_turn_sb, u0 + e - 1)
                        for j in range(len(units[e][3])):
                            ins = tr(PS[:, 3 + e % 2, P * j:P * j + P], logit[:, e % 3, P * j:P * j + P], ident[:, :])
                        ins.then_inc(at_turn, 1)
                    e = t - 3
                    if e >= 0:
                        v = units[e][3]
                        pe.wait_ge(at_turn_sb, u0 + e + 1)
                        if e >= 2:
                            pe.wait_ge(at_out, u0 + e - 1)
                        for j in range(len(v)):
                            ins = mm(PS[:, 5 + e % 2, 0:P], probT[:, e % 2, P * j:P * j + P], v[j],
                                     start=j == 0, stop=j == len(v) - 1)
                        ins.then_inc(at_pv, 1)

            pe.wait_ge(head_t_sb, 20)
            pe.wait_ge(n_free, TB * (DSA_PANEL + 9))
            pe.wait_ge(idx_chosen, 3)
            attend_pe(dsa_units, DSA_UNIT)
            pe.wait_ge(at_out, SOFT_UNIT)
            turn_rows(3 * KT, KT, o_nat)
            pe.wait_ge(x_lo_done, 4 * KT)
            for j in range(2):
                panel(WO_SLOT + 2 * j, WO_PANEL + j)
            turn_normed(2, 4 * KT)
            ffn_pe(1, 5 * KT)

            turn_normed(3, 5 * KT)
            for j in range(8):
                g = HIN_SLOT + j
                t_slot(g, g % 2, HIN_TILE + j, (HIN_TILE + j) % 2, xT_hi, xT_lo, step=(192, 64) if j == 5 else (256, P),
                       turns=None if j else 6 * KT)
                if j == 0:
                    pe.wait_ge(ld_bias, 48)
                    mm(PS[0:NREL, 4, :], table[:, :], basis[:, 0:512], start=True, stop=True)
                    mm(PS[0:NREL, 5, 0:BIAS_W - 512], table[:, :], basis[:, 512:BIAS_W], start=True, stop=True).then_inc(bias_row, 1)
            pe.wait_ge(bias_row_sb, 1)
            panel(HIN_SLOT + 8, HIN_PANEL)
            panel(HIN_SLOT + 10, HIN_PANEL + 1, 384)
            pe.wait_ge(t_free, HIN_TILE + 10)
            pe.wait_ge(n_free, TB * (HIN_PANEL + 3))
            attend_pe(soft_units, SOFT_UNIT)
            attend_pe(stick_units, STICK_UNIT)
            pe.wait_ge(mem_norm, 2)
            turn_rows(6 * KT, KT, mem, 2)
            pe.wait_ge(x_lo_done, 7 * KT)
            t_slot(MEM_SLOT, MEM_SLOT % 2, MEM_TILE, MEM_TILE % 2, memT_hi, memT_lo, MEM)
            pe.wait_ge(at_out, MEM_UNIT)
            n_slot(MEM_SLOT + 1, (MEM_SLOT + 1) % 2, MEM_PANEL, range(KT), memT_hi, memT_lo, True, True, 256, 2, 3)
            pe.wait_ge(t_free, MEM_TILE + 3)
            pe.wait_ge(grp_norm, TB)
            turn_rows(7 * KT, KT, o_nat)
            pe.wait_ge(x_lo_done, 8 * KT)
            for j in range(2):
                panel(HOUT_SLOT + 2 * j, HOUT_PANEL + j)

            turn_normed(4, 8 * KT)
            pe.wait_ge(x_lo_done, 9 * KT)
            t_slot(XQ_SLOT, XQ_SLOT % 2, XQ_TILE, XQ_TILE % 2, xT_hi, xT_lo)
            pe.wait_ge(t_free, XQ_TILE + 3)
            pe.wait_ge(n_free, TB * (MEM_PANEL + 2))
            attend_pe(mem_units, MEM_UNIT)
            pe.wait_ge(at_out, MEM_UNIT + 16)
            turn_rows(9 * KT, 2, ox)
            pe.wait_ge(x_lo_done, 9 * KT + 2)
            par = XO_SLOT % 2
            pe.wait_ge(w_split, XO_SLOT + 1)
            for j in range(2):
                for tb in range(TB):
                    pe.wait_ge(n_free, TB * (XO_PANEL + j) + tb + 1)
                    for k in range(2):
                        cols = slice(D * k + 512 * j, D * k + 512 * j + 512)
                        ins = three(PS[:, 4 + tb, :], w_hi[:, par, cols], w_lo[:, par, cols],
                                    xT_hi[:, k, P * tb:P * tb + P], xT_lo[:, k, P * tb:P * tb + P], False, k == 0, k == 1)
                    ins.then_inc(w_used if j == 1 and tb == TB - 1 else n_ready, 1)

            turn_normed(5, 9 * KT + 2)
            for part in range(MLP_PARTS):
                g0, t0, h0 = MLP_SLOT[part], MLP_TILE[part], MLP_HID[part]
                with pe.Fori(0, MT // 4) as i:
                    for j in range(2):
                        t_slot(i * 2 + (g0 + j), (g0 + j) % 2, i * 2 + (t0 + j), (t0 + j) % 2, xT_hi, xT_lo,
                               turns=None if part or j else 10 * KT + 2)
                g0 += MT // 2
                m = MT // 4
                with pe.Fori(0, 2) as i:
                    for j in range(m):
                        pe.wait_ge(hid_done, h0 + 2 * j + 4)
                        n_slot(i * m + (g0 + j), (g0 + j) % 2, i + MLP_PANEL[part], range(4 * j, 4 * j + 4), hT_hi, hT_lo,
                               j == 0, j == m - 1)


def chunk_view(o, i):
    return o.rearrange("p (c s) -> p s c", s=CH), i.rearrange("p (s c) -> p s c", s=CH)


_INS = ["x", "s5_lambda_re", "s5_lambda_im", "s5_log_dt", "s5_b_re", "s5_b_im", "s5_c_re", "s5_c_im", "s5_d", "s5_w_glu",
        "dsa_w_in", "dsa_q_norm", "dsa_k_norm", "dsa_w_o", "ffn_w_gate_up", "ffn_w_down", "norm_mix", "norm_ffn",
        "mem_2", "rel_table_2", "g_mix_2", "w_in_2", "g_group_2", "sinks_2", "w_out_2", "g_cross_2", "g_mem_2",
        "w_xq_2", "w_xkv_2", "w_xo_2", "g_mlp_2", "w_up_2", "w_down_2", "g_final_2"]


def kernel(**inputs):
    import concourse.bacc as bacc
    from concourse.bass_utils import run_bass_kernel_spmd

    nc = bacc.Bacc("TRN2", target_bir_lowering=False, num_devices=1)
    arrays, w = {}, {}
    for name, value in {**{n: inputs[n] for n in _INS}, **shape_constants()}.items():
        a = np.ascontiguousarray(value)
        if name in ("x", "mem_2"):
            a = a[0]
        arrays[f"in_{name}"] = a
        w[name] = nc.dram_tensor(f"in_{name}", a.shape, mybir.dt.from_np(a.dtype), kind="ExternalInput").ap()
    out = nc.dram_tensor("out_x", (S, D), F32, kind="ExternalOutput").ap()
    program(nc, w, out)
    r = run_bass_kernel_spmd(nc, [arrays], core_ids=[0])
    return r.results[0]["out_x"][None]
```

```python
from contextlib import ExitStack

import numpy as np

import concourse.bass as bass
from concourse import mybir

F32 = mybir.dt.float32
F32R = mybir.dt.float32r
I32 = mybir.dt.int32
ALU = mybir.AluOpType
ACT = mybir.ActivationFunctionType
AX = mybir.AxisListType

P = 128
S = 512
D = 1024
TB = S // P
KT = D // P
EPS = 1e-6
NEG = -1e30

G, GH, GP = 64, 16, 64
CH = P // GH
NC = S // CH
GB = P // GH
NB = G // GB
POOL_TABLES = NB // 2

HD = 64
NH = 16
NI = 8
TOPK = min(256, S // 4)
ROUNDS = TOPK // 8
DSA_W = 3 * D + NI * HD + HD + NI

FF = 2816
FT = FF // P
FF2 = 4096
MLP_PARTS = 2
MT = FF2 // P // MLP_PARTS

MEM = 256
NREL = 12
BUCKETS = 32
BIAS_W = S + P - 1

SLOT = 2048

GAINS = ["norm_mix0", "norm_mix1", "norm_ffn0", "norm_ffn1", "g_mix", "g_cross", "g_mem", "g_mlp", "g_group"]


def shape_constants():
    f = np.float32
    row, col = np.arange(P)[:, None], np.arange(P)[None, :]
    masks = np.stack([np.where(col <= row, 0, NEG), col >= row, col < row], 1).astype(f)
    inv = f(10000.0) ** (-np.arange(0, HD, 2, dtype=f) / f(HD))
    ang = np.arange(S, dtype=f)[:, None] * inv[None, :]
    cos, sin = np.cos(ang).astype(f), np.sin(ang).astype(f)
    rope = np.stack([np.concatenate([cos, cos], 1), np.concatenate([-sin, sin], 1)])
    rope = np.ascontiguousarray(rope.reshape(2, TB, P, HD).transpose(2, 0, 1, 3))
    dist = np.arange(BIAS_W) - (P - 1)
    n = np.maximum(dist, 0)
    big = 16 + (np.log(np.maximum(n, 1).astype(f) / f(16)) / f(np.log(128.0)) * f(16)).astype(np.int32)
    bucket = np.where(n < 16, n, np.minimum(big, BUCKETS - 1))
    times = np.where(dist >= 0, (n <= 128).astype(int) + (n % 4 == 0) + (n % 16 == 0), 0)
    basis = np.zeros((BUCKETS + 3, BIAS_W), f)
    basis[bucket, np.arange(BIAS_W)] = 1
    basis[BUCKETS] = np.where(times > 0, np.log(np.maximum(times, 1)), NEG)
    basis[BUCKETS + 1] = np.where((dist >= 0) & (dist < 128), 0, NEG)
    basis[BUCKETS + 2] = np.where(dist >= 0, 0, NEG)
    pick = np.zeros((3, NREL), f)
    pick[np.arange(NREL) // 4, np.arange(NREL)] = 1
    sign = np.where(np.arange(P) < GP, 1, -1).astype(f)[:, None]
    return {
        "c_ident": np.eye(P, dtype=f), "c_masks": masks, "c_rope": rope, "c_basis": basis, "c_pick": pick,
        "c_sign": sign,
    }


GLU_SLOT, GLU_SLOTS = 0, 8
FFN_SLOT = [8, 61]
FFN_DOWN = [4, 4, 4, 4, 4, 2]
DSA_SLOT = 42
WO_SLOT = 57
HIN_SLOT = 95
MEM_SLOT = 107
HOUT_SLOT = 109
XQ_SLOT = 113
XO_SLOT = 114
MLP_SLOT = [115, 131]
SLOTS = 147
FFN_TILE, HIN_TILE, MEM_TILE, XQ_TILE, MLP_TILE = [0, 22], 44, 52, 53, [54, 62]
GLU_PANEL, FFN_PANEL, DSA_PANEL, WO_PANEL, HIN_PANEL = 0, [4, 16], 6, 14, 18
MEM_PANEL, HOUT_PANEL, XO_PANEL, MLP_PANEL = 20, 21, 23, [25, 27]
FFN_HID, MLP_HID = [0, 22], [44, 52]




def program(nc, w, out):
    with ExitStack() as ctx:
        def sem(name):
            return ctx.enter_context(nc.semaphore(name))

        def fixed(name, shape, dt=F32):
            return ctx.enter_context(nc.sbuf_tensor(name, shape, dt))

        x_res = fixed("x_res", [P, TB, D])
        xT_hi = fixed("xT_hi", [P, KT, S], F32R)
        xT_lo = fixed("xT_lo", [P, KT, S], F32R)
        raw = fixed("raw", [P, 2, SLOT])
        w_hi = fixed("w_hi", [P, 2, SLOT], F32R)
        w_lo = fixed("w_lo", [P, 2, SLOT], F32R)
        arena = fixed("arena", [P, 2 * FT * S])
        spare = fixed("spare", [P, 3072])
        ident = fixed("ident", [P, P])
        masks = fixed("masks", [P, 3, P])
        sign = fixed("sign", [P, 1])
        gain_rows = fixed("gain_rows", [len(GAINS) * KT, P])
        gains = fixed("gains", [P, len(GAINS) * KT])
        half_neg = fixed("half_neg", [P, 64])
        minus_one = fixed("minus_one", [P, 1])
        half_mask = fixed("half_mask", [P, 2])
        one = fixed("one", [P, 1])
        ssq = fixed("ssq", [P, 64])
        rstd = fixed("rstd", [P, 64])
        r8 = fixed("r8", [P, G])
        neg_max = fixed("neg_max", [P, 4])
        row_sum = fixed("row_sum", [P, 4])
        inv_sum = fixed("inv_sum", [P, 4])
        sinks = fixed("sinks", [P, 4])
        sinks_neg = fixed("sinks_neg", [P, 4])
        rope = fixed("rope", [P, 2, TB, HD])
        rope_q = fixed("rope_q", [P, 2, TB, HD])
        rope_k = fixed("rope_k", [P, 2, TB, HD])
        gain_qk = fixed("gain_qk", [P, 2, HD])
        head_ss = fixed("head_ss", [P, 3, 8])
        head_rs = fixed("head_rs", [P, 3, 8])
        w_idx = fixed("w_idx", [P, TB, NI])
        top = fixed("top", [P, 8])
        above = fixed("above", [P, 1])
        sink_e = fixed("sink_e", [P, 4])
        PS = ctx.enter_context(nc.psum_tensor("PS", [P, 8, 512], F32))

        KB = 1024
        region_at = {n: nc.lookup_mloc(t).addr for n, t in (
            ("arena", arena), ("spare", spare), ("x_hi", xT_hi), ("x_lo", xT_lo), ("w_hi", w_hi), ("w_lo", w_lo), ("raw", raw),
            ("x_res", x_res), ("rope_q", rope_q), ("rope_k", rope_k))}

        def place(name, where, at, shape, dt=F32):
            return nc.alloc_sbuf_tensor_at(name, shape, dt, offset=region_at[where] + at)

        u = place("u", "arena", 0, [NC, G, CH, GH])
        y = place("y", "arena", 0, [NC, NB, CH, P])
        xp = place("xp", "arena", 32 * KB, [NC, CH, D])
        tab_c = place("tab_c", "arena", 32 * KB, [P, G, NC])
        tab_s = place("tab_s", "arena", 48 * KB, [P, G, NC])
        b_n = place("b_n", "arena", 64 * KB, [P, G, GH])
        b_s = place("b_s", "arena", 68 * KB, [P, G, GH])
        c_n = place("c_n", "arena", 72 * KB, [P, G, GH])
        c_s = place("c_s", "arena", 76 * KB, [P, G, GH])
        decay = place("decay", "arena", 80 * KB, [P, GB, NC])
        tmp_b = place("tmp_b", "arena", 82 * KB, [P, GB, CH, GH])
        pw_r = place("pw_r", "spare", 0, [P, G, CH + 1])
        pw_i = place("pw_i", "spare", 2304, [P, G, CH + 1])
        pw_rs = place("pw_rs", "spare", 4608, [P, G, CH + 1])
        pw_is = place("pw_is", "spare", 6912, [P, G, CH + 1])
        uT = place("uT", "x_hi", 0, [P, G, NC])
        nat_b = place("nat_b", "x_lo", 0, [G, 3, GP, GH])
        nat_c = place("nat_c", "x_hi", 0, [P, NB, 3, GP])
        nat_l = place("nat_l", "x_lo", 12 * KB, [G, 2, 2, GP])
        out_a = [place("out_a0", "x_lo", 0, [P, GB, CH + 1, GH]), place("out_a1", "x_res", 8704, [P, GB, CH + 1, GH]),
                 place("out_a2", "raw", 8 * KB, [P, GB, CH + 1, GH])]
        out_b = place("out_b", "w_lo", 12 * KB, [P, GB, CH, GH])
        in_w = place("in_w", "x_lo", 4608, [P, GB, CH, GH])
        small = place("small", "w_hi", 0, [P, 32, G])
        in_t = place("in_t", "w_hi", 0, [P, GB, 2, GP])
        in_s = place("in_s", "w_hi", 4 * KB, [P, GB, 2, GP])
        taps = place("taps", "w_hi", 8 * KB, [P, GB, CH, GH])
        lag = place("lag", "w_hi", 12 * KB, [GH, GB, CH, GH])
        bar = place("bar", "w_lo", 0, [P, 2, G, GH])
        prod1 = place("prod1", "w_lo", 0, [P, G, NC // 4])
        prod2 = place("prod2", "w_lo", 4 * KB, [P, G, NC // 4])
        part1 = place("part1", "w_lo", 0, [P, GB, NC // 2])
        part2 = place("part2", "w_lo", 4 * KB, [P, GB, NC // 2])
        spin_p = place("spin_p", "spare", 9216, [P, 6, G])
        half_p = [place("half_p0", "arena", 82 * KB, [P, G * NC // 8]), place("half_p1", "arena", 84 * KB, [P, G * NC // 8])]
        spin = place("spin", "rope_q", 0, [P, 6, G])
        v1 = place("v1", "w_lo", 0, [P, GB, NC])
        v2 = place("v2", "w_lo", 2 * KB, [P, GB, NC])
        glu_sg = place("glu_sg", "spare", 0, [P, 2, 256])
        glu_v = place("glu_v", "spare", 2 * KB, [P, 2, 256])
        z = place("z", "w_lo", 4 * KB, [P, GB, NC])
        cz = place("cz", "w_lo", 8 * KB, [P, GB, NC])
        sz = place("sz", "w_lo", 10 * KB, [P, GB, NC])
        skip = place("skip", "x_res", 0, [GH, G, GH])
        junk = place("junk", "x_res", 4 * KB, [NC, D])
        g_row = place("g_row", "x_res", 8 * KB, [NC, D])
        tmp_a = place("tmp_a", "x_res", 4 * KB, [P, GB, CH + 1, GH])

        diag = place("diag", "rope_q", 0, [P, TB, P])
        x_out = place("x_out", "x_lo", 0, [P, TB, D])
        hT_hi = place("hT_hi", "arena", 0, [P, FT, S], F32R)
        hT_lo = place("hT_lo", "arena", FT * S * 4, [P, FT, S], F32R)
        gbuf = place("gbuf", "spare", 0, [P, 2, 2, 512])
        sq_junk = place("sq_junk", "spare", 8 * KB, [P, D])

        stage = place("stage", "arena", 0, [P, 2, TB, 512])
        o_nat = place("o_nat", "arena", 0, [P, TB, D])
        qT = place("qT", "arena", 16 * KB, [P, KT, S])
        kT = place("kT", "arena", 32 * KB, [P, KT, S])
        v_dsa = place("v_dsa", "arena", 48 * KB, [P, TB, D])
        qiT = place("qiT", "arena", 64 * KB, [P, NI // 2, S])
        kiT = [place("kiT0", "arena", 72 * KB, [P, S]), place("kiT1", "arena", 48 * KB, [P, S])]
        head_n = place("head_n", "arena", 74 * KB, [P, 3, 512])
        head_sq = place("head_sq", "arena", 80 * KB, [P, 2, 512])
        head_c = place("head_c", "arena", 84 * KB, [P, 2, 512])
        ki_raw = place("ki_raw", "spare", 0, [P, TB, HD + NI])
        relu_i = place("relu_i", "spare", 2 * KB, [P, 2, 512])
        ki_n = place("ki_n", "spare", 8 * KB, [P, TB, HD])
        ki_c = place("ki_c", "spare", 1152, [P, TB, HD])
        ki_st = place("ki_st", "spare", 9 * KB, [P, TB, 3, HD])
        BLK = [0, 0, 2 * P, 5 * P]
        score = place("score", "spare", 6 * KB, [P, 9 * P])
        ranked = place("ranked", "arena", 64 * KB, [P, 9 * P])
        chosen = place("chosen", "arena", 64 * KB + 36 * P, [P, 9 * P])
        equal = place("equal", "spare", 2 * KB, [P, 512])
        seen = place("seen", "spare", 4 * KB, [P, 512])
        score3 = place("score3", "arena", 74 * KB, [P, 512])
        equal3 = place("equal3", "arena", 76 * KB, [P, 512])
        seen3 = place("seen3", "arena", 78 * KB, [P, 512])
        q_pad = place("q_pad", "rope_k", 0, [P, 4, P])
        logit = place("logit", "spare", 0, [P, 3, 512])
        probT = place("probT", "spare", 6 * KB, [P, 2, 512])
        stay = [place("stay0", "spare", 10 * KB, [P, 512]), place("stay1", "arena", 86 * KB, [P, 512])]
        hqk = place("hqk", "arena", 16 * KB, [P, 16, S])
        v_ab = place("v_ab", "arena", 48 * KB, [P, TB, 512])
        v_cd = place("v_cd", "arena", 56 * KB, [P, TB, 384])
        bias = place("bias", "arena", 62 * KB, [P, NREL, S])
        basis = place("basis", "spare", 0, [BUCKETS + 3, BIAS_W])
        table = place("table", "spare", 3 * KB, [BUCKETS + 3, NREL])
        bias_v = place("bias_v", "spare", 4 * KB, [NREL, BIAS_W])
        bias_dram = nc.dram_tensor("bias_dram", (NREL, BIAS_W), F32, kind="Internal").ap()
        mem = place("mem", "x_hi", 8 * KB, [P, 2, D])
        memT_hi = place("memT_hi", "x_hi", 0, [P, KT, MEM], F32R)
        memT_lo = place("memT_lo", "x_lo", 0, [P, KT, MEM], F32R)
        kxT = place("kxT", "arena", 62 * KB, [P, 2, MEM])
        vx = place("vx", "arena", 64 * KB, [P, 2, MEM])
        qxT = place("qxT", "arena", 66 * KB, [P, 2, S])
        late_junk = place("late_junk", "arena", 72 * KB, [P, D])
        ox = place("ox", "arena", 48 * KB, [P, TB, 256])
        g_last = place("g_last", "arena", 78 * KB, [P, D])

        w_raw = [sem("w_raw0"), sem("w_raw1")]
        w_rounded, w_split, w_used = sem("w_rounded"), sem("w_split"), sem("w_used")
        t_free, t_first = sem("t_free"), sem("t_first")
        n_free, n_ready = sem("n_free"), sem("n_ready")
        hid_act, hid_hi, hid_done = sem("hid_act"), sem("hid_hi"), sem("hid_done")
        row_sq, row_rstd, row_mean, row_norm = sem("row_sq"), sem("row_rstd"), sem("row_mean"), sem("row_norm")
        turned, x_hi_done, x_lo_done = sem("turned"), sem("x_hi_done"), sem("x_lo_done")
        glu_sig, glu_done = sem("glu_sig"), sem("glu_done")
        v_step, a_step, p_step = sem("v_step"), sem("a_step"), sem("p_step")
        ld_x, ld_lam, ld_par, ld_rows, ld_const, ld_late, ld_res, stored = (
            sem("ld_x"), sem("ld_lam"), sem("ld_par"), sem("ld_rows"), sem("ld_const"), sem("ld_late"), sem("ld_res"), sem("stored"))
        s5_q, s5_b_read, s5_bs_read, s5_bs, s5_scaled = (
            sem("s5_q"), sem("s5_b_read"), sem("s5_bs_read"), sem("s5_bs"), sem("s5_scaled"))
        const_set = sem("const_set")
        s5_sq, s5_rstd, s5_u, s5_ut, s5_ut_sb = sem("s5_sq"), sem("s5_rstd"), sem("s5_u"), sem("s5_ut"), sem("s5_ut_sb")
        s5_nat, s5_nat_sb, s5_ang, s5_sin = sem("s5_nat"), sem("s5_nat_sb"), sem("s5_ang"), sem("s5_sin")
        s5_par, s5_outa, s5_outb, s5_inw, s5_dec, s5_skip = sem("s5_par"), sem("s5_outa"), sem("s5_outb"), sem("s5_inw"), sem("s5_dec"), sem("s5_skip")
        s5_step, s5_spin, s5_tab, s5_half = sem("s5_step"), sem("s5_spin"), sem("s5_tab"), sem("s5_half")
        s5_lag, s5_lag_sb, s5_taps, s5_zero = sem("s5_lag"), sem("s5_lag_sb"), sem("s5_taps"), sem("s5_zero")
        s5_int, s5_int_sb, s5_v, s5_rot, s5_cz, s5_y, s5_gelu = (
            sem("s5_int"), sem("s5_int_sb"), sem("s5_v"), sem("s5_rot"), sem("s5_cz"), sem("s5_y"), sem("s5_gelu"))
        x_final = sem("x_final")
        ld_qk, qk_tables = sem("ld_qk"), sem("qk_tables")
        head_sq_done, head_sum, head_rstd, head_norm, head_sin, head_cos, head_done = (
            sem("head_sq_done"), sem("head_sum"), sem("head_rstd"), sem("head_norm"), sem("head_sin"), sem("head_cos"), sem("head_done"))
        head_t, head_t_sb = sem("head_t"), sem("head_t_sb")
        ki_squared = sem("ki_squared")
        ki_sq, ki_rs, ki_done, ki_t, ki_t_sb = sem("ki_sq"), sem("ki_rs"), sem("ki_done"), sem("ki_t"), sem("ki_t_sb")
        idx_dot, idx_relu, idx_sum, idx_chosen = sem("idx_dot"), sem("idx_relu"), sem("idx_sum"), sem("idx_chosen")
        q_padded, at_dot, at_logit, at_max, at_prob, at_turn, at_turn_sb, at_pv, at_inv, at_out = (
            sem("q_padded"), sem("at_dot"), sem("at_logit"), sem("at_max"), sem("at_prob"), sem("at_turn"),
            sem("at_turn_sb"), sem("at_pv"), sem("at_inv"), sem("at_out"))
        ld_bias, bias_row, bias_row_sb, bias_out, ld_bias_t = (
            sem("ld_bias"), sem("bias_row"), sem("bias_row_sb"), sem("bias_out"), sem("ld_bias_t"))
        grp_sq, grp_rstd, grp_norm = sem("grp_sq"), sem("grp_rstd"), sem("grp_norm")
        ld_mem, mem_sq, mem_rstd, mem_norm, ld_last = sem("ld_mem"), sem("mem_sq"), sem("mem_rstd"), sem("mem_norm"), sem("ld_last")
        gains_t, gains_sb = sem("gains_t"), sem("gains_sb")

        block = ctx.enter_context(nc.Block())

        def f32(ap):
            return ap.bitcast(F32)

        dsa_units = []
        for b in range(TB):
            for h in range(NH):
                mask = masks[:, 0, :] if b == 0 else chosen[:, BLK[b]:BLK[b] + P * (b + 1)]
                dsa_units.append((qT[:, h // 2, P * b:P * b + P], kT[:, h // 2, 0:P * (b + 1)], mask,
                                  [v_dsa[:, k, P * (h // 2):P * (h // 2) + P] for k in range(b + 1)], h % 2,
                                  o_nat[:, b, HD * h:HD * h + HD], None))

        def hybrid_units(group):
            q_at, k_at, rel, v, v_at = {"a": (0, 2, 0, v_ab, 0), "b": (4, 6, None, v_ab, 256),
                                        "c": (8, 10, 4, v_cd, 0), "d": (12, 14, 8, v_cd, 128)}[group]
            units = []
            for b in range(TB):
                for h in range(4):
                    first = max(0, b - 1) if group == "c" else 0
                    k_tile = (0, 1, 1, 0)[h] if group == "c" else h // 2
                    v_head = h // 2 if group == "c" else h
                    v_cols = slice(v_at + P * (v_head // 2), v_at + P * (v_head // 2) + P)
                    o_at = 256 * "abcd".index(group) + HD * h
                    units.append((hqk[:, q_at + h // 2, P * b:P * b + P],
                                  hqk[:, k_at + k_tile, P * first:P * (b + 1)],
                                  None if rel is None else bias[:, rel + h, 0:P * (b + 1 - first)][:, ::-1],
                                  [v[:, k, v_cols] for k in range(first, b + 1)], v_head % 2,
                                  o_nat[:, b, o_at:o_at + HD], h if group == "c" else None))
            return units

        soft_units = hybrid_units("a") + hybrid_units("c") + hybrid_units("d")
        stick_units = hybrid_units("b")
        mem_units = [(qxT[:, h // 2, P * b:P * b + P], kxT[:, h // 2, :], None,
                      [vx[:, m, P * (h // 2):P * (h // 2) + P] for m in range(2)], h % 2,
                      ox[:, b, HD * h:HD * h + HD], None)
                     for b in range(TB) for h in range(4)]
        DSA_UNIT, SOFT_UNIT, STICK_UNIT, MEM_UNIT = 0, 64, 112, 128

        def head_copied(e):
            return TB * (DSA_PANEL + 1 + (e >= TB)) + e + 1

        @block.sync
        def _(sp):
            for j, name in ((0, "s5_lambda_re"), (1, "s5_lambda_im")):
                for half in range(2):
                    sp.dma_start(nat_l[:, j, half, :], w[name][0]).then_inc(ld_lam, 16)
            sp.dma_start(small[:, 0, :], w["s5_log_dt"][0:1, :].broadcast_to([P, G])).then_inc(ld_lam, 16)
            for j, name in ((0, "s5_b_re"), (1, "s5_b_im"), (2, "s5_b_re")):
                sp.dma_start(nat_b[:, j, :, :], w[name][0]).then_inc(ld_par, 16)
            for j, name in ((0, "s5_c_re"), (1, "s5_c_im"), (2, "s5_c_re")):
                sp.dma_start(nat_c[:, :, j, :], w[name][0].rearrange("(b g) h p -> (g h) b p", g=GB)).then_inc(ld_par, 16)
            sp.dma_start(g_row[:, :], w["norm_mix"][0:1, :].broadcast_to([NC, D])).then_inc(ld_rows, 16)
            sp.dma_start(skip[:, :, :].rearrange("p g h -> p (g h)"), w["s5_d"][0:1, :].broadcast_to([GH, D])).then_inc(ld_rows, 16)

            def slot_free(g):
                sp.wait_ge(w_split, g - 1)

            def put(par, dst, src):
                sp.dma_start(dst, src).then_inc(w_raw[par], 16)

            def load_pair(par, a, b, n):
                v = raw[:, par, 0:KT * 2 * n].rearrange("p (k t n) -> p k t n", t=2, n=n)
                put(par, v[:, :, 0, :], a)
                put(par, v[:, :, 1, :], b)

            def load_rows(par, src, n):
                m = src.shape[1]
                v = raw[:, par, 0:m * n].rearrange("p (k n) -> p k n", n=n)
                put(par, v[:, 0:m // 2, :], src[:, 0:m // 2, :])
                put(par, v[:, m // 2:m, :], src[:, m // 2:m, :])

            def tiles(ap):
                return ap.rearrange("(k p) n -> p k n", p=P)

            glu = tiles(w["s5_w_glu"][0])
            for j in range(4):
                for k in range(0, KT, 4):
                    g = GLU_SLOT + 2 * j + k // 4
                    if g >= 2:
                        slot_free(g)
                    v = raw[:, g % 2, :].rearrange("p (k t n) -> p k t n", t=2, n=256)
                    put(g % 2, v[:, :, 0, :], glu[:, k:k + 4, 256 * j:256 * j + 256])
                    put(g % 2, v[:, :, 1, :], glu[:, k:k + 4, D + 256 * j:D + 256 * j + 256])
                    if g == 0:
                        sp.wait_ge(s5_zero, 1)
                        for b in range(NB):
                            sp.wait_ge(s5_lag_sb, b + 1)
                            if b >= 1:
                                sp.wait_ge(s5_y, b)
                            for s in range(CH):
                                sp.dma_start(taps[GH * s:GH * s + GH, :, s:CH, :].rearrange("p g t h -> p g (t h)"),
                                             lag[:, :, 0:CH - s, :].rearrange("p g t h -> p g (t h)")).then_inc(s5_taps, 16)
                if j == 0:
                    sp.wait_ge(s5_gelu, NB)
                    sp.dma_start(x_res[:, :, :], w["x"].rearrange("(b p) d -> p b d", p=P)).then_inc(ld_res, 16)

            def ffn_loads(layer):
                up = tiles(w["ffn_w_gate_up"][layer])
                down = tiles(w["ffn_w_down"][layer])
                g0 = FFN_SLOT[layer]
                with sp.Fori(0, FT // 2) as i:
                    for j in range(2):
                        slot_free(i * 2 + (g0 + j))
                        v = raw[:, (g0 + j) % 2, :].rearrange("p (k t n) -> p k t n", t=2, n=P)
                        put((g0 + j) % 2, v[:, :, 0, :], up[:, :, bass.ds(i * (2 * P) + j * P, P)])
                        put((g0 + j) % 2, v[:, :, 1, :], up[:, :, bass.ds(i * (2 * P) + (FF + j * P), P)])
                g0 += FT
                with sp.Fori(0, 2) as i:
                    k = 0
                    for j, m in enumerate(FFN_DOWN):
                        slot_free(i * len(FFN_DOWN) + (g0 + j))
                        load_rows((g0 + j) % 2, down[:, k:k + m, bass.ds(i * 512, 512)], 512)
                        k += m

            ffn_loads(0)

            def panel_loads(g0, src, n, kt=KT):
                for k in range(0, kt, 4):
                    slot_free(g0 + k // 4)
                    load_rows((g0 + k // 4) % 2, src[:, k:k + 4, :], n)

            w_in = tiles(w["dsa_w_in"][0])
            panel_loads(DSA_SLOT, w_in[:, :, 3 * D:3 * D + 512], 512)
            slot_free(DSA_SLOT + 2)
            load_rows((DSA_SLOT + 2) % 2, w_in[:, :, 3 * D + 512:DSA_W], DSA_W - 3 * D - 512)
            for j in range(6):
                panel_loads(DSA_SLOT + 3 + 2 * j, w_in[:, :, 512 * j:512 * j + 512], 512)
            for j in range(2):
                panel_loads(WO_SLOT + 2 * j, tiles(w["dsa_w_o"][0])[:, :, 512 * j:512 * j + 512], 512)
            ffn_loads(1)

            sp.wait_ge(hid_done, FFN_HID[1] + FT + 2)
            sp.dma_start(basis[:, :], w["c_basis"]).then_inc(ld_bias, 16)
            sp.dma_start(table[0:BUCKETS, :], w["rel_table_2"]).then_inc(ld_bias, 16)
            sp.dma_start(table[BUCKETS:BUCKETS + 3, :], w["c_pick"]).then_inc(ld_bias, 16)
            w_h = tiles(w["w_in_2"][0])

            def h_slot(g, c):
                slot_free(g)
                load_pair(g % 2, w_h[:, :, c:c + P], w_h[:, :, c + P:c + 2 * P], P)

            h_slot(HIN_SLOT, 0)
            h_slot(HIN_SLOT + 1, 256)
            for j, c in enumerate((768, 1024, 1536)):
                h_slot(HIN_SLOT + 2 + j, c)
            g = HIN_SLOT + 5
            slot_free(g)
            v = raw[:, g % 2, 0:KT * 192].rearrange("p (k n) -> p k n", n=192)
            put(g % 2, v[:, :, 0:P], w_h[:, :, 1792:1920])
            put(g % 2, v[:, :, P:192], w_h[:, :, 1792:1856])
            for j, c in enumerate((2048, 2304)):
                h_slot(HIN_SLOT + 6 + j, c)
            for k in range(0, KT, 4):
                g = HIN_SLOT + 8 + k // 4
                slot_free(g)
                v = raw[:, g % 2, :].rearrange("p (k t n) -> p k t n", t=2, n=256)
                put(g % 2, v[:, :, 0, :], w_h[:, k:k + 4, 512:768])
                put(g % 2, v[:, :, 1, :], w_h[:, k:k + 4, 1280:1536])
            for k in range(0, KT, 4):
                g = HIN_SLOT + 10 + k // 4
                slot_free(g)
                v = raw[:, g % 2, 0:4 * 384].rearrange("p (k n) -> p k n", n=384)
                put(g % 2, v[:, :, 0:P], w_h[:, k:k + 4, 1920:2048])
                put(g % 2, v[:, :, P:384], w_h[:, k:k + 4, 2560:2816])
            w_kv, w_q = tiles(w["w_xkv_2"][0]), tiles(w["w_xq_2"][0])
            slot_free(MEM_SLOT)
            load_pair(MEM_SLOT % 2, w_kv[:, :, 0:P], w_kv[:, :, P:2 * P], P)
            slot_free(MEM_SLOT + 1)
            load_rows((MEM_SLOT + 1) % 2, w_kv[:, :, 256:512], 256)
            sp.wait_ge(w_used, HIN_SLOT + 12)
            sp.dma_start(mem[:, :, :], w["mem_2"].rearrange("(b p) d -> p b d", p=P)).then_inc(ld_mem, 16)
            for j in range(2):
                panel_loads(HOUT_SLOT + 2 * j, tiles(w["w_out_2"][0])[:, :, 512 * j:512 * j + 512], 512)
            slot_free(XQ_SLOT)
            load_pair(XQ_SLOT % 2, w_q[:, :, 0:P], w_q[:, :, P:2 * P], P)
            slot_free(XO_SLOT)
            load_rows(XO_SLOT % 2, tiles(w["w_xo_2"][0]), D)
            sp.dma_start(g_last[:, :], w["g_final_2"].rearrange("(a d) -> a d", a=1).broadcast_to([P, D])).then_inc(ld_last, 16)

            up, down = tiles(w["w_up_2"][0]), tiles(w["w_down_2"][0])
            for part in range(MLP_PARTS):
                g0 = MLP_SLOT[part]
                with sp.Fori(0, MT // 4) as i:
                    for j in range(2):
                        slot_free(i * 2 + (g0 + j))
                        c = MT * P * part + 2 * P * j
                        load_pair((g0 + j) % 2, up[:, :, bass.ds(i * (4 * P) + c, P)],
                                  up[:, :, bass.ds(i * (4 * P) + (c + P), P)], P)
                g0 += MT // 2
                with sp.Fori(0, 2) as i:
                    for j in range(MT // 4):
                        slot_free(i * (MT // 4) + (g0 + j))
                        k = MT * part + 4 * j
                        load_rows((g0 + j) % 2, down[:, k:k + 4, bass.ds(i * 512, 512)], 512)

            for tb in range(TB):
                sp.wait_ge(x_final, tb + 1)
                sp.dma_start(out[P * tb:P * tb + P, :], x_out[:, tb, :]).then_inc(stored, 16)
            sp.wait_ge(stored, 16 * TB)

        @block.gpsimd
        def _(pool):
            steps = [0]

            def link(ins):
                ins.then_inc(p_step, 1)
                steps[0] += 1
                pool.wait_ge(p_step, steps[0])

            pool.memset(taps[:, :, :, :], 0.0).then_inc(s5_zero, 1)
            link(pool.memset(half_neg[:, :], -0.5))
            link(pool.memset(minus_one[:, :], -1.0))
            pool.memset(one[:, :], 1.0).then_inc(const_set, 1)
            pool.wait_ge(ld_const, 16 * 2)
            for half in range(2):
                link(pool.tensor_scalar(half_mask[:, half:half + 1], sign[:, :], 1.0 - 2 * half, 0.0, ALU.mult, ALU.max))

            def rsqrt(dst, src, n, scale, parts=P):
                link(pool.tensor_scalar(dst, src, scale, EPS, ALU.mult, ALU.add))
                return pool.tensor_tensor(dst, dst, half_neg[0:parts, 0:n], ALU.pow)

            pool.wait_ge(ld_rows, 32)
            pool.tensor_tensor(skip[:, :, :], skip[:, :, :], ident[0:GH, 0:GH].unsqueeze(1).broadcast_to([GH, G, GH]), ALU.mult).then_inc(s5_skip, 1)
            pool.wait_ge(s5_sq, CH)
            rsqrt(rstd[0:NC, 0:CH], ssq[0:NC, 0:CH], CH, 1.0 / D, NC).then_inc(s5_rstd, 1)

            pool.wait_ge(s5_q, 1)
            pool.wait_ge(s5_nat_sb, 3)
            q_re, q_im = (small[:, i, :].unsqueeze(2).broadcast_to([P, G, GH]) for i in (15, 16))
            b_im = tmp_b[:, :, :, :].rearrange("p a k h -> p (a k) h")
            pool.tensor_tensor(b_im, b_n[:, :, :], q_im, ALU.mult).then_inc(s5_b_read, 1)
            pool.wait_ge(s5_bs_read, 1)
            link(pool.tensor_tensor(b_s[:, :, :], b_s[:, :, :], q_re, ALU.mult))
            pool.wait_ge(s5_b_read, 1)
            pool.tensor_tensor(b_s[:, :, :], b_s[:, :, :], b_im, ALU.add).then_inc(s5_bs, 1)
            pool.wait_ge(ld_rows, 32)
            for s in range(CH // 2):
                pool.wait_ge(s5_scaled, s + 1)
                pool.tensor_tensor(u[:, :, s, :], xp[:, s, :].rearrange("p (g h) -> p g h", h=GH),
                                   g_row[:, :].rearrange("p (g h) -> p g h", h=GH), ALU.mult).then_inc(s5_u, 1)

            def output_rest(b):
                gs = slice(GB * b, GB * b + GB)
                cn = c_n[:, gs, :].unsqueeze(2).broadcast_to([P, GB, CH, GH])
                cs = c_s[:, gs, :].unsqueeze(2).broadcast_to([P, GB, CH, GH])
                pr = pw_r[:, gs, 1:CH + 1].unsqueeze(3).broadcast_to([P, GB, CH, GH])
                pi = pw_is[:, gs, 1:CH + 1].unsqueeze(3).broadcast_to([P, GB, CH, GH])
                if b >= 1:
                    pool.wait_ge(s5_y, b)
                link(pool.tensor_tensor(out_b[:, :, :, :], cn, pi, ALU.mult))
                link(pool.tensor_tensor(tmp_b[:, :, :, :], cs, pr, ALU.mult))
                pool.tensor_tensor(out_b[:, :, :, :], out_b[:, :, :, :], tmp_b[:, :, :, :], ALU.subtract).then_inc(s5_outb, 1)
                pool.wait_ge(s5_outb, b + 1)

            def rotated(o_r, o_i, x_r, x_i, y_r, y_i, groups, n):
                y_r, y_i = (y.unsqueeze(2).broadcast_to([P, groups, n]) for y in (y_r, y_i))
                h0, h1 = (h[:, 0:groups * n].rearrange("p (g n) -> p g n", n=n) for h in half_p)
                link(pool.tensor_tensor(h0, x_r, y_r, ALU.mult))
                link(pool.tensor_tensor(h1, x_i, y_i, ALU.mult))
                link(pool.tensor_tensor(o_r, h0, h1, ALU.subtract))
                link(pool.tensor_tensor(h0, x_r, y_i, ALU.mult))
                link(pool.tensor_tensor(h1, x_i, y_r, ALU.mult))
                return pool.tensor_tensor(o_i, h0, h1, ALU.add)

            def spin_at(k):
                return spin_p[:, 2 * (k % 2), :], spin_p[:, 2 * (k % 2) + 1, :]

            def squared(k, c0, s0):
                c1, s1 = spin_at(k + 1)
                t0, t1 = spin_p[:, 4, :], spin_p[:, 5, :]
                link(pool.tensor_tensor(t0, c0, c0, ALU.mult))
                link(pool.tensor_tensor(t1, s0, s0, ALU.mult))
                link(pool.tensor_tensor(c1, t0, t1, ALU.subtract))
                link(pool.tensor_tensor(t0, c0, s0, ALU.mult))
                return pool.tensor_scalar(s1, t0, 2.0, None, ALU.mult)

            def second_half(b):
                gs, n = slice(GB * b, GB * b + GB), NC // 2
                c0, s0 = spin_at(8)
                rotated(tab_c[:, gs, n:NC], tab_s[:, gs, n:NC], tab_c[:, gs, 0:n], tab_s[:, gs, 0:n],
                        c0[:, gs], s0[:, gs], GB, n).then_inc(s5_half, 1)
                pool.wait_ge(s5_half, b)

            pool.wait_ge(s5_par, 1)
            pool.wait_ge(s5_step, 1)
            squared(0, small[:, 14, :], small[:, 12, :]).then_inc(s5_spin, 1)
            pool.wait_ge(s5_spin, 1)
            output_rest(0)
            pool.wait_ge(s5_u, CH)
            for k in range(1, 3):
                link(squared(k, *spin_at(k)))
            gs = slice(GB * POOL_TABLES, G)
            link(pool.memset(tab_c[:, gs, 0:1], 1.0))
            link(pool.memset(tab_s[:, gs, 0:1], 0.0))
            for k in range(3, 8):
                n = 1 << (k - 3)
                c0, s0 = spin_at(k)
                link(rotated(tab_c[:, gs, n:2 * n], tab_s[:, gs, n:2 * n], tab_c[:, gs, 0:n], tab_s[:, gs, 0:n],
                             c0[:, gs], s0[:, gs], G - GB * POOL_TABLES, n))
                link(squared(k, c0, s0))
            pool.wait_ge(s5_tab, 1)
            second_half(1)
            for b in range(1, NB):
                output_rest(b)
                if b + 1 < NB:
                    second_half(b + 1)

            def split_rest(g, par):
                pool.wait_ge(w_rounded, g + 1)
                pool.tensor_tensor(w_lo[:, par, :], raw[:, par, :], f32(w_hi[:, par, :]), ALU.subtract).then_inc(w_split, 1)

            def split_run(g0, n):
                for g in range(g0, g0 + n):
                    if g < SLOTS:
                        split_rest(g, g % 2)

            def norm_rstd(n):
                for tb in range(TB):
                    pool.wait_ge(row_sq, TB * n + tb + 1)
                    rsqrt(rstd[:, tb:tb + 1], ssq[:, tb:tb + 1], 1, 1.0 / D).then_inc(row_rstd, 1)

            pool.wait_ge(s5_cz, NB)
            split_run(0, 1 + GLU_SLOTS)
            norm_rstd(0)
            split_run(1 + GLU_SLOTS, 1)

            def ffn_split(layer):
                g0 = FFN_SLOT[layer] + 2
                with pool.Fori(0, FT // 2) as i:
                    for j in range(2):
                        split_rest(i * 2 + (g0 + j), (g0 + j) % 2)
                g0 += FT
                split_run(g0, 2 * len(FFN_DOWN) - 1)
                norm_rstd(1 + 2 * layer)
                split_run(g0 + 2 * len(FFN_DOWN) - 1, 1)

            ffn_split(0)

            def head_rsqrt(n):
                pool.wait_ge(head_sum, n + 1)
                if n >= 2:
                    pool.wait_ge(head_norm, n - 1)
                rsqrt(head_rs[:, n % 2, :], head_ss[:, n % 2, :], 8, 1.0 / HD).then_inc(head_rstd, 1)

            def head_cosine(e, table, tb):
                if e < TB:
                    pool.wait_ge(n_free, head_copied(e))
                else:
                    pool.wait_ge(head_norm, e - TB + 1)
                if e >= 2:
                    pool.wait_ge(head_done, e - 1)
                pool.tensor_tensor(head_c[:, e % 2, :].rearrange("p (h d) -> p h d", d=HD),
                                   head_n[:, e % 3, :].rearrange("p (h d) -> p h d", d=HD),
                                   table[:, 0, tb, :].unsqueeze(1).broadcast_to([P, 8, HD]), ALU.mult).then_inc(head_cos, 1)

            pool.wait_ge(qk_tables, 1)
            split_run(DSA_SLOT + 2, 1)
            for tb in range(TB):
                if tb == TB - 1:
                    split_run(DSA_SLOT + 3, 1)
                head_cosine(tb, rope, tb)
            split_run(DSA_SLOT + 4, 1)
            pool.wait_ge(ki_sq, 1)
            rsqrt(head_rs[:, 2, 0:TB], head_ss[:, 2, 0:TB], TB, 1.0 / HD).then_inc(ki_rs, 1)
            for j in range(4):
                split_run(DSA_SLOT + 5 + 2 * j, 1)
                for t in range(TB + 1):
                    if t == TB - 1:
                        split_run(DSA_SLOT + 6 + 2 * j, 1)
                    if t < TB:
                        head_rsqrt(TB * j + t)
                    if t >= 1:
                        head_cosine(TB * (1 + j) + t - 1, rope_q if j < 2 else rope_k, t - 1)
            split_run(DSA_SLOT + 13, 2)

            def invert_sum(units, u0, e):
                c, sink = slice(e % 4, e % 4 + 1), units[e][6]
                pool.wait_ge(at_prob, u0 + e + 1)
                if e >= 4:
                    pool.wait_ge(at_out, u0 + e - 3)
                if sink is not None:
                    link(pool.tensor_tensor(row_sum[:, c], row_sum[:, c], sink_e[:, c], ALU.add))
                pool.tensor_tensor(inv_sum[:, c], row_sum[:, c], minus_one[:, 0:1], ALU.pow).then_inc(at_inv, 1)

            def pad_queries(units, u0, first=0, last=None, soft=True):
                n = len(units)
                for t in range(first, n if last is None else last):
                    if soft and t >= 4:
                        invert_sum(units, u0, t - 4)
                    if u0 + t >= 4:
                        pool.wait_ge(at_dot, u0 + t - 3)
                    pool.tensor_tensor(q_pad[:, (u0 + t) % 4, :], units[t][0], half_mask[:, t % 2:t % 2 + 1].broadcast_to([P, P]),
                                       ALU.mult).then_inc(q_padded, 1)
                if soft and last is None:
                    for e in range(n - 4, n):
                        invert_sum(units, u0, e)

            pool.wait_ge(head_done, 5 * TB)
            pool.wait_ge(head_t_sb, 20)
            pad_queries(dsa_units, DSA_UNIT, 0, 4)
            split_run(DSA_SLOT + 15, 2)
            pad_queries(dsa_units, DSA_UNIT, 4)
            split_run(WO_SLOT + 2, 3)
            norm_rstd(2)
            split_run(WO_SLOT + 5, 1)
            ffn_split(1)
            split_run(HIN_SLOT + 2, 10)
            pool.wait_ge(t_free, HIN_TILE + 10)
            pad_queries(soft_units, SOFT_UNIT, 0, 4)
            split_run(MEM_SLOT, 2)
            pad_queries(soft_units, SOFT_UNIT, 4)
            pad_queries(stick_units, STICK_UNIT, 0, 10, soft=False)
            pool.wait_ge(mem_sq, 2)
            rsqrt(rstd[:, 32:34], ssq[:, 32:34], 2, 1.0 / D).then_inc(mem_rstd, 1)
            pad_queries(stick_units, STICK_UNIT, 10, soft=False)
            pool.wait_ge(grp_sq, 4 * TB)
            rsqrt(rstd[:, 16:32], ssq[:, 16:32], 16, 1.0 / 256).then_inc(grp_rstd, 1)
            split_run(MEM_SLOT + 2, 2)
            split_run(HOUT_SLOT + 2, 3)
            norm_rstd(4)
            split_run(HOUT_SLOT + 5, 1)
            pool.wait_ge(t_free, XQ_TILE + 3)
            pad_queries(mem_units, MEM_UNIT)
            split_run(XQ_SLOT + 2, 1)
            norm_rstd(5)
            split_run(XO_SLOT + 2, 1)
            for part in range(MLP_PARTS):
                g0 = MLP_SLOT[part] + 2
                with pool.Fori(0, MT // 4) as i:
                    for j in range(2):
                        split_rest(i * 2 + (g0 + j), (g0 + j) % 2)
                split_run(g0 + MT // 2, MT // 2)
            norm_rstd(6)

        @block.scalar
        def _(act):
            act.dma_start(ident[:, :], w["c_ident"]).then_inc(ld_const, 16)
            act.dma_start(sign[:, :], w["c_sign"]).then_inc(ld_const, 16)
            act.dma_start(xp[:, :, :], w["x"].rearrange("(c s) d -> c s d", s=CH)).then_inc(ld_x, 16)
            act.dma_start(masks[:, :, :], w["c_masks"]).then_inc(ld_late, 16)
            row = 0
            for name in ("norm_mix", "norm_ffn", "g_mix_2", "g_cross_2", "g_mem_2", "g_mlp_2", "g_group_2"):
                n = w[name].shape[0] * KT
                act.dma_start(gain_rows[row:row + n, :], w[name].rearrange("a (k p) -> (a k) p", p=P)).then_inc(ld_late, 16)
                row += n

            act.dma_start(rope[:, :, :, :], w["c_rope"]).then_inc(ld_qk, 16)
            for j, name in enumerate(("dsa_q_norm", "dsa_k_norm")):
                act.dma_start(gain_qk[:, j, :], w[name][0:1, :].broadcast_to([P, HD])).then_inc(ld_qk, 16)
            act.dma_start(sinks[:, :], w["sinks_2"][0:1, :].broadcast_to([P, 4])).then_inc(ld_qk, 16)
            steps = [0]

            def link(ins):
                ins.then_inc(a_step, 1)
                steps[0] += 1
                act.wait_ge(a_step, steps[0])

            def square(first, last):
                act.wait_ge(ld_x, 16)
                for s in range(first, last):
                    if s >= 1:
                        act.wait_ge(s5_sq, s)
                    act.activation(junk[:, :], xp[:, s, :], ACT.Square, accum_out=ssq[0:NC, s:s + 1]).then_inc(s5_sq, 1)

            act.wait_ge(s5_nat, 1)
            act.activation(small[:, 1:3, :].rearrange("p a g -> p (a g)"), PS[:, 0, 0:2 * G], ACT.Copy).then_inc(s5_nat_sb, 1)
            act.wait_ge(s5_nat, 2)
            act.activation(b_n[:, :, :].rearrange("p g h -> p h g"),
                           PS[:, 1:3, :].rearrange("p b (h g) -> p (b h) g", g=G), ACT.Copy).then_inc(s5_nat_sb, 1)
            act.wait_ge(s5_nat, 3)
            act.activation(b_s[:, :, :].rearrange("p g h -> p h g"),
                           PS[:, 3:5, :].rearrange("p b (h g) -> p (b h) g", g=G), ACT.Copy).then_inc(s5_nat_sb, 1)
            square(0, 3)
            act.wait_ge(s5_ang, 1)
            act.activation(small[:, 12, :], small[:, 11, :], ACT.Sin).then_inc(s5_sin, 1)
            act.activation(small[:, 13, :], small[:, 11, :], ACT.Sin, scale=0.5).then_inc(s5_sin, 1)
            square(3, CH)
            act.wait_ge(s5_nat, 4)
            act.activation(c_n[:, :, :].rearrange("p g h -> p (g h)"), PS[:, 5:7, :].rearrange("p b n -> p (b n)"), ACT.Copy).then_inc(s5_nat_sb, 1)
            act.wait_ge(s5_nat, 5)
            act.activation(c_s[:, 0:G // 2, :].rearrange("p g h -> p (g h)"), PS[:, 7, :], ACT.Copy).then_inc(s5_nat_sb, 1)
            act.wait_ge(s5_nat, 6)
            act.activation(c_s[:, G // 2:G, :].rearrange("p g h -> p (g h)"), PS[:, 1, :], ACT.Copy).then_inc(s5_nat_sb, 1)
            act.wait_ge(gains_t, 1)
            act.activation(gains[:, :], PS[:, 0, 0:len(GAINS) * KT], ACT.Copy).then_inc(gains_sb, 1)
            act.wait_ge(s5_rstd, 1)
            for s in range(CH // 2):
                act.activation(xp[:, s, :], xp[:, s, :], ACT.Copy, scale=rstd[0:NC, s:s + 1]).then_inc(s5_scaled, 1)

            def gelu(b):
                act.wait_ge(s5_y, b + 1)
                act.activation(y[:, b, :, :].rearrange("p t (g h) -> p g t h", h=GH),
                               PS[0:NC, 6:8, :].rearrange("p b (g t h) -> p (b g) t h", t=CH, h=GH), ACT.Gelu_apprx_tanh).then_inc(s5_gelu, 1)

            def decay_out(b):
                if b >= 1:
                    act.wait_ge(s5_cz, b)
                act.activation(decay[:, :, 1:NC], r8[:, GB * b:GB * b + GB].unsqueeze(2).broadcast_to([P, GB, NC - 1]), ACT.Copy).then_inc(s5_dec, 1)

            def maps_out(b):
                act.wait_ge(s5_int, b + 1)
                if b >= 1:
                    act.wait_ge(s5_v, b)
                pt = PS[:, 2:4, :].rearrange("p b (g r q) -> p (b g) r q", r=2, q=GP)
                act.activation(in_t[:, :, :, :], pt, ACT.Copy)
                act.activation(in_s[:, :, 0, :], pt[:, :, 1, :], ACT.Copy)
                act.activation(in_s[:, :, 1, :], pt[:, :, 0, :], ACT.Copy, scale=-1.0).then_inc(s5_int_sb, 1)
                act.wait_ge(s5_lag, b + 1)
                if b >= 1:
                    act.wait_ge(s5_taps, 16 * CH * b)
                act.activation(lag[:, :, :, :].rearrange("p g t h -> p (g t h)"),
                               PS[0:GH, 0:2, :].rearrange("p b n -> p (b n)"), ACT.Copy).then_inc(s5_lag_sb, 1)

            act.wait_ge(s5_spin, 1)
            maps_out(0)
            for q in range(8):
                act.wait_ge(s5_ut, q + 1)
                act.activation(uT[:, GB * q:GB * q + GB, :].rearrange("p g c -> p (g c)"), PS[:, q, :], ACT.Copy).then_inc(s5_ut_sb, 1)
            decay_out(0)
            for b in range(1, NB):
                maps_out(b)
                decay_out(b)
                gelu(b - 1)

            def turn_hi(j0, n, gain=None, width=S, dst=xT_hi, view=None, banks=4, k0=0):
                for k in range(k0, n):
                    act.wait_ge(turned, j0 + k + 1)
                    o, i = dst[:, k, 0:width], PS[:, k % banks, 0:width]
                    if view:
                        o, i = view(o, i)
                    act.activation(o, i, ACT.Copy, scale=1.0 if gain is None else gains[:, gain * KT + k:gain * KT + k + 1]).then_inc(x_hi_done, 1)

            def round_slot(g, par, use):
                act.wait_ge(w_raw[par], use * 32)
                if not isinstance(g, int) or g >= 2:
                    act.wait_ge(w_used, g - 1)
                act.activation(w_hi[:, par, :], raw[:, par, :], ACT.Copy).then_inc(w_rounded, 1)

            def round_run(g0, n):
                for g in range(g0, g0 + n):
                    if g < SLOTS:
                        round_slot(g, g % 2, g // 2 + 1)

            turn_hi(0, 4, view=chunk_view)
            act.wait_ge(s5_v, NB)
            round_run(0, 1)
            gelu(NB - 1)
            turn_hi(0, KT, view=chunk_view, k0=4)
            round_run(1, 1)
            act.wait_ge(ld_res, 16)
            for j in range(4):
                round_run(2 + 2 * j, 1)
                for tb in range(TB):
                    e = TB * j + tb
                    if tb < TB - 1:
                        act.wait_ge(n_ready, 3 * (GLU_PANEL + j) + tb + 1)
                    else:
                        act.wait_ge(w_used, GLU_SLOT + 2 * j + 2)
                    if e >= 2:
                        act.wait_ge(n_free, TB + e - 1)
                    act.activation(glu_sg[:, e % 2, :], PS[:, 4 + tb, 256:512], ACT.Sigmoid).then_inc(glu_sig, 1)
                if j < 3:
                    round_run(3 + 2 * j, 1)

            def norm_sq(n, sem_x, value):
                for tb in range(TB):
                    act.wait_ge(sem_x, value - (TB - 1 - tb))
                    if n + tb >= 1:
                        act.wait_ge(row_sq, TB * n + tb)
                    act.activation(sq_junk[:, :], x_res[:, tb, :], ACT.Square, accum_out=ssq[:, tb:tb + 1]).then_inc(row_sq, 1)

            norm_sq(0, glu_done, 4 * TB)
            round_run(9, 1)
            turn_hi(KT, KT, gain=2, banks=8)

            def ffn_act(layer):
                g0, t0, h0 = FFN_SLOT[layer], FFN_TILE[layer], FFN_HID[layer]
                with act.Fori(0, FT // 2) as i:
                    for j in range(2):
                        pair = (t0 + j) % 2
                        act.wait_ge(t_first, i * 2 + (t0 + j + 1))
                        act.wait_ge(hid_done, i * 2 + (h0 + j + 1))
                        act.activation(gbuf[:, pair, 0, :], PS[:, 2 * pair, :], ACT.Silu).then_inc(hid_act, 1)
                        g = g0 + j + 2
                        round_slot(i * 2 + g, g % 2, i + (g // 2 + 1))
                round_run(g0 + FT + 2, 2 * len(FFN_DOWN) - 1)
                norm_sq(1 + 2 * layer, n_free, TB * (FFN_PANEL[layer] + 3))
                round_run(g0 + FT + 1 + 2 * len(FFN_DOWN), 1)

            ffn_act(0)
            turn_hi(2 * KT, KT, gain=1, banks=8)

            def panel_wait(ni, tb, g_last_slot):
                if tb < TB - 1:
                    act.wait_ge(n_ready, 3 * ni + tb + 1)
                else:
                    act.wait_ge(w_used, g_last_slot + 1)

            def head_turned(pi, dst, at):
                for j in range(4):
                    act.wait_ge(head_t, 4 * pi + j + 1)
                    act.activation(dst[:, at + j, :], PS[:, j, :], ACT.Copy).then_inc(head_t_sb, 1)

            g = DSA_SLOT
            round_run(g + 2, 1)
            for tb in range(TB):
                if tb == TB - 1:
                    round_run(g + 3, 1)
                panel_wait(DSA_PANEL, tb, g + 1)
                if tb >= 3:
                    act.wait_ge(head_done, tb - 2)
                act.activation(head_n[:, tb % 3, :], PS[:, 4 + tb, :], ACT.Copy).then_inc(n_free, 1)
            round_run(g + 4, 1)
            act.wait_ge(w_used, g + 3)
            act.activation(ki_raw[:, :, :], PS[:, 4:8, 0:HD + NI], ACT.Copy).then_inc(n_free, TB)
            act.wait_ge(n_free, TB * (DSA_PANEL + 3))
            act.activation(ki_c[:, :, :], ki_raw[:, :, 0:HD], ACT.Square).then_inc(ki_squared, 1)
            for j in range(4):
                round_run(g + 5 + 2 * j, 1)
                for tb in range(TB):
                    if tb == TB - 1:
                        round_run(g + 6 + 2 * j, 1)
                    n, e = TB * j + tb, TB * (1 + j) + tb
                    panel_wait(DSA_PANEL + 2 + j, tb, g + 4 + 2 * j)
                    if n >= 2:
                        act.wait_ge(head_sum, n - 1)
                    act.activation(head_sq[:, n % 2, :], PS[:, 4 + tb, :], ACT.Square).then_inc(head_sq_done, 1)
                    act.wait_ge(head_done, e - 2)
                    act.activation(head_n[:, e % 3, :], PS[:, 4 + tb, :], ACT.Copy).then_inc(n_free, 1)
                if j == 0:
                    head_turned(0, qiT, 0)
                    for head in range(2):
                        act.wait_ge(ki_t, head + 1)
                        act.activation(kiT[head][:, :], PS[:, head, :], ACT.Copy).then_inc(ki_t_sb, 1)
                    for e in range(3 * NI):
                        n = P * (e // NI + 2)
                        act.wait_ge(idx_dot, e + 1)
                        if e >= 2:
                            act.wait_ge(idx_sum, e - 1)
                        act.activation(relu_i[:, e % 2, 0:n], PS[:, e % 4, 0:n], ACT.Relu, scale=HD ** -0.5).then_inc(idx_relu, 1)
                else:
                    head_turned(j, qT if j < 3 else kT, (0, 0, 4, 0)[j])
            for j in range(2):
                round_run(g + 13 + 2 * j, 1)
                for tb in range(TB):
                    if tb == TB - 1:
                        round_run(g + 14 + 2 * j, 1)
                    panel_wait(DSA_PANEL + 6 + j, tb, g + 12 + 2 * j)
                    act.activation(v_dsa[:, tb, 512 * j:512 * j + 512], PS[:, 4 + tb, :], ACT.Copy).then_inc(n_free, 1)
                if j == 0:
                    head_turned(4, kT, 4)

            def attend_act(units, u0, stick=False):
                n = len(units)
                for t in range(n + 3):
                    if stick and t < n:
                        cols = units[t][1].shape[1]
                        act.wait_ge(at_dot, u0 + t + 1)
                        if t >= 2:
                            act.wait_ge(at_prob, u0 + t - 1)
                        if t >= 3:
                            act.wait_ge(at_turn, u0 + t - 2)
                        act.activation(stay[t % 2][:, 0:cols], PS[:, t % 3, 0:cols], ACT.Sigmoid, scale=-1.0)
                        act.activation(logit[:, t % 3, 0:cols], PS[:, t % 3, 0:cols], ACT.Sigmoid).then_inc(at_logit, 1)
                        if 2 <= t < 4:
                            mem_square(t - 2)
                        if 4 <= t < 16:
                            group_sq(t - 4, (0, 2, 3))
                    e = t - 2
                    if 0 <= e < n:
                        cols = units[e][1].shape[1]
                        act.wait_ge(at_turn, u0 + e + 1)
                        if e >= 2:
                            act.wait_ge(at_pv, u0 + e - 1)
                        act.activation(probT[:, e % 2, 0:cols], PS[:, 3 + e % 2, 0:cols], ACT.Copy).then_inc(at_turn_sb, 1)
                    if not stick and t < n:
                        cols, sink = units[t][1].shape[1], units[t][6]
                        act.wait_ge(at_max, u0 + t + 1)
                        p = logit[:, t % 3, 0:cols]
                        m = neg_max[:, t % 4:t % 4 + 1]
                        if sink is not None:
                            act.activation(sink_e[:, t % 4:t % 4 + 1], sinks[:, sink:sink + 1], ACT.Exp, bias=m)
                        act.activation(p, PS[:, t % 3, 0:cols] if units[t][2] is None else p, ACT.Exp, bias=m, accum_out=row_sum[:, t % 4:t % 4 + 1]).then_inc(at_prob, 1)

            def mem_square(m):
                act.wait_ge(ld_mem, 16)
                if m:
                    act.wait_ge(mem_sq, 1)
                act.activation(late_junk[:, :], mem[:, m, :], ACT.Square, accum_out=ssq[:, 32 + m:33 + m]).then_inc(mem_sq, 1)

            def group_sq(e, groups):
                tb, j = divmod(e, len(groups))
                j = groups[j]
                if e >= 1 or j == 1:
                    act.wait_ge(grp_sq, e + (12 if j == 1 else 0))
                else:
                    act.wait_ge(at_out, STICK_UNIT)
                    act.wait_ge(mem_sq, 2)
                c = 16 + 4 * tb + j
                act.activation(late_junk[:, 0:256], o_nat[:, tb, 256 * j:256 * j + 256], ACT.Square,
                               accum_out=ssq[:, c:c + 1]).then_inc(grp_sq, 1)

            attend_act(dsa_units, DSA_UNIT)
            turn_hi(3 * KT, KT)
            round_run(WO_SLOT + 2, 3)
            norm_sq(2, n_free, TB * (WO_PANEL + 3))
            round_run(WO_SLOT + 5, 1)
            turn_hi(4 * KT, KT, gain=3, banks=8)
            ffn_act(1)

            turn_hi(5 * KT, KT, gain=4, banks=8)

            def tiles_out(g, ti, dst, scale=1.0, width=S):
                pair = ti % 2
                act.wait_ge(t_first, ti + 1)
                act.activation(dst[:, 0, :], PS[:, 2 * pair, 0:width], ACT.Copy, scale=scale)
                act.wait_ge(w_used, g + 1)
                act.activation(dst[:, 1, :], PS[:, 2 * pair + 1, 0:width], ACT.Copy, scale=scale).then_inc(t_free, 1)

            for j in range(8):
                tiles_out(HIN_SLOT + j, HIN_TILE + j, hqk[:, 2 * j:2 * j + 2, :], HD ** -0.5 if j % 2 == 0 else 1.0)
                round_run(HIN_SLOT + j + 2, 1)
                if j == 0:
                    act.wait_ge(bias_row, 1)
                    act.activation(bias_v[:, 0:512], PS[0:NREL, 4, :], ACT.Copy)
                    act.activation(bias_v[:, 512:BIAS_W], PS[0:NREL, 5, 0:BIAS_W - 512], ACT.Copy).then_inc(bias_row_sb, 1)
                    act.wait_ge(bias_row_sb, 1)
                    act.dma_start(bias_dram, bias_v[:, :]).then_inc(bias_out, 16)
                if j == 1:
                    act.wait_ge(bias_out, 16)
                    act.dma_start(bias[:, :, :], bass.AP(tensor=bias_dram.tensor, offset=0, ap=[[1, P], [BIAS_W, NREL], [1, S]]))\
                       .then_inc(ld_bias_t, 16)
            for j, (dst, n) in enumerate(((v_ab, 512), (v_cd, 384))):
                g = HIN_SLOT + 8 + 2 * j
                round_run(g + 2, 1)
                for tb in range(TB):
                    panel_wait(HIN_PANEL + j, tb, g + 1)
                    act.activation(dst[:, tb, :], PS[:, 4 + tb, 0:n], ACT.Copy).then_inc(n_free, 1)
                round_run(g + 3, 1)
            attend_act(soft_units, SOFT_UNIT)
            attend_act(stick_units, STICK_UNIT, stick=True)
            act.wait_ge(at_out, MEM_UNIT)
            for tb in range(TB):
                group_sq(tb, (1,))

            turn_hi(6 * KT, KT, gain=6, width=MEM, dst=memT_hi)
            tiles_out(MEM_SLOT, MEM_TILE, kxT, width=MEM)
            round_run(MEM_SLOT + 2, 1)
            act.wait_ge(n_ready, 3 * MEM_PANEL + 3)
            act.activation(vx[:, 0, :], PS[:, 4, 0:MEM], ACT.Copy)
            act.wait_ge(w_used, MEM_SLOT + 2)
            act.activation(vx[:, 1, :], PS[:, 5, 0:MEM], ACT.Copy).then_inc(n_free, TB)
            round_run(MEM_SLOT + 3, 1)
            turn_hi(7 * KT, KT, gain=8)
            round_run(HOUT_SLOT + 2, 3)

            norm_sq(4, n_free, TB * (HOUT_PANEL + 3))
            round_run(HOUT_SLOT + 5, 1)
            turn_hi(8 * KT, KT, gain=5, banks=8)
            tiles_out(XQ_SLOT, XQ_TILE, qxT, HD ** -0.5)
            attend_act(mem_units, MEM_UNIT)
            turn_hi(9 * KT, 2)
            round_run(XQ_SLOT + 2, 1)

            norm_sq(5, n_free, TB * (XO_PANEL + 3))
            round_run(XO_SLOT + 2, 1)
            turn_hi(9 * KT + 2, KT, gain=7, banks=8)
            for part in range(MLP_PARTS):
                g0, t0, h0 = MLP_SLOT[part], MLP_TILE[part], MLP_HID[part]
                with act.Fori(0, MT // 4) as i:
                    for j in range(2):
                        pair = (t0 + j) % 2
                        act.wait_ge(t_first, i * 2 + (t0 + j + 1))
                        act.wait_ge(hid_done, i * 2 + (h0 + j + 1))
                        act.activation(gbuf[:, pair, 0, :], PS[:, 2 * pair, :], ACT.Relu)
                        act.wait_ge(w_used, i * 2 + (g0 + j + 1))
                        act.activation(gbuf[:, pair, 1, :], PS[:, 2 * pair + 1, :], ACT.Relu).then_inc(t_free, 1)
                        g = g0 + j + 2
                        round_slot(i * 2 + g, g % 2, i + (g // 2 + 1))
                round_run(g0 + MT // 2 + 2, MT // 2)
            norm_sq(6, n_free, TB * (MLP_PANEL[1] + 3))

        @block.vector
        def _(dve):
            steps = [0]

            def link(ins):
                ins.then_inc(v_step, 1)
                steps[0] += 1
                dve.wait_ge(v_step, steps[0])

            def pt(i):
                return small[:, i, :]

            tt, ts, stt = dve.tensor_tensor, dve.tensor_scalar, dve.scalar_tensor_tensor
            dve.wait_ge(const_set, 1)
            dve.memset(neg_max[:, 0:1], 0.0).then_inc(t_free, 2)
            dve.memset(neg_max[:, 1:2], 0.0).then_inc(n_free, TB)
            dve.memset(neg_max[:, 2:3], 0.0).then_inc(hid_done, 2)

            def exp_small(dst, x, a, b, c):
                link(ts(a, x, 88.0, -87.0, ALU.min, ALU.max))
                link(ts(b.bitcast(I32), a, 1.4426950408889634, None, ALU.mult))
                link(dve.tensor_copy(c, b.bitcast(I32)))
                link(stt(a, c, -0.693359375, a, ALU.mult, ALU.add))
                link(stt(a, c, 2.12194440e-4, a, ALU.mult, ALU.add))
                link(ts(b.bitcast(I32), c, 127.0, 8388608.0, ALU.add, ALU.mult))
                link(ts(c, a, 1.0 / 5040, None, ALU.mult))
                for f in (720, 120, 24, 6, 2, 1):
                    link(stt(c, c, 1.0 / f, a, ALU.add, ALU.mult))
                link(stt(dst, c, 1.0, b, ALU.add, ALU.mult))

            dve.wait_ge(ld_lam, 16 * 5)
            dve.wait_ge(ld_const, 16 * 2)
            dve.wait_ge(s5_nat_sb, 1)
            exp_small(pt(3), pt(0), pt(4), pt(5), pt(6))
            link(tt(pt(7), pt(1), pt(3), ALU.mult))
            exp_small(pt(8), pt(7), pt(4), pt(5), pt(6))
            link(tt(pt(9), pt(2), pt(3), ALU.mult))
            link(ts(pt(5).bitcast(I32), pt(9), 0.15915494309189535, None, ALU.mult))
            link(dve.tensor_copy(pt(6), pt(5).bitcast(I32)))
            link(stt(pt(9), pt(6), -6.28125, pt(9), ALU.mult, ALU.add))
            link(stt(pt(9), pt(6), -1.9353071795864769e-3, pt(9), ALU.mult, ALU.add))
            ts(pt(11), pt(9), 3.1415925, -3.1415925, ALU.min, ALU.max).then_inc(s5_ang, 1)
            dve.wait_ge(s5_sin, 2)
            link(tt(pt(14), pt(13), pt(13), ALU.mult))
            link(ts(pt(14), pt(14), -2.0, 1.0, ALU.mult, ALU.add))
            dve.memset(decay[:, :, 0:1], 0.0).then_inc(s5_step, 1)
            link(tt(pw_r[:, :, 1], pt(8), pt(14), ALU.mult))
            link(tt(pw_i[:, :, 1], pt(8), pt(12), ALU.mult))
            link(dve.memset(pw_r[:, :, 0], 1.0))
            link(dve.memset(pw_i[:, :, 0], 0.0))
            link(tt(pt(4), pt(8), pt(8), ALU.mult))
            link(tt(pt(4), pt(4), pt(4), ALU.mult))
            link(tt(r8[:, :], pt(4), pt(4), ALU.mult))
            link(tt(pt(4), pt(1), pt(1), ALU.mult))
            link(tt(pt(5), pt(2), pt(2), ALU.mult))
            link(tt(pt(4), pt(4), pt(5), ALU.add))
            link(dve.reciprocal(pt(4), pt(4)))
            link(ts(pt(5), pw_r[:, :, 1], -1.0, None, ALU.add))
            link(tt(pt(15), pt(5), pt(1), ALU.mult))
            link(tt(pt(16), pw_i[:, :, 1], pt(2), ALU.mult))
            link(tt(pt(15), pt(15), pt(16), ALU.add))
            link(tt(pt(15), pt(15), pt(4), ALU.mult))
            link(tt(pt(16), pw_i[:, :, 1], pt(1), ALU.mult))
            link(tt(pt(17), pt(5), pt(2), ALU.mult))
            link(tt(pt(16), pt(16), pt(17), ALU.subtract))
            link(tt(pt(16), pt(16), pt(4), ALU.mult))
            ts(pt(16), pt(16), sign[:, 0:1], None, ALU.mult).then_inc(s5_q, 1)
            qr = pt(15).unsqueeze(2).broadcast_to([P, G, GH])
            qi = pt(16).unsqueeze(2).broadcast_to([P, G, GH])
            dve.wait_ge(s5_q, 1)
            dve.wait_ge(s5_nat_sb, 3)
            link(tt(bar[:, 0, :, :], b_n[:, :, :], qr, ALU.mult))
            tt(bar[:, 1, :, :], b_s[:, :, :], qi, ALU.mult).then_inc(s5_bs_read, 1)
            dve.wait_ge(s5_bs_read, 1)
            dve.wait_ge(s5_b_read, 1)
            link(tt(b_n[:, :, :], bar[:, 0, :, :], bar[:, 1, :, :], ALU.subtract))

            def cmul(o_r, o_i, x_r, x_i, y_r, y_i, n, s1, s2, groups=G):
                y_r, y_i = (y.unsqueeze(2).broadcast_to([P, groups, n]) for y in (y_r, y_i))
                link(tt(s1, x_r, y_r, ALU.mult))
                link(tt(s2, x_i, y_i, ALU.mult))
                link(tt(o_r, s1, s2, ALU.subtract))
                link(tt(s1, x_r, y_i, ALU.mult))
                link(tt(s2, x_i, y_r, ALU.mult))
                link(tt(o_i, s1, s2, ALU.add))

            for lo, n, e in ((1, 1, 1), (1, 2, 2), (1, 4, 4)):
                cmul(pw_r[:, :, lo + e:lo + e + n], pw_i[:, :, lo + e:lo + e + n],
                     pw_r[:, :, lo:lo + n], pw_i[:, :, lo:lo + n], pw_r[:, :, e], pw_i[:, :, e], n,
                     prod1[:, :, 0:n], prod2[:, :, 0:n])
            link(ts(pw_rs[:, :, :], pw_r[:, :, :], sign[:, 0:1], None, ALU.mult))
            ts(pw_is[:, :, :], pw_i[:, :, :], sign[:, 0:1], -1.0, ALU.mult, ALU.mult).then_inc(s5_par, 1)
            dve.wait_ge(s5_rstd, 1)
            dve.wait_ge(ld_rows, 32)
            for s in range(CH // 2, CH):
                stt(u[:, :, s, :], xp[:, s, :].rearrange("p (g h) -> p g h", h=GH), rstd[0:NC, s:s + 1],
                    g_row[:, :].rearrange("p (g h) -> p g h", h=GH), ALU.mult, ALU.mult).then_inc(s5_u, 1)

            def spin_pair(k):
                return spin[:, 2 * (k % 2), :], spin[:, 2 * (k % 2) + 1, :]

            def square_spin(k, c0, s0):
                c1, s1 = spin_pair(k + 1)
                t0, t1 = spin[:, 4, :], spin[:, 5, :]
                link(tt(t0, c0, c0, ALU.mult))
                link(tt(t1, s0, s0, ALU.mult))
                link(tt(c1, t0, t1, ALU.subtract))
                link(tt(t0, c0, s0, ALU.mult))
                link(ts(s1, t0, 2.0, None, ALU.mult))

            square_spin(0, pt(14), pt(12))

            def chunk_tables():
                for k in range(1, 3):
                    square_spin(k, *spin_pair(k))
                gs = slice(0, GB * POOL_TABLES)
                link(dve.memset(tab_c[:, gs, 0:1], 1.0))
                link(dve.memset(tab_s[:, gs, 0:1], 0.0))
                for k in range(3, 8):
                    n = 1 << (k - 3)
                    c0, s0 = spin_pair(k)
                    cmul(tab_c[:, gs, n:2 * n], tab_s[:, gs, n:2 * n], tab_c[:, gs, 0:n], tab_s[:, gs, 0:n], c0[:, gs], s0[:, gs], n,
                         prod1[:, gs, 0:n], prod2[:, gs, 0:n], GB * POOL_TABLES)
                    square_spin(k, c0, s0)
                gs, n = slice(0, GB), NC // 2
                c0, s0 = spin_pair(8)
                cmul(tab_c[:, gs, n:NC], tab_s[:, gs, n:NC], tab_c[:, gs, 0:n], tab_s[:, gs, 0:n], c0[:, gs], s0[:, gs], n,
                     part1[:, :, :], part2[:, :, :], GB)
                link(dve.memset(cz[:, :, 0:1], 0.0))
                dve.memset(sz[:, :, 0:1], 0.0).then_inc(s5_tab, 1)
                dve.wait_ge(s5_tab, 1)

            def over_k(ap, b, n):
                return ap[:, GB * b:GB * b + GB, :].unsqueeze(2).broadcast_to([P, GB, n, GH])

            def output_map(b):
                o = out_a[b % 3]
                gs = slice(GB * b, GB * b + GB)
                p_re, p_im = (t[:, gs, 0:CH + 1].unsqueeze(3).broadcast_to([P, GB, CH + 1, GH]) for t in (pw_rs, pw_i))
                if b >= 3:
                    dve.wait_ge(s5_y, b - 2)
                dve.wait_ge(s5_inw, min(b + 1, NB))
                link(tt(o[:, :, :, :], over_k(c_n, b, CH + 1), p_re, ALU.mult))
                link(tt(tmp_a[:, :, :, :], over_k(c_s, b, CH + 1), p_im, ALU.mult))
                tt(o[:, :, :, :], o[:, :, :, :], tmp_a[:, :, :, :], ALU.subtract).then_inc(s5_outa, 1)

            def input_map(b):
                gs = slice(GB * b, GB * b + GB)
                p_re, p_im = (t[:, gs, 0:CH][:, :, ::-1].unsqueeze(3).broadcast_to([P, GB, CH, GH]) for t in (pw_r, pw_is))
                if b >= 1:
                    dve.wait_ge(s5_int, b)
                    dve.wait_ge(s5_outa, b)
                link(tt(in_w[:, :, :, :], over_k(b_n, b, CH), p_re, ALU.mult))
                link(tt(tmp_a[:, :, 0:CH, :], over_k(b_s, b, CH), p_im, ALU.mult))
                tt(in_w[:, :, :, :], in_w[:, :, :, :], tmp_a[:, :, 0:CH, :], ALU.add).then_inc(s5_inw, 1)

            def chunk_scan(b):
                gs = slice(GB * b, GB * b + GB)
                dve.wait_ge(s5_v, b + 1)
                if b >= 1:
                    dve.wait_ge(s5_half, b)
                ps_v = PS[:, 4, :].rearrange("p (g c) -> p g c", c=NC)
                ps_s = PS[:, 5, :].rearrange("p (g c) -> p g c", c=NC)
                link(tt(v1[:, :, :], ps_v, tab_c[:, gs, :], ALU.mult))
                tt(v2[:, :, :], ps_s, tab_s[:, gs, :], ALU.mult).then_inc(s5_rot, 1)
                dve.wait_ge(s5_rot, b + 1)
                link(tt(v1[:, :, :], v1[:, :, :], v2[:, :, :], ALU.add))
                dve.wait_ge(s5_dec, b + 1)
                if b >= 1:
                    dve.wait_ge(s5_cz, b)
                link(dve.tensor_tensor_scan(z[:, :, :].rearrange("p g c -> p (g c)"),
                                            decay[:, :, :].rearrange("p g c -> p (g c)"),
                                            v1[:, :, :].rearrange("p g c -> p (g c)"), 0.0, ALU.mult, ALU.add))
                if b >= 1:
                    dve.wait_ge(s5_y, b)
                link(tt(cz[:, :, 1:NC], z[:, :, 0:NC - 1], tab_c[:, gs, 0:NC - 1], ALU.mult))
                tt(sz[:, :, 1:NC], z[:, :, 0:NC - 1], tab_s[:, gs, 0:NC - 1], ALU.mult).then_inc(s5_cz, 1)

            dve.wait_ge(s5_bs, 1)
            dve.wait_ge(s5_nat_sb, 6)
            dve.wait_ge(s5_u, CH)
            for b in range(2):
                input_map(b)
                output_map(b)
            chunk_tables()
            for b in range(NB):
                chunk_scan(b)
                if b + 2 < NB:
                    input_map(b + 2)
                    output_map(b + 2)

            def turn_lo(j0, n, gain=None, width=S, hi=xT_hi, lo=xT_lo, view=None, banks=4):
                for k in range(n):
                    dve.wait_ge(x_hi_done, j0 + k + 1)
                    o, h, i = lo[:, k, 0:width], f32(hi[:, k, 0:width]), PS[:, k % banks, 0:width]
                    if view:
                        (o, i), (h, i) = view(o, i), view(h, i)
                        tt(o, i, h, ALU.subtract).then_inc(x_lo_done, 1)
                    else:
                        s = 1.0 if gain is None else gains[:, gain * KT + k:gain * KT + k + 1]
                        stt(o, i, s, h, ALU.mult, ALU.subtract).then_inc(x_lo_done, 1)

            turn_lo(0, KT, view=chunk_view)
            def norm_row(n, tb):
                dve.wait_ge(row_rstd, TB * n + tb + 1)
                if n == 6:
                    dve.wait_ge(ld_last, 16)
                    stt(x_out[:, tb, :], x_res[:, tb, :], rstd[:, tb:tb + 1], g_last[:, :], ALU.mult, ALU.mult).then_inc(x_final, 1)
                    return
                ts(diag[:, tb, :], ident[:, :], rstd[:, tb:tb + 1], None, ALU.mult).then_inc(row_norm, 1)

            def norm_after(n, tb):
                if tb >= 1:
                    norm_row(n, tb - 1)
                if tb == TB - 1:
                    norm_row(n, tb)

            dve.wait_ge(ld_res, 16)
            dve.wait_ge(gains_sb, 1)
            dve.wait_ge(ld_late, 16 * 8)
            for e in range(4 * TB):
                j, tb = divmod(e, TB)
                dve.wait_ge(glu_sig, e + 1)
                tt(glu_v[:, e % 2, :], PS[:, 4 + tb, 0:256], glu_sg[:, e % 2, :], ALU.mult).then_inc(n_free, 1)
                dve.wait_ge(n_free, TB + e + 1)
                xs = x_res[:, tb, 256 * j:256 * j + 256]
                tt(xs, xs, glu_v[:, e % 2, :], ALU.add).then_inc(glu_done, 1)
                if j == 3:
                    norm_after(0, tb)
            turn_lo(KT, KT, gain=2, banks=8)

            def add_panel(ni, g_done, cols, extra=0, norm=None):
                for tb in range(TB):
                    if tb < TB - 1:
                        dve.wait_ge(n_ready, ni * 3 + (tb + 1 + extra))
                    else:
                        dve.wait_ge(w_used, g_done)
                    tt(x_res[:, tb, cols], x_res[:, tb, cols], PS[:, 4 + tb, :], ALU.add).then_inc(n_free, 1)
                    if norm is not None:
                        norm_after(norm, tb)

            def ffn_dve(layer):
                t0, h0 = FFN_TILE[layer], FFN_HID[layer]
                g0 = FFN_SLOT[layer]
                with dve.Fori(0, FT // 2) as i:
                    for j in range(2):
                        pair = (t0 + j) % 2
                        dve.wait_ge(w_used, i * 2 + (g0 + j + 1))
                        dve.wait_ge(hid_act, i * 2 + (h0 + j + 1))
                        tt(gbuf[:, pair, 1, :], gbuf[:, pair, 0, :], PS[:, 2 * pair + 1, :], ALU.mult).then_inc(t_free, 1)
                        dve.wait_ge(t_free, i * 2 + (t0 + j + 3))
                        dve.tensor_copy(hT_hi[:, bass.ds(i * 2 + j, 1), :], gbuf[:, pair, 1:2, :]).then_inc(hid_hi, 1)
                        dve.wait_ge(hid_hi, i * 2 + (h0 + j + 1))
                        tt(hT_lo[:, bass.ds(i * 2 + j, 1), :], gbuf[:, pair, 1:2, :], f32(hT_hi[:, bass.ds(i * 2 + j, 1), :]),
                           ALU.subtract).then_inc(hid_done, 1)
                m = len(FFN_DOWN)
                for i in range(2):
                    add_panel(i + FFN_PANEL[layer], i * m + (g0 + FT + m), slice(512 * i, 512 * i + 512),
                              norm=(None, 1 + 2 * layer)[i])

            ffn_dve(0)
            turn_lo(2 * KT, KT, gain=1, banks=8)
            dve.wait_ge(ld_qk, 16 * 4)
            for j, (dst, scale) in enumerate(((rope_q, HD ** -0.5), (rope_k, 1.0))):
                g = gain_qk[:, j, :].unsqueeze(1).broadcast_to([P, TB, HD])
                link(tt(dst[:, 0, :, :], rope[:, 0, :, :], g, ALU.mult))
                for half in range(2):
                    to, of = slice(32 * half, 32 * half + 32), slice(32 - 32 * half, 64 - 32 * half)
                    g = gain_qk[:, j, of].unsqueeze(1).broadcast_to([P, TB, 32])
                    link(tt(dst[:, 1, :, to], rope[:, 1, :, to], g, ALU.mult))
                if scale != 1.0:
                    link(ts(dst[:, :, :, :], dst[:, :, :, :], scale, None, ALU.mult))
            ts(sinks_neg[:, :], sinks[:, :], -1.0, None, ALU.mult).then_inc(qk_tables, 1)

            def swap_halves(ap):
                return ap.rearrange("p (h t d) -> p h t d", t=2, d=HD // 2)[:, :, ::-1, :]

            def head_sums(n):
                dve.wait_ge(head_sq_done, n + 1)
                if n >= 2:
                    dve.wait_ge(head_rstd, n - 1)
                dve.tensor_reduce(head_ss[:, n % 2, :], head_sq[:, n % 2, :].rearrange("p (h d) -> p h d", d=HD),
                                  AX.X, ALU.add).then_inc(head_sum, 1)

            def head_scale(n):
                e = n + TB
                dve.wait_ge(n_free, head_copied(e))
                dve.wait_ge(head_rstd, n + 1)
                hn = head_n[:, e % 3, :].rearrange("p (h d) -> p h d", d=HD)
                tt(hn, hn, head_rs[:, n % 2, :].unsqueeze(2).broadcast_to([P, 8, HD]), ALU.mult).then_inc(head_norm, 1)

            def head_sine(e, table, tb):
                pi = e // TB
                if pi == 0:
                    dve.wait_ge(n_free, head_copied(e))
                else:
                    dve.wait_ge(head_norm, e - TB + 1)
                if pi >= 2:
                    dve.wait_ge(head_t, 4 * (pi - 1))
                sin = table[:, 1, tb, :].rearrange("p (t d) -> p t d", t=2).unsqueeze(1).broadcast_to([P, 8, 2, HD // 2])
                tt(stage[:, pi % 2, tb, :].rearrange("p (h t d) -> p h t d", t=2, d=HD // 2),
                   swap_halves(head_n[:, e % 3, :]), sin, ALU.mult).then_inc(head_sin, 1)

            def head_add(e, tb):
                st = stage[:, (e // TB) % 2, tb, :]
                dve.wait_ge(head_cos, e + 1)
                dve.wait_ge(head_sin, e + 1)
                tt(st, st, head_c[:, e % 2, :], ALU.add).then_inc(head_done, 1)

            for t in range(TB + 1):
                if t < TB:
                    head_sine(t, rope, t)
                if t >= 1:
                    head_add(t - 1, t - 1)
            dve.wait_ge(ki_squared, 1)
            dve.tensor_reduce(head_ss[:, 2, 0:TB], ki_c[:, :, :], AX.X, ALU.add).then_inc(ki_sq, 1)
            ts(w_idx[:, :, :], ki_raw[:, :, HD:HD + NI], NI ** -0.5, None, ALU.mult)
            dve.wait_ge(ki_rs, 1)
            link(tt(ki_n[:, :, :], ki_raw[:, :, 0:HD], head_rs[:, 2, 0:TB].unsqueeze(2).broadcast_to([P, TB, HD]), ALU.mult))
            for half in range(2):
                to, of = slice(32 * half, 32 * half + 32), slice(32 - 32 * half, 64 - 32 * half)
                link(tt(ki_c[:, :, to], ki_n[:, :, of], rope[:, 1, :, to], ALU.mult))
            link(tt(ki_n[:, :, :], ki_n[:, :, :], rope[:, 0, :, :], ALU.mult))
            tt(ki_st[:, :, 1, :], ki_n[:, :, :], ki_c[:, :, :], ALU.add).then_inc(ki_done, 1)
            for side in (0, 2):
                dve.memset(ki_st[:, :, side, :], 0.0).then_inc(ki_done, 1)

            def index_scores():
                for e in range(3 * NI):
                    b, h = e // NI + 1, e % NI
                    n = P * (b + 1)
                    sc = score[:, BLK[b]:BLK[b] + n]
                    dve.wait_ge(idx_relu, e + 1)
                    if h == 0:
                        if e:
                            dve.wait_ge(idx_sum, e)
                        ts(sc, relu_i[:, e % 2, 0:n], w_idx[:, b, h:h + 1], None, ALU.mult).then_inc(idx_sum, 1)
                    else:
                        dve.wait_ge(idx_sum, e)
                        stt(sc, relu_i[:, e % 2, 0:n], w_idx[:, b, h:h + 1], sc, ALU.mult, ALU.add).then_inc(idx_sum, 1)

            def choose_rounds(b, first, last):
                n = P * (b + 1)
                cols = slice(BLK[b], BLK[b] + n)
                sc, rk = score3[:, :] if b == 3 else score[:, cols], ranked[:, cols]
                if first == 0:
                    link(tt(sc[:, n - P:n], sc[:, n - P:n], masks[:, 0, :], ALU.add))
                for r in range(first, last):
                    link(dve.max(top[:, :], sc if r == 0 else rk))
                    if r < ROUNDS - 1:
                        link(dve.match_replace(rk, top[:, :], sc if r == 0 else rk, 3 * NEG))

            def choose(b):
                n = P * (b + 1)
                cols = slice(BLK[b], BLK[b] + n)
                sc, rk = score3[:, :] if b == 3 else score[:, cols], ranked[:, cols]
                eq, sn = (equal3, seen3) if b == 3 else (equal[:, 0:n], seen[:, 0:n])
                least = top[:, 7:8]
                link(ts(rk, sc, least, None, ALU.is_gt))
                link(dve.tensor_reduce(above[:, :], rk, AX.X, ALU.add))
                link(ts(eq[:, 0:n], sc, least, None, ALU.is_equal))
                link(dve.tensor_tensor_scan(sn[:, 0:n], one[:, 0:1].broadcast_to([P, n]), eq[:, 0:n], 0.0, ALU.mult, ALU.add))
                link(ts(sn[:, 0:n], sn[:, 0:n], above[:, 0:1], float(TOPK), ALU.add, ALU.is_le))
                link(tt(sn[:, 0:n], sn[:, 0:n], eq[:, 0:n], ALU.mult))
                link(tt(rk, rk, sn[:, 0:n], ALU.add))
                ts(chosen[:, cols], rk, -1.0, -NEG, ALU.add, ALU.mult).then_inc(idx_chosen, 1)

            for j in range(4):
                table = rope_q if j < 2 else rope_k
                for t in range(TB + 2):
                    n, e = TB * j + t, TB * (1 + j) + t
                    if t < TB:
                        head_sums(n)
                    if 1 <= t <= TB:
                        head_scale(n - 1)
                        head_sine(e - 1, table, t - 1)
                    if t >= 2:
                        head_add(e - 2, t - 2)
                if j == 0:
                    index_scores()
                if j == 1:
                    choose_rounds(1, 0, 10)
                if j == 2:
                    choose_rounds(1, 10, ROUNDS)
                    choose(1)
            choose_rounds(2, 0, ROUNDS)
            choose(2)
            link(dve.tensor_copy(score3[:, :], score[:, BLK[3]:BLK[3] + 4 * P]))

            def attend_dve(units, u0, stick=False, ranking=False):
                n = len(units)
                for t in range(n + 3):
                    if t < n:
                        cols, add, sink = units[t][1].shape[1], units[t][2], units[t][6]
                        lg, s, m = logit[:, t % 3, 0:cols], PS[:, t % 3, 0:cols], neg_max[:, t % 4:t % 4 + 1]
                        if ranking and t >= NH and t % NH == 0:
                            dve.wait_ge(idx_chosen, t // NH)
                        dve.wait_ge(at_dot, u0 + t + 1)
                        if t >= 3 and not stick:
                            dve.wait_ge(at_turn, u0 + t - 2)
                        if stick:
                            dve.wait_ge(at_logit, u0 + t + 1)
                            rest, diagonal = stay[t % 2][:, 0:cols], slice(cols - P, cols)
                            link(tt(rest[:, diagonal], rest[:, diagonal], masks[:, 1, :], ALU.max))
                            link(tt(lg[:, diagonal], lg[:, diagonal], masks[:, 2, :], ALU.mult))
                            dve.tensor_tensor_scan(rest[:, ::-1], rest[:, ::-1], one[:, 0:1].broadcast_to([P, cols]), 1.0,
                                                   ALU.mult, ALU.mult).then_inc(at_max, 1)
                            dve.wait_ge(at_max, u0 + t + 1)
                            tt(lg[:, 0:cols - 1], lg[:, 0:cols - 1], rest[:, 1:cols], ALU.mult).then_inc(at_prob, 1)
                        else:
                            if add is not None:
                                tt(lg, s, add, ALU.add).then_inc(at_logit, 1)
                                dve.wait_ge(at_logit, u0 + t + 1)
                            ins = dve.tensor_reduce(m, s if add is None else lg, AX.X, ALU.max, negate=True)
                            if sink is not None:
                                link(ins)
                                ins = tt(m, m, sinks_neg[:, sink:sink + 1], ALU.min)
                            ins.then_inc(at_max, 1)
                    if stick and n <= t < n + 2:
                        m = t - n
                        dve.wait_ge(mem_rstd, 1)
                        ts(mem[:, m, :], mem[:, m, :], rstd[:, 32 + m:33 + m], None, ALU.mult).then_inc(mem_norm, 1)
                    if ranking and 4 <= t < 4 + 2 * ROUNDS and t % 2 == 0:
                        choose_rounds(3, t // 2 - 2, t // 2 - 1)
                    if ranking and t == 4 + 2 * ROUNDS:
                        choose(3)
                    e = t - 3
                    if e >= 0:
                        half, o = units[e][4:6]
                        c = slice(e % 4, e % 4 + 1)
                        dve.wait_ge(at_pv, u0 + e + 1)
                        if stick:
                            dve.tensor_copy(o, PS[:, 5 + e % 2, HD * half:HD * half + HD]).then_inc(at_out, 1)
                            continue
                        dve.wait_ge(at_inv, u0 + e + 1 - (len(stick_units) if u0 > STICK_UNIT else 0))
                        ts(o, PS[:, 5 + e % 2, HD * half:HD * half + HD], inv_sum[:, c], None, ALU.mult).then_inc(at_out, 1)

            attend_dve(dsa_units, DSA_UNIT, ranking=True)
            turn_lo(3 * KT, KT)
            for j in range(2):
                add_panel(WO_PANEL + j, WO_SLOT + 2 * j + 2, slice(512 * j, 512 * j + 512), norm=(None, 2)[j])
            turn_lo(4 * KT, KT, gain=3, banks=8)
            ffn_dve(1)

            turn_lo(5 * KT, KT, gain=4, banks=8)
            dve.wait_ge(ld_bias_t, 16)
            attend_dve(soft_units, SOFT_UNIT)
            attend_dve(stick_units, STICK_UNIT, stick=True)
            turn_lo(6 * KT, KT, gain=6, width=MEM, hi=memT_hi, lo=memT_lo)
            dve.wait_ge(grp_rstd, 1)
            for tb in range(TB):
                y4 = o_nat[:, tb, :].rearrange("p (g n) -> p g n", g=4)
                tt(y4, y4, rstd[:, 16 + 4 * tb:20 + 4 * tb].unsqueeze(2).broadcast_to([P, 4, 256]), ALU.mult).then_inc(grp_norm, 1)
            turn_lo(7 * KT, KT, gain=8)
            for j in range(2):
                add_panel(HOUT_PANEL + j, HOUT_SLOT + 2 * j + 2, slice(512 * j, 512 * j + 512), norm=(None, 4)[j])

            turn_lo(8 * KT, KT, gain=5, banks=8)
            attend_dve(mem_units, MEM_UNIT)
            turn_lo(9 * KT, 2)
            for j in range(2):
                for tb in range(TB):
                    if j == 1 and tb == TB - 1:
                        dve.wait_ge(w_used, XO_SLOT + 1)
                    else:
                        dve.wait_ge(n_ready, 3 * XO_PANEL + TB * j + tb + 1)
                    xs = x_res[:, tb, 512 * j:512 * j + 512]
                    tt(xs, xs, PS[:, 4 + tb, :], ALU.add).then_inc(n_free, 1)
                    if j == 1:
                        norm_after(5, tb)

            turn_lo(9 * KT + 2, KT, gain=7, banks=8)
            for part in range(MLP_PARTS):
                g0, t0, h0 = MLP_SLOT[part], MLP_TILE[part], MLP_HID[part]
                with dve.Fori(0, MT // 4) as i:
                    for j in range(2):
                        pair = (t0 + j) % 2
                        gb = gbuf[:, pair, :, :]
                        hi = hT_hi[:, bass.ds(i * 4 + 2 * j, 2), :]
                        dve.wait_ge(t_free, i * 2 + (t0 + j + 3))
                        tt(gb, gb, gb, ALU.mult).then_inc(hid_act, 1)
                        dve.wait_ge(hid_act, i * 2 + (h0 + j + 1))
                        dve.tensor_copy(hi, gb).then_inc(hid_hi, 1)
                        dve.wait_ge(hid_hi, i * 2 + (h0 + j + 1))
                        tt(hT_lo[:, bass.ds(i * 4 + 2 * j, 2), :], gb, f32(hi), ALU.subtract).then_inc(hid_done, 1)
                m = MT // 4
                for i in range(2):
                    add_panel(i + MLP_PANEL[part], i * m + (g0 + MT // 2 + m), slice(512 * i, 512 * i + 512), 1,
                              norm=6 if part and i else None)

        @block.tensor
        def _(pe):
            mm, tr = pe.matmul, pe.transpose
            id64 = ident[0:64, 0:64]
            pe.wait_ge(ld_const, 16 * 2)
            pe.wait_ge(ld_lam, 16 * 5)
            for j in range(2):
                ins = tr(PS[:, 0, G * j:G * j + G], nat_l[:, j, :, :].rearrange("g a p -> g (a p)"), id64)
            ins.then_inc(s5_nat, 1)
            pe.wait_ge(ld_par, 16 * 6)
            for order, bank in ((0, 1), (1, 3)):
                for h in range(GH):
                    ins = tr(PS[:, bank + h // 8, G * (h % 8):G * (h % 8) + G],
                             nat_b[:, order:order + 2, :, h].rearrange("g a p -> g (a p)"), id64)
                ins.then_inc(s5_nat, 1)
            for b in range(NB):
                ins = tr(PS[:, 5 + b // 4, P * (b % 4):P * (b % 4) + P], nat_c[:, b, 0:2, :].rearrange("g a p -> g (a p)"), ident[:, :])
            ins.then_inc(s5_nat, 1)
            for b in range(NB // 2):
                ins = tr(PS[:, 7, P * b:P * b + P], nat_c[:, b, 1:3, :].rearrange("g a p -> g (a p)"), ident[:, :])
            ins.then_inc(s5_nat, 1)
            pe.wait_ge(s5_nat_sb, 2)
            for b in range(NB // 2):
                ins = tr(PS[:, 1, P * b:P * b + P], nat_c[:, NB // 2 + b, 1:3, :].rearrange("g a p -> g (a p)"), ident[:, :])
            ins.then_inc(s5_nat, 1)
            pe.wait_ge(ld_late, 16 * 8)
            tr(PS[:, 0, 0:len(GAINS) * KT], gain_rows[:, :], ident[0:len(GAINS) * KT, 0:len(GAINS) * KT]).then_inc(gains_t, 1)
            def s5_out(b):
                pe.wait_ge(s5_cz, b + 1)
                pe.wait_ge(s5_outb, b + 1)
                pe.wait_ge(s5_taps, 16 * CH * (b + 1))
                if b >= 1:
                    pe.wait_ge(s5_gelu, b)
                for g in range(GB):
                    o = PS[0:NC, 6 + g // 4, P * (g % 4):P * (g % 4) + P]
                    mm(o, uT[:, GB * b + g, :], taps[:, g, :, :].rearrange("p t h -> p (t h)"), start=True, stop=False)
                    mm(o, cz[:, g, :], out_a[b % 3][:, g, 1:CH + 1, :].rearrange("p t h -> p (t h)"), start=False, stop=False)
                    ins = mm(o, sz[:, g, :], out_b[:, g, :, :].rearrange("p t h -> p (t h)"), start=False, stop=True)
                ins.then_inc(s5_y, 1)

            def s5_maps(b):
                pe.wait_ge(s5_inw, b + 1)
                if b >= 1:
                    pe.wait_ge(s5_int_sb, b)
                for g in range(GB):
                    ins = tr(PS[:, 2 + g // 4, P * (g % 4):P * (g % 4) + P], in_w[:, g, :, :].rearrange("p s h -> p (s h)"), ident[:, :])
                ins.then_inc(s5_int, 1)
                pe.wait_ge(s5_outa, b + 1)
                if b >= 1:
                    pe.wait_ge(s5_lag_sb, b)
                pe.wait_ge(s5_skip, 1)
                for g in range(GB):
                    o = PS[0:GH, g // 4, P * (g % 4):P * (g % 4) + P]
                    mm(o, b_n[:, GB * b + g, :], out_a[b % 3][:, g, 0:CH, :].rearrange("p t h -> p (t h)"), start=True, stop=False)
                    ins = mm(o[:, 0:GH], ident[0:GH, 0:GH], skip[:, GB * b + g, :], start=False, stop=True)
                ins.then_inc(s5_lag, 1)

            def s5_in(b):
                pe.wait_ge(s5_int_sb, b + 1)
                if b >= 1:
                    pe.wait_ge(s5_rot, b)
                for g in range(GB):
                    mm(PS[:, 4, NC * g:NC * g + NC], in_t[:, g, :, :].rearrange("p r q -> p (r q)"), uT[:, GB * b + g, :], start=True, stop=True)
                    ins = mm(PS[:, 5, NC * g:NC * g + NC], in_s[:, g, :, :].rearrange("p r q -> p (r q)"), uT[:, GB * b + g, :], start=True, stop=True)
                ins.then_inc(s5_v, 1)

            pe.wait_ge(s5_nat_sb, 6)
            pe.wait_ge(gains_sb, 1)
            s5_maps(0)
            pe.wait_ge(s5_u, CH)
            for q in range(8):
                if q == 0:
                    pe.wait_ge(s5_lag_sb, 1)
                if q == 2:
                    pe.wait_ge(s5_int_sb, 1)
                for g in range(GB):
                    ins = tr(PS[:, q, NC * g:NC * g + NC], u[:, GB * q + g, :, :].rearrange("p t h -> p (t h)"), id64)
                ins.then_inc(s5_ut, 1)
            pe.wait_ge(s5_ut_sb, 8)
            s5_in(0)
            def s5_turn(first, last):
                for b in range(first, last):
                    pe.wait_ge(s5_gelu, b + 1)
                    if b >= 4:
                        pe.wait_ge(x_lo_done, b - 3)
                    for s in range(CH):
                        ins = tr(PS[:, b % 4, NC * s:NC * s + NC], y[:, b, s, :], id64)
                    ins.then_inc(turned, 1)

            for b in range(NB):
                if b + 1 < NB:
                    s5_maps(b + 1)
                    s5_in(b + 1)
                else:
                    pe.wait_ge(s5_lag_sb, NB)
                    s5_turn(0, 4)
                s5_out(b)
            s5_turn(4, NB)

            def three(o, wgt_hi, wgt_lo, x_hi, x_lo, weights_stay, first, last):
                for n, (a, c) in enumerate(((wgt_hi, x_hi), (wgt_lo, x_hi), (wgt_hi, x_lo))):
                    ins = mm(o, a if weights_stay else c, c if weights_stay else a,
                             start=first and n == 0, stop=last and n == 2)
                return ins

            def n_slot(g, par, ni, ks, hi, lo, first, last, n=512, tbs=TB, inc=1, turns=None):
                pe.wait_ge(w_split, g + 1)
                for tb in range(tbs):
                    if turns is not None:
                        pe.wait_ge(x_lo_done, turns[tb])
                    if first:
                        pe.wait_ge(n_free, ni * TB + (tb + 1))
                    for j, k in enumerate(ks):
                        cols = slice(n * j, n * j + n)
                        ins = three(PS[:, 4 + tb, 0:n], w_hi[:, par, cols], w_lo[:, par, cols],
                                    hi[:, k, P * tb:P * tb + P], lo[:, k, P * tb:P * tb + P], False,
                                    first and j == 0, last and j == len(ks) - 1)
                    if tb == tbs - 1:
                        ins.then_inc(w_used, 1)
                    elif last:
                        ins.then_inc(n_ready, inc)

            def t_slot(g, par, ti, pair, hi, lo, width=S, step=(2 * P, P), turns=None):
                pe.wait_ge(w_split, g + 1)
                pe.wait_ge(t_free, ti + 1)
                for t in range(2):
                    for k in range(KT):
                        if turns is not None and t == 0:
                            pe.wait_ge(x_lo_done, turns - KT + k + 1)
                        at = step[0] * k + step[1] * t
                        cols = slice(at, at + P)
                        ins = three(PS[:, 2 * pair + t, 0:width], w_hi[:, par, cols], w_lo[:, par, cols],
                                    hi[:, k, 0:width], lo[:, k, 0:width], True, k == 0, k == KT - 1)
                    ins.then_inc(w_used if t else t_first, 1)

            def turn_rows(j0, n, src, tbs=TB):
                for k in range(n):
                    if k >= 4:
                        pe.wait_ge(x_lo_done, j0 + k - 3)
                    for tb in range(tbs):
                        ins = tr(PS[:, k % 4, P * tb:P * tb + P], src[:, tb, P * k:P * k + P], ident[:, :])
                    ins.then_inc(turned, 1)

            for j in range(4):
                for k in range(2):
                    g = GLU_SLOT + 2 * j + k
                    n_slot(g, g % 2, GLU_PANEL + j, range(4 * k, 4 * k + 4), xT_hi, xT_lo, k == 0, k == 1,
                           turns=None if j else [4 * k + 4] * TB)
            def turn_normed(n, j0):
                def turn(k, tb):
                    ins = mm(PS[:, k, P * tb:P * tb + P], x_res[:, tb, P * k:P * k + P], diag[:, tb, :], start=True, stop=True)
                    if tb == TB - 1:
                        ins.then_inc(turned, 1)

                for tb in range(TB):
                    pe.wait_ge(row_norm, TB * n + tb + 1)
                    for k in range(4):
                        turn(k, tb)
                    if tb == TB - 2:
                        for k in range(4, 7):
                            for t in range(TB - 1):
                                turn(k, t)
                for k in range(4, 7):
                    turn(k, TB - 1)
                for t in range(TB):
                    turn(7, t)

            turn_normed(0, KT)

            def ffn_pe(layer, turns):
                g0, t0, h0 = FFN_SLOT[layer], FFN_TILE[layer], FFN_HID[layer]
                with pe.Fori(0, FT // 2) as i:
                    for j in range(2):
                        t_slot(i * 2 + (g0 + j), (g0 + j) % 2, i * 2 + (t0 + j), (t0 + j) % 2, xT_hi, xT_lo,
                               turns=(turns, None)[j])
                g0 += FT
                m = len(FFN_DOWN)
                with pe.Fori(0, 2) as i:
                    k = 0
                    for j, n in enumerate(FFN_DOWN):
                        pe.wait_ge(hid_done, h0 + k + n + 2)
                        n_slot(i * m + (g0 + j), (g0 + j) % 2, i + FFN_PANEL[layer], range(k, k + n), hT_hi, hT_lo,
                               j == 0, j == m - 1)
                        k += n

            ffn_pe(0, 2 * KT)
            turn_normed(1, 2 * KT)

            def panel(g0, ni, n=512, turns=None, banks=4):
                for k in range(2):
                    need = [turns + min(KT, (4 + 4 * k if banks == 4 else 5 + tb + 4 * k)) for tb in range(TB)] if turns is not None else None
                    n_slot(g0 + k, (g0 + k) % 2, ni, range(4 * k, 4 * k + 4), xT_hi, xT_lo, k == 0, k == 1, n, turns=need)

            def turn_heads(pi):
                pe.wait_ge(head_done, TB * (pi + 1))
                for j in range(4):
                    if pi >= 1:
                        pe.wait_ge(head_t_sb, 4 * (pi - 1) + j + 1)
                    for tb in range(TB):
                        ins = tr(PS[:, j, P * tb:P * tb + P], stage[:, pi % 2, tb, P * j:P * j + P], ident[:, :])
                    ins.then_inc(head_t, 1)

            g = DSA_SLOT
            panel(g, DSA_PANEL, turns=2 * KT, banks=8)
            n_slot(g + 2, (g + 2) % 2, DSA_PANEL + 1, range(KT), xT_hi, xT_lo, True, True, DSA_W - 3 * D - 512)
            panel(g + 3, DSA_PANEL + 2)
            turn_heads(0)
            pe.wait_ge(ki_done, 3)
            for head in range(2):
                pe.wait_ge(head_t_sb, head + 1)
                for tb in range(TB):
                    ins = tr(PS[:, head, P * tb:P * tb + P],
                             ki_st[:, tb, 1 - head:3 - head, :].rearrange("p a d -> p (a d)"), ident[:, :])
                ins.then_inc(ki_t, 1)
            pe.wait_ge(head_t_sb, 4)
            pe.wait_ge(ki_t_sb, 2)
            for e in range(3 * NI):
                b, h = e // NI + 1, e % NI
                if e >= 4:
                    pe.wait_ge(idx_relu, e - 3)
                mm(PS[:, e % 4, 0:P * (b + 1)], qiT[:, h // 2, P * b:P * b + P], kiT[h % 2][:, 0:P * (b + 1)],
                   start=True, stop=True).then_inc(idx_dot, 1)
            for j in range(1, 6):
                panel(g + 3 + 2 * j, DSA_PANEL + 2 + j)
                if j == 1:
                    pe.wait_ge(idx_relu, 3 * NI)
                if j < 5:
                    turn_heads(j)

            def attend_pe(units, u0):
                n = len(units)
                for t in range(n + 3):
                    if t < n:
                        k = units[t][1]
                        pe.wait_ge(q_padded, u0 + t + 1)
                        if t >= 3:
                            pe.wait_ge(at_prob if u0 == MEM_UNIT else at_logit, u0 + t - 2)
                        mm(PS[:, t % 3, 0:k.shape[1]], q_pad[:, (u0 + t) % 4, :], k, start=True, stop=True).then_inc(at_dot, 1)
                    e = t - 2
                    if 0 <= e < n:
                        pe.wait_ge(at_prob, u0 + e + 1)
                        if e >= 2:
                            pe.wait_ge(at_turn_sb, u0 + e - 1)
                        for j in range(len(units[e][3])):
                            ins = tr(PS[:, 3 + e % 2, P * j:P * j + P], logit[:, e % 3, P * j:P * j + P], ident[:, :])
                        ins.then_inc(at_turn, 1)
                    e = t - 3
                    if e >= 0:
                        v = units[e][3]
                        pe.wait_ge(at_turn_sb, u0 + e + 1)
                        if e >= 2:
                            pe.wait_ge(at_out, u0 + e - 1)
                        for j in range(len(v)):
                            ins = mm(PS[:, 5 + e % 2, 0:P], probT[:, e % 2, P * j:P * j + P], v[j],
                                     start=j == 0, stop=j == len(v) - 1)
                        ins.then_inc(at_pv, 1)

            pe.wait_ge(head_t_sb, 20)
            pe.wait_ge(n_free, TB * (DSA_PANEL + 9))
            pe.wait_ge(idx_chosen, 2)
            attend_pe(dsa_units, DSA_UNIT)
            pe.wait_ge(at_out, SOFT_UNIT)
            turn_rows(3 * KT, KT, o_nat)
            for j in range(2):
                panel(WO_SLOT + 2 * j, WO_PANEL + j, turns=(3 * KT, None)[j])
            turn_normed(2, 4 * KT)
            ffn_pe(1, 5 * KT)

            turn_normed(3, 5 * KT)
            for j in range(8):
                g = HIN_SLOT + j
                t_slot(g, g % 2, HIN_TILE + j, (HIN_TILE + j) % 2, xT_hi, xT_lo, step=(192, 64) if j == 5 else (256, P),
                       turns=None if j else 6 * KT)
                if j == 0:
                    pe.wait_ge(ld_bias, 48)
                    mm(PS[0:NREL, 4, :], table[:, :], basis[:, 0:512], start=True, stop=True)
                    mm(PS[0:NREL, 5, 0:BIAS_W - 512], table[:, :], basis[:, 512:BIAS_W], start=True, stop=True).then_inc(bias_row, 1)
            pe.wait_ge(bias_row_sb, 1)
            panel(HIN_SLOT + 8, HIN_PANEL)
            panel(HIN_SLOT + 10, HIN_PANEL + 1, 384)
            pe.wait_ge(t_free, HIN_TILE + 10)
            pe.wait_ge(n_free, TB * (HIN_PANEL + 3))
            attend_pe(soft_units, SOFT_UNIT)
            attend_pe(stick_units, STICK_UNIT)
            pe.wait_ge(mem_norm, 2)
            turn_rows(6 * KT, KT, mem, 2)
            pe.wait_ge(x_lo_done, 7 * KT)
            t_slot(MEM_SLOT, MEM_SLOT % 2, MEM_TILE, MEM_TILE % 2, memT_hi, memT_lo, MEM)
            pe.wait_ge(at_out, MEM_UNIT)
            n_slot(MEM_SLOT + 1, (MEM_SLOT + 1) % 2, MEM_PANEL, range(KT), memT_hi, memT_lo, True, True, 256, 2, 3)
            pe.wait_ge(t_free, MEM_TILE + 3)
            pe.wait_ge(grp_norm, TB)
            turn_rows(7 * KT, KT, o_nat)
            for j in range(2):
                panel(HOUT_SLOT + 2 * j, HOUT_PANEL + j, turns=(7 * KT, None)[j])

            turn_normed(4, 8 * KT)
            pe.wait_ge(x_lo_done, 9 * KT)
            t_slot(XQ_SLOT, XQ_SLOT % 2, XQ_TILE, XQ_TILE % 2, xT_hi, xT_lo)
            pe.wait_ge(t_free, XQ_TILE + 3)
            pe.wait_ge(n_free, TB * (MEM_PANEL + 2))
            attend_pe(mem_units, MEM_UNIT)
            pe.wait_ge(at_out, MEM_UNIT + 16)
            turn_rows(9 * KT, 2, ox)
            pe.wait_ge(x_lo_done, 9 * KT + 2)
            par = XO_SLOT % 2
            pe.wait_ge(w_split, XO_SLOT + 1)
            for j in range(2):
                for tb in range(TB):
                    pe.wait_ge(n_free, TB * (XO_PANEL + j) + tb + 1)
                    for k in range(2):
                        cols = slice(D * k + 512 * j, D * k + 512 * j + 512)
                        ins = three(PS[:, 4 + tb, :], w_hi[:, par, cols], w_lo[:, par, cols],
                                    xT_hi[:, k, P * tb:P * tb + P], xT_lo[:, k, P * tb:P * tb + P], False, k == 0, k == 1)
                    ins.then_inc(w_used if j == 1 and tb == TB - 1 else n_ready, 1)

            turn_normed(5, 9 * KT + 2)
            for part in range(MLP_PARTS):
                g0, t0, h0 = MLP_SLOT[part], MLP_TILE[part], MLP_HID[part]
                with pe.Fori(0, MT // 4) as i:
                    for j in range(2):
                        t_slot(i * 2 + (g0 + j), (g0 + j) % 2, i * 2 + (t0 + j), (t0 + j) % 2, xT_hi, xT_lo,
                               turns=None if part or j else 10 * KT + 2)
                g0 += MT // 2
                m = MT // 4
                with pe.Fori(0, 2) as i:
                    for j in range(m):
                        pe.wait_ge(hid_done, h0 + 2 * j + 4)
                        n_slot(i * m + (g0 + j), (g0 + j) % 2, i + MLP_PANEL[part], range(4 * j, 4 * j + 4), hT_hi, hT_lo,
                               j == 0, j == m - 1)


def chunk_view(o, i):
    return o.rearrange("p (c s) -> p s c", s=CH), i.rearrange("p (s c) -> p s c", s=CH)


_INS = ["x", "s5_lambda_re", "s5_lambda_im", "s5_log_dt", "s5_b_re", "s5_b_im", "s5_c_re", "s5_c_im", "s5_d", "s5_w_glu",
        "dsa_w_in", "dsa_q_norm", "dsa_k_norm", "dsa_w_o", "ffn_w_gate_up", "ffn_w_down", "norm_mix", "norm_ffn",
        "mem_2", "rel_table_2", "g_mix_2", "w_in_2", "g_group_2", "sinks_2", "w_out_2", "g_cross_2", "g_mem_2",
        "w_xq_2", "w_xkv_2", "w_xo_2", "g_mlp_2", "w_up_2", "w_down_2", "g_final_2"]


def kernel(**inputs):
    import concourse.bacc as bacc
    from concourse.bass_utils import run_bass_kernel_spmd

    nc = bacc.Bacc("TRN2", target_bir_lowering=False, num_devices=1)
    arrays, w = {}, {}
    for name, value in {**{n: inputs[n] for n in _INS}, **shape_constants()}.items():
        a = np.ascontiguousarray(value)
        if name in ("x", "mem_2"):
            a = a[0]
        arrays[f"in_{name}"] = a
        w[name] = nc.dram_tensor(f"in_{name}", a.shape, mybir.dt.from_np(a.dtype), kind="ExternalInput").ap()
    out = nc.dram_tensor("out_x", (S, D), F32, kind="ExternalOutput").ap()
    program(nc, w, out)
    r = run_bass_kernel_spmd(nc, [arrays], core_ids=[0])
    return r.results[0]["out_x"][None]
```
